# Optimizing a Trainium2 kernel written in Bass

```python
import math
import jax
import jax.numpy as jnp
from jax import lax
import numpy as np

D_MODEL = 1024
BATCH = 1
SEQ = 256
DEPTH = 1
DEC_BATCH = 8
DEC_SEQ = 1
PAST_LEN = 1024
PAGE_SIZE = 128

N_HEADS = 8
QK_NOPE = 64
QK_ROPE = 32
QK_DIM = QK_NOPE + QK_ROPE
V_DIM = 64
Q_LORA = 384
KV_LORA = 256
ROPE_THETA = 10000.0
Q_BLOCK = 128
CONV_W = 3
CONV_DIM = 512
CHUNK = 128
GM_GROUPS = 8
GM_DIM = 512
GM_GROUP_DIM = GM_DIM // GM_GROUPS
N_EXPERTS = 64
TOP_K = 8
N_EXPERT_GROUPS = 8
TOPK_GROUPS = 4
D_EXPERT = 256
D_SHARED = 256
ROUTED_SCALE = 2.5
TOKEN_BLOCK = 128
N_BRANCH = 3
EPS = 1e-6

OFF_Q = 0
OFF_KV = OFF_Q + Q_LORA
OFF_KR = OFF_KV + KV_LORA
OFF_CB = OFF_KR + QK_ROPE
OFF_CC = OFF_CB + CONV_DIM
OFF_CH = OFF_CC + CONV_DIM
OFF_U = OFF_CH + CONV_DIM
OFF_V = OFF_U + GM_DIM
OFF_G = OFF_V + GM_DIM
IN_DIM = OFF_G + N_BRANCH * D_MODEL

kernel_name = "hybrid_mla_conv_gmlp_moe_adaln_step"

def rmsnorm(x, g):
    xf = x.astype(jnp.float32)
    inv = lax.rsqrt(jnp.mean(xf * xf, axis=-1, keepdims=True) + EPS)
    return (xf * inv).astype(x.dtype) * g

def layernorm(x, g):
    xf = x.astype(jnp.float32)
    xc = xf - jnp.mean(xf, axis=-1, keepdims=True)
    inv = lax.rsqrt(jnp.mean(xc * xc, axis=-1, keepdims=True) + EPS)
    return (xc * inv).astype(x.dtype) * g

def rope_cos_sin(pos):
    inv_freq = ROPE_THETA ** (-jnp.arange(0, QK_ROPE, 2, dtype=jnp.float32) / QK_ROPE)
    ang = pos.astype(jnp.float32)[:, None] * inv_freq[None, :]
    return jnp.cos(ang), jnp.sin(ang)

def apply_rope(x, cos, sin):
    x1, x2 = jnp.split(x.astype(jnp.float32), 2, axis=-1)
    return jnp.concatenate([x1 * cos - x2 * sin, x1 * sin + x2 * cos], axis=-1).astype(x.dtype)

def adaln_modulation(c, w_ada, b_ada):
    m = jnp.einsum('nd,de->ne', jax.nn.silu(c), w_ada) + b_ada
    return jnp.split(m[:, None, :], 6, axis=-1)

def mla_queries(cq_raw, pos, g_q_lat, w_uq, g_qk_q):
    q = jnp.einsum('ntc,chd->nthd', rmsnorm(cq_raw, g_q_lat), w_uq)
    cos, sin = rope_cos_sin(pos)
    q = jnp.concatenate([q[..., :QK_NOPE], apply_rope(q[..., QK_NOPE:], cos[:, None, :], sin[:, None, :])], axis=-1)
    return rmsnorm(q, g_qk_q) * (QK_DIM ** -0.5)

def mla_keys(c_kv, k_rope, w_uk, g_qk_k):
    k_nope = jnp.einsum('...tc,chd->...thd', c_kv, w_uk)
    k_rot = jnp.broadcast_to(k_rope[..., None, :], k_nope.shape[:-1] + (QK_ROPE,))
    return rmsnorm(jnp.concatenate([k_nope, k_rot], axis=-1), g_qk_k)

def attend(q, k, c_kv, w_uv, q_pos, k_pos):
    s = jnp.einsum('...qhd,...khd->...hqk', q, k).astype(jnp.float32)
    s = jnp.where(k_pos[None, :] <= q_pos[:, None], s, -jnp.inf)
    prob = jax.nn.softmax(s, axis=-1).astype(c_kv.dtype)
    o_lat = jnp.einsum('...hqk,...kc->...qhc', prob, c_kv)
    return jnp.einsum('...qhc,chd->...qhd', o_lat, w_uv)

def mla_prompt(q, c_kv, k_rope, pos, w_uk, w_uv, g_qk_k):
    n, t = q.shape[:2]
    nb = t // Q_BLOCK
    k = mla_keys(c_kv, k_rope, w_uk, g_qk_k)
    q_blocks = q.reshape(n, nb, Q_BLOCK, N_HEADS, QK_DIM).swapaxes(0, 1)
    pos_blocks = pos.reshape(nb, Q_BLOCK)

    def block(args):
        q_b, pos_b = args
        return attend(q_b, k, c_kv, w_uv, pos_b, pos)

    out = lax.map(block, (q_blocks, pos_blocks))
    return out.swapaxes(0, 1).reshape(n, t, N_HEADS * V_DIM)

def mla_sample(q, c_new, kr_new, pos, pool_c, pool_kr, page_table, w_uk, w_uv, g_qk_k):
    n, t = q.shape[:2]
    k_pos = jnp.concatenate([jnp.arange(PAST_LEN), pos])

    def one(args):
        q_i, pages_i, c_i, kr_i = args
        c_all = jnp.concatenate([pool_c[pages_i].reshape(PAST_LEN, KV_LORA), c_i], axis=0)
        kr_all = jnp.concatenate([pool_kr[pages_i].reshape(PAST_LEN, QK_ROPE), kr_i], axis=0)
        k = mla_keys(c_all, kr_all, w_uk, g_qk_k)
        return attend(q_i, k, c_all, w_uv, pos, k_pos)

    out = lax.map(one, (q, page_table, c_new, kr_new))
    return out.reshape(n, t, N_HEADS * V_DIM)

def short_conv(z_full, w_conv):
    return lax.conv_general_dilated(z_full, w_conv[:, None, :], (1,), 'VALID',
                                    dimension_numbers=('NWC', 'WIO', 'NWC'),
                                    feature_group_count=CONV_DIM)

def chunk_spatial_gate(u, v_n, w_s, b_s):
    n, nc, tc, _ = u.shape
    w = jnp.where(jnp.tril(jnp.ones((tc, tc), dtype=bool)), w_s[:, :tc, :tc], 0)
    vg = v_n.reshape(n, nc, tc, GM_GROUPS, GM_GROUP_DIM)
    s = jnp.einsum('gts,ncsgd->nctgd', w, vg) + b_s[:, :tc].T[None, None, :, :, None]
    return u * s.reshape(n, nc, tc, GM_DIM)

def sigmoid_topk_gates(h, w_router, b_router):
    scores = jax.nn.sigmoid(jnp.einsum('td,de->te', h, w_router).astype(jnp.float32))
    choice = scores + b_router.astype(jnp.float32)
    grp = choice.reshape(-1, N_EXPERT_GROUPS, N_EXPERTS // N_EXPERT_GROUPS)
    grp_score = jnp.sum(lax.top_k(grp, 2)[0], axis=-1)
    _, gidx = lax.top_k(grp_score, TOPK_GROUPS)
    gmask = jnp.sum(jax.nn.one_hot(gidx, N_EXPERT_GROUPS, dtype=jnp.float32), axis=-2)
    emask = jnp.repeat(gmask, N_EXPERTS // N_EXPERT_GROUPS, axis=-1)
    _, idx = lax.top_k(jnp.where(emask > 0, choice, -jnp.inf), TOP_K)
    w = jnp.take_along_axis(scores, idx, axis=-1)
    w = w / jnp.sum(w, axis=-1, keepdims=True) * ROUTED_SCALE
    return jnp.sum(jax.nn.one_hot(idx, N_EXPERTS, dtype=jnp.float32) * w[..., None], axis=-2)

def moe_ffn(h, lw):
    n, t, d = h.shape
    flat = h.reshape(n * t, d)

    def block(hb):
        gates = sigmoid_topk_gates(hb, lw['w_router'], lw['b_router']).astype(hb.dtype)
        a = jnp.einsum('td,edf->tef', hb, lw['w_e_gate'])
        b = jnp.einsum('td,edf->tef', hb, lw['w_e_up'])
        routed = jnp.einsum('tef,efd->td', jax.nn.silu(a) * b * gates[..., None], lw['w_e_down'])
        shared = (jax.nn.silu(hb @ lw['w_sh_gate']) * (hb @ lw['w_sh_up'])) @ lw['w_sh_down']
        return routed + shared

    if flat.shape[0] % TOKEN_BLOCK == 0:
        out = lax.map(block, flat.reshape(-1, TOKEN_BLOCK, d)).reshape(n * t, d)
    else:
        out = block(flat)
    return out.reshape(n, t, d)

def decoder_layer(x, c, pos, conv_hist, paged, lw):
    n, t, _ = x.shape
    shift_m, scale_m, gate_m, shift_f, scale_f, gate_f = adaln_modulation(c, lw['w_ada'], lw['b_ada'])
    h = rmsnorm(x, lw['g_norm_mix']) * (1.0 + scale_m) + shift_m
    p = jnp.einsum('ntd,de->nte', h, lw['w_in'])

    q = mla_queries(p[..., OFF_Q:OFF_KV], pos, lw['g_q_lat'], lw['w_uq'], lw['g_qk_q'])
    c_kv = rmsnorm(p[..., OFF_KV:OFF_KR], lw['g_kv_lat'])
    cos, sin = rope_cos_sin(pos)
    k_rope = apply_rope(p[..., OFF_KR:OFF_CB], cos, sin)
    if paged is None:
        o_a = mla_prompt(q, c_kv, k_rope, pos, lw['w_uk'], lw['w_uv'], lw['g_qk_k'])
    else:
        pool_c, pool_kr, page_table = paged
        o_a = mla_sample(q, c_kv, k_rope, pos, pool_c, pool_kr, page_table, lw['w_uk'], lw['w_uv'], lw['g_qk_k'])
    br_a = jnp.einsum('nte,ed->ntd', o_a, lw['w_br_a'])

    gate_b = p[..., OFF_CB:OFF_CC]
    z = p[..., OFF_CC:OFF_CH] * p[..., OFF_CH:OFF_U]
    z_full = jnp.concatenate([conv_hist, z], axis=1)
    br_b = jnp.einsum('ntc,cd->ntd', gate_b * short_conv(z_full, lw['w_conv']), lw['w_br_b'])
    conv_tail = z_full[:, z_full.shape[1] - (CONV_W - 1):]

    tc = min(t, CHUNK)
    u = p[..., OFF_U:OFF_V].reshape(n, t // tc, tc, GM_DIM)
    v_n = layernorm(p[..., OFF_V:OFF_G], lw['g_v_ln'])
    sg = chunk_spatial_gate(u, v_n.reshape(n, t // tc, tc, GM_DIM), lw['w_spatial'], lw['b_spatial'])
    br_c = jnp.einsum('nte,ed->ntd', sg.reshape(n, t, GM_DIM), lw['w_br_c'])
    chunk_v = v_n[:, t - tc:]

    bgate = jax.nn.sigmoid(p[..., OFF_G:]).reshape(n, t, N_BRANCH, D_MODEL)
    merged = bgate[:, :, 0] * br_a + bgate[:, :, 1] * br_b + bgate[:, :, 2] * br_c
    x = x + gate_m * jnp.einsum('ntd,de->nte', merged, lw['w_out'])

    h2 = rmsnorm(x, lw['g_norm_ffn']) * (1.0 + scale_f) + shift_f
    x = x + gate_f * moe_ffn(h2, lw)
    return x, (c_kv, k_rope, conv_tail, chunk_v)

def setup_inputs(seed: int = 0) -> dict:
    key = jax.random.key(seed)
    ks = list(jax.random.split(key, 40))
    f32 = jnp.float32

    def nrm(i, shape, scale):
        return jax.random.normal(ks[i], shape, f32) * scale

    def gain(i, shape):
        return 1.0 + nrm(i, shape, 0.01)

    n_pages = PAST_LEN // PAGE_SIZE
    n_used = DEC_BATCH * n_pages
    n_pool = n_used + max(1, n_used // 4)
    page_table = jax.random.permutation(ks[5], n_pool)[:n_used].reshape(DEC_BATCH, n_pages).astype(jnp.int32)
    return {
        'x_prompt': nrm(0, (BATCH, SEQ, D_MODEL), 1.0),
        'x_sample': nrm(1, (DEC_BATCH, DEC_SEQ, D_MODEL), 1.0),
        'cache_kv_latent': nrm(2, (DEPTH, n_pool, PAGE_SIZE, KV_LORA), 1.0),
        'cache_k_rope': nrm(3, (DEPTH, n_pool, PAGE_SIZE, QK_ROPE), 1.0),
        'state_conv': nrm(4, (DEPTH, DEC_BATCH, CONV_W - 1, CONV_DIM), 1.0),
        'page_table': page_table,
        'c_prompt': nrm(6, (BATCH, D_MODEL), 1.0),
        'c_sample': nrm(7, (DEC_BATCH, D_MODEL), 1.0),
        'w_ada': nrm(8, (DEPTH, D_MODEL, 6 * D_MODEL), 0.5 * D_MODEL ** -0.5),
        'b_ada': nrm(9, (DEPTH, 6 * D_MODEL), 0.01),
        'g_norm_mix': gain(10, (DEPTH, D_MODEL)),
        'g_norm_ffn': gain(11, (DEPTH, D_MODEL)),
        'w_in': nrm(12, (DEPTH, D_MODEL, IN_DIM), D_MODEL ** -0.5),
        'g_q_lat': gain(13, (DEPTH, Q_LORA)),
        'w_uq': nrm(14, (DEPTH, Q_LORA, N_HEADS, QK_DIM), Q_LORA ** -0.5),
        'g_kv_lat': gain(15, (DEPTH, KV_LORA)),
        'w_uk': nrm(16, (DEPTH, KV_LORA, N_HEADS, QK_NOPE), KV_LORA ** -0.5),
        'w_uv': nrm(17, (DEPTH, KV_LORA, N_HEADS, V_DIM), KV_LORA ** -0.5),
        'g_qk_q': gain(18, (DEPTH, QK_DIM)),
        'g_qk_k': gain(19, (DEPTH, QK_DIM)),
        'w_br_a': nrm(20, (DEPTH, N_HEADS * V_DIM, D_MODEL), (N_HEADS * V_DIM) ** -0.5),
        'w_conv': nrm(21, (DEPTH, CONV_W, CONV_DIM), CONV_W ** -0.5),
        'w_br_b': nrm(22, (DEPTH, CONV_DIM, D_MODEL), CONV_DIM ** -0.5),
        'g_v_ln': gain(23, (DEPTH, GM_DIM)),
        'w_spatial': nrm(24, (DEPTH, GM_GROUPS, CHUNK, CHUNK), CHUNK ** -0.5),
        'b_spatial': 1.0 + nrm(25, (DEPTH, GM_GROUPS, CHUNK), 0.1),
        'w_br_c': nrm(26, (DEPTH, GM_DIM, D_MODEL), GM_DIM ** -0.5),
        'w_out': nrm(27, (DEPTH, D_MODEL, D_MODEL), D_MODEL ** -0.5),
        'w_router': nrm(28, (DEPTH, D_MODEL, N_EXPERTS), D_MODEL ** -0.5),
        'b_router': nrm(29, (DEPTH, N_EXPERTS), 0.01),
        'w_e_gate': nrm(30, (DEPTH, N_EXPERTS, D_MODEL, D_EXPERT), D_MODEL ** -0.5),
        'w_e_up': nrm(31, (DEPTH, N_EXPERTS, D_MODEL, D_EXPERT), D_MODEL ** -0.5),
        'w_e_down': nrm(32, (DEPTH, N_EXPERTS, D_EXPERT, D_MODEL), D_EXPERT ** -0.5),
        'w_sh_gate': nrm(33, (DEPTH, D_MODEL, D_SHARED), D_MODEL ** -0.5),
        'w_sh_up': nrm(34, (DEPTH, D_MODEL, D_SHARED), D_MODEL ** -0.5),
        'w_sh_down': nrm(35, (DEPTH, D_SHARED, D_MODEL), D_SHARED ** -0.5),
    }

def reference(x_prompt, x_sample, cache_kv_latent, cache_k_rope, state_conv, page_table, c_prompt, c_sample,
              w_ada, b_ada, g_norm_mix, g_norm_ffn, w_in, g_q_lat, w_uq, g_kv_lat, w_uk, w_uv, g_qk_q, g_qk_k,
              w_br_a, w_conv, w_br_b, g_v_ln, w_spatial, b_spatial, w_br_c, w_out, w_router, b_router,
              w_e_gate, w_e_up, w_e_down, w_sh_gate, w_sh_up, w_sh_down):
    pos_p = jnp.arange(x_prompt.shape[1])
    pos_s = PAST_LEN + jnp.arange(x_sample.shape[1])
    conv_zero = jnp.zeros((x_prompt.shape[0], CONV_W - 1, CONV_DIM), x_prompt.dtype)
    hp, hs = x_prompt, x_sample
    st_p, st_s = [], []
    for l in range(DEPTH):
        lw = dict(w_ada=w_ada[l], b_ada=b_ada[l], g_norm_mix=g_norm_mix[l], g_norm_ffn=g_norm_ffn[l],
                  w_in=w_in[l], g_q_lat=g_q_lat[l], w_uq=w_uq[l], g_kv_lat=g_kv_lat[l], w_uk=w_uk[l],
                  w_uv=w_uv[l], g_qk_q=g_qk_q[l], g_qk_k=g_qk_k[l], w_br_a=w_br_a[l], w_conv=w_conv[l],
                  w_br_b=w_br_b[l], g_v_ln=g_v_ln[l], w_spatial=w_spatial[l], b_spatial=b_spatial[l],
                  w_br_c=w_br_c[l], w_out=w_out[l], w_router=w_router[l], b_router=b_router[l],
                  w_e_gate=w_e_gate[l], w_e_up=w_e_up[l], w_e_down=w_e_down[l],
                  w_sh_gate=w_sh_gate[l], w_sh_up=w_sh_up[l], w_sh_down=w_sh_down[l])
        hp, sp = decoder_layer(hp, c_prompt, pos_p, conv_zero, None, lw)
        hs, ss = decoder_layer(hs, c_sample, pos_s, state_conv[l],
                               (cache_kv_latent[l], cache_k_rope[l], page_table), lw)
        st_p.append(sp)
        st_s.append(ss)
    new_kv_latent_prompt = jnp.stack([s[0] for s in st_p])
    new_k_rope_prompt = jnp.stack([s[1] for s in st_p])
    new_conv_prompt = jnp.stack([s[2] for s in st_p])
    new_chunk_v_prompt = jnp.stack([s[3] for s in st_p])
    new_kv_latent_sample = jnp.stack([s[0] for s in st_s])
    new_k_rope_sample = jnp.stack([s[1] for s in st_s])
    new_conv_sample = jnp.stack([s[2] for s in st_s])
    new_chunk_v_sample = jnp.stack([s[3] for s in st_s])
    return (hp, hs, new_kv_latent_prompt, new_k_rope_prompt, new_conv_prompt, new_chunk_v_prompt,
            new_kv_latent_sample, new_k_rope_sample, new_conv_sample, new_chunk_v_sample)


_drawn_inputs = setup_inputs


def setup_inputs(seed=0):
    import zlib

    import numpy as np

    out = dict(_drawn_inputs(seed))
    spreads = {}
    factors = {'cache_kv_latent': 2.776,
     'cache_k_rope': 8.0,
     'g_norm_mix': 2.969,
     'g_norm_ffn': 2.934,
     'g_q_lat': 8.0,
     'g_kv_lat': 6.024,
     'g_qk_q': 8.0,
     'g_qk_k': 8.0,
     'g_v_ln': 5.562}
    for name, (base, spread) in spreads.items():
        noise = np.random.default_rng([zlib.crc32(name.encode()), seed]).standard_normal(out[name].shape)
        drawn = base * np.exp(spread * noise) if base else spread * noise
        out[name] = jnp.asarray(drawn.astype(out[name].dtype))
    for name, factor in factors.items():
        out[name] = (out[name] * factor).astype(out[name].dtype)
    return out
```

```python
from contextlib import ExitStack

import numpy as np
import concourse.bass as bass
from concourse import mybir

ALU = mybir.AluOpType
ACT = mybir.ActivationFunctionType
AX = mybir.AxisListType
F32 = mybir.dt.float32
I32 = mybir.dt.int32
RMAX = bass.bass_isa.ReduceOp.max

P = 128
D = 1024
DT = D // P
NP_ = 256
NS = 8
NT = NP_ + NS
NC = 1 + NS
H = 8
NOPE, ROPE = 64, 32
QK = NOPE + ROPE
QL, KL = 384, 256
QT, KT_ = QL // P, KL // P
CW = 512
CT = CW // P
NPG = 8
NPOOL = 80
E = 64
FE = 256
FT = FE // P
EPS = 1e-6
ROUTED = 2.5
BIG = 1e30
GATE0 = 672 + 5 * CW
SLOT = 8 * 768
NSLOT = 4

V_BADA, V_GMIX, V_GFFN, V_GQ, V_GKV, V_GV, V_CONV, V_W00, V_GQQ, V_GQK = 0, 48, 56, 64, 67, 69, 73, 85, 89, 90
NVEC = 91
T_Q, T_KV, T_CB, T_CC, T_CH, T_U, T_V = 0, 3, 5, 9, 13, 17, 21
NTILE = 25
STAGES = [("norm1", 1), ("in0", 6), ("in1", 20), ("cqn", 1), ("kvn", 1), ("krs", 1),
          ("q", 8), ("qswap", 8), ("qss", 8), ("k", 8), ("kss", 8), ("v", 2), ("self", 1), ("qlat", 1), ("s_pad", 2),
          ("know", 64), ("uvs", 4), ("att", 3 * H), ("vmean", 1), ("vvar", 1), ("vtr", 2), ("spat", 4),
          ("br", 48), ("out", 8), ("norm2", 1), ("rout", 3), ("gtr", 1), ("e_pad", 3), ("shared", 12), ("exp", 12 * E)]
BASE = {}
_n = 0
for _s, _c in STAGES:
    BASE[_s] = _n
    _n += _c
for _s in ("know", "exp"):
    assert BASE[_s] % 4 == 0, (_s, BASE[_s])

PAGES = [("pages", 2 * NPG)] * 4
ITEMS = [[("ada", 1)] * 3 + [("in0", 1), ("u", 1)] + PAGES + [("ga0", 1), ("ga1", 1), ("out0", 1), ("exp", 3)],
         [("ada", 1)] * 3 + [("cb", 1), ("v", 1)] + PAGES + [("gb0", 1), ("gb1", 1), ("out1", 1), ("exp", 3)],
         [("ada", 1)] * 3 + [("cc", 1), ("mla", 3), ("gc0", 1), ("gc1", 1), ("shared", 3), ("exp", 3)],
         [("ada", 1)] * 3 + [("ch", 1), ("late", 2), ("br0", 3), ("br1", 3), ("exp", 3)]]


def before(b, name):
    return [n for n, _ in ITEMS[b]].index(name)


def arrival(b, name):
    return 16 * sum(d for _, d in ITEMS[b][:before(b, name) + 1])


def build(nc, A, O):
    with ExitStack() as ctx:
        def sb(name, shape, dt=F32):
            return ctx.enter_context(nc.sbuf_tensor(name, shape, dt))

        def sem(name):
            return ctx.enter_context(nc.semaphore(name))

        ring = sb("ring", [P, NSLOT, SLOT])
        xT = sb("xT", [P, DT, NT])
        hT = sb("hT", [P, DT, NT])
        sq = sb("sq", [P, DT, NT])
        pT = sb("pT", [P, NTILE, NT])
        vec = sb("vec", [P, NVEC])
        cT = sb("cT", [P, DT, NC])
        csig = sb("csig", [P, DT, NC])
        ada = sb("ada", [P, 6, DT, NC])
        ones = sb("ones", [P, P])
        ident = sb("ident", [P, P])
        swapm = sb("swapm", [P, ROPE])
        cosT = sb("cosT", [P, NT])
        sinT = sb("sinT", [P, NT])
        mask = sb("mask", [P, 3 * P])
        rstd = sb("rstd", [P, NT])
        krT = sb("krT", [P, 2, NT])
        bsp = sb("bsp", [P, CT, P])
        brou = sb("brou", [P, E])
        wrou = sb("wrou", [P, DT, E])
        gqp = sb("gqp", [P, 1])
        qT = sb("qT", [P, H, NT])
        kT = sb("kT", [P, H, NT])
        vtok = sb("vtok", [P, 2, CW])
        oaT = sb("oaT", [P, CT, NT])
        ptab = sb("ptab", [1, NS * NPG], I32)
        qlat = sb("qlat", [P, KT_, NS, H])
        qrp = sb("qrp", [P, NS, H])
        qsg = sb("qsg", [P, H, NS])
        sself = sb("sself", [P, NS, H])
        ksq = sb("ksq", [P, 2, H * NOPE])
        krsq = sb("krsq", [P, NPG, ROPE])
        krss = sb("krss", [P, NPG])
        kss = sb("kss", [P, NPG, H])
        ssc = sb("ssc", [P, NPG, H])
        sp_ = sb("sp_", [P, 2, NPG, H])
        smx = sb("smx", [P, H])
        samx = sb("samx", [P, H])
        ssub = sb("ssub", [P, H])
        eself = sb("eself", [P, H])
        ssum = sb("ssum", [P, H])
        stot = sb("stot", [P, H])
        olat = sb("olat", [P, KT_, H, NS])
        olt = sb("olt", [P, KT_, H])
        abuf = sb("abuf", [P, 9 * P])
        am, aP, aPT = (abuf[:, j * 3 * P:(j + 1) * 3 * P] for j in range(3))
        amx = sb("amx", [P, 2])
        asum = sb("asum", [P, 2])
        arc = sb("arc", [P, 2])
        zp = sb("zp", [P, CT, 2 + NP_])
        zs = sb("zs", [P, CT, NS, 3])
        lg = sb("lg", [P, 3, E])
        ch = sb("ch", [P, 3, E])
        cm = sb("cm", [P, 3, E])
        top = sb("top", [P, 3, 8, 8])
        gsc = sb("gsc", [P, 3, 12])
        gtop = sb("gtop", [P, 3, 8])
        gms = sb("gms", [P, 3, 12])
        wsum = sb("wsum", [P, 3])
        gatesT = abuf[0:E, 0:NT]
        gsel = abuf[0:E, NT:3 * NT].rearrange("p (a t) -> p a t", a=2)
        kTf = kT[:].rearrange("p h t -> p (h t)")
        acts = kTf[:, 0:4 * NT].rearrange("p (a f t) -> p a f t", a=2, f=2)
        actg = kTf[:, 4 * NT:8 * NT].rearrange("p (a f t) -> p a f t", a=2, f=2)
        vn = kTf[:, 0:CT * NT].rearrange("p (k t) -> p k t", k=CT)
        vntok = kTf[:, CT * NT:CT * NT + 2 * CW].rearrange("p (b c) -> p b c", b=2)
        mg = qT
        yacc = pT[:, 0:DT, :]

        def part(b, at, *dims):
            n = int(np.prod(dims))
            ap = ring[:, b, at:at + n]
            if len(dims) == 2:
                return ap.rearrange("p (a b) -> p a b", a=dims[0])
            return ap.rearrange("p (a b c) -> p a b c", a=dims[0], b=dims[1])

        wuq = part(2, 0, QT, H * QK)
        wuk = part(2, QT * H * QK, KT_, H * NOPE)
        wuv = part(2, QT * H * QK + KT_ * H * NOPE, KT_, H * NOPE)
        wukT = part(3, 0, H, KL)[0:NOPE]
        wspT = part(3, H * KL, 8, P)
        pgR = [part(b, 0, NPG, KL + ROPE) for b in range(2)]
        pgT = [part(b, NPG * (KL + ROPE), NPG, 3, P) for b in range(2)]

        bk = [ctx.enter_context(nc.psum_tensor(f"bank{i}", [P, 512], F32)) for i in range(4)]
        pA = ctx.enter_context(nc.psum_tensor("pA", [P, 512], F32))
        pB = ctx.enter_context(nc.psum_tensor("pB", [P, 512], F32))
        pC = ctx.enter_context(nc.psum_tensor("pC", [P, 512], F32))
        pD = ctx.enter_context(nc.psum_tensor("pD", [P, 512], F32))

        full = [sem(f"bank_full{i}") for i in range(4)]
        free = [sem(f"bank_free{i}") for i in range(4)]
        wgt = [sem(f"slot_filled{i}") for i in range(NSLOT)]
        used = [sem(f"slot_used{i}") for i in range(NSLOT)]
        d_in = sem("small_inputs")
        d_late = sem("late_inputs")
        d_ptab = sem("page_table")
        d_out = sem("outputs")
        d_vout = sem("v_outputs")
        d_y = sem("y_output")
        c_dve = sem("vector_chain")
        c_act = sem("scalar_chain")
        s = {n: sem(n) for n in (
            "consts", "csig", "csilu", "ada_mm", "ada", "sq1", "var1", "rs1", "h1", "in_done", "gsig",
            "sqq", "varq", "rsq", "cqn", "sqkv", "varkv", "rskv", "ckv", "kvout", "krin", "krot",
            "qcopy", "qrot", "sqh", "varh", "rsh", "qn", "kcopy", "kfull", "kn", "vtok", "prodself", "sself",
            "qsg", "qlat", "s_mm", "ksq", "ksq_used", "kss", "rstds", "smx", "allmx", "ssub", "pexp", "psumd", "tot_mm",
            "pg_used", "pv", "olat", "oa_s",
            "amx", "aexp", "anorm", "aPT", "oa", "z", "conv", "vcen", "sqv", "varv", "rsv", "vn", "vntok", "sg", "wsp",
            "merged", "x1", "sq2", "var2", "rs2", "h2", "lsig", "gates", "gatesT", "gsel", "gbc", "gbc_used",
            "silu", "act", "act_used", "yout")}

        def bank(n):
            return n % 4, n // 4

        block = ctx.enter_context(nc.Block())

        @block.sync
        def _(sp):
            sp.dma_start(cT[:], A["cT"]).then_inc(d_in, 16)
            sp.dma_start(vec[:], A["vec"]).then_inc(d_in, 16)
            sp.dma_start(xT[:], A["xT"]).then_inc(d_in, 16)
            sp.dma_start(ptab[:], A["ptab"]).then_inc(d_ptab, 16)

            def cols(w, c0, nc_):
                return w.rearrange("(k p) c -> p k c", p=P)[:, :, c0:c0 + nc_]

            def reuse(b, name):
                sp.wait_ge(used[b], before(b, name))

            ada_w = A["w_ada"].rearrange("(k p) (n c) -> n p k c", p=P, c=512)
            for b in range(4):
                sp.dma_start(part(b, 0, DT, 512), ada_w[b]).then_inc(wgt[b], 16)
            with sp.Fori(1, 3) as i:
                for b in range(4):
                    sp.wait_ge(used[b], i)
                    sp.dma_start(part(b, 0, DT, 512), ada_w[bass.ds(i * 4 + b, 1)].rearrange("o p k c -> (o p) k c")
                                 ).then_inc(wgt[b], 16)
            reuse(0, "in0")
            sp.dma_start(part(0, 0, DT, 672), cols(A["w_in"], 0, 672)).then_inc(wgt[0], 16)
            for j, (b, name) in enumerate(((1, "cb"), (2, "cc"), (3, "ch"), (0, "u"), (1, "v"))):
                reuse(b, name)
                sp.dma_start(part(b, 0, DT, 512), cols(A["w_in"], 672 + j * 512, 512)).then_inc(wgt[b], 16)
            reuse(2, "mla")
            sp.dma_start(wuq, A["w_uq"]).then_inc(wgt[2], 16)
            sp.dma_start(wuk, A["w_uk"]).then_inc(wgt[2], 16)
            sp.dma_start(wuv, A["w_uv"]).then_inc(wgt[2], 16)
            reuse(3, "late")
            sp.dma_start(wukT, A["w_ukT"]).then_inc(wgt[3], 16)
            sp.dma_start(wspT, A["wspT"]).then_inc(wgt[3], 16)
            sp.wait_ge(d_ptab, 16)
            with sp.Fori(0, NS // 2) as i:
                for b in range(2):
                    sp.wait_ge(used[b], i + before(b, "pages"))
                    for j in range(NPG):
                        pg = sp.value_load(ptab[0:1, bass.ds(i * (2 * NPG) + (b * NPG + j), 1)],
                                           min_val=0, max_val=NPOOL - 1)
                        sp.dma_start(pgR[b][:, j, :], A["poolR"][bass.ds(pg, 1)].rearrange("o r c -> (o r) c")
                                     ).then_inc(wgt[b], 16)
                        sp.dma_start(pgT[b][:, j], A["poolT"][bass.ds(pg, 1)].rearrange("o p k c -> (o p) k c")
                                     ).then_inc(wgt[b], 16)
            for hf in range(2):
                for b, x in enumerate("abc"):
                    reuse(b, f"g{x}{hf}")
                    sp.dma_start(part(b, 0, DT, 512), cols(A["w_in"], GATE0 + b * D + hf * 512, 512)).then_inc(wgt[b], 16)
                reuse(3, f"br{hf}")
                for b, x in enumerate("abc"):
                    sp.dma_start(part(3, b * CT * 512, CT, 512), A[f"w_br_{x}"].rearrange("(k p) c -> p k c", p=P)
                                 [:, :, hf * 512:(hf + 1) * 512]).then_inc(wgt[3], 16)
            for b in range(2):
                reuse(b, f"out{b}")
                sp.dma_start(part(b, 0, DT, 512), cols(A["w_out"], b * 512, 512)).then_inc(wgt[b], 16)

            def expert(b, g, u, d):
                sp.dma_start(part(b, 0, DT, FE), g.rearrange("(k p) c -> p k c", p=P)).then_inc(wgt[b], 16)
                sp.dma_start(part(b, DT * FE, DT, FE), u.rearrange("(k p) c -> p k c", p=P)).then_inc(wgt[b], 16)
                sp.dma_start(part(b, 2 * DT * FE, FT, D), d.rearrange("(k p) c -> p k c", p=P)).then_inc(wgt[b], 16)

            reuse(2, "shared")
            expert(2, A["w_sh_gate"], A["w_sh_up"], A["w_sh_down"])

            def one(w, e):
                return A[w][bass.ds(e, 1)].rearrange("o r c -> (o r) c")

            with sp.Fori(0, E // 4) as i:
                for b in (3, 0, 1, 2):
                    sp.wait_ge(used[b], i + before(b, "exp"))
                    expert(b, *(one(w, i * 4 + (b + 1) % 4) for w in ("w_e_gate", "w_e_up", "w_e_down")))
            sp.wait_ge(s["yout"], 1)
            sp.dma_start(O["yT"], hT[:]).then_inc(d_y, 16)
            sp.wait_ge(d_y, 16)
            sp.wait_ge(d_out, 16 * 4)
            sp.wait_ge(d_vout, 16 * 2)

        @block.gpsimd
        def _(pool):
            nc.gpsimd.memset(ones[:], 1.0).then_inc(s["consts"], 1)
            nc.gpsimd.memset(qrp[:], 0.0).then_inc(s["consts"], 1)
            nc.gpsimd.memset(zp[:, :, 0:2], 0.0).then_inc(s["consts"], 1)
            for t, n in ((ident, "ident"), (swapm, "swapm"), (cosT, "cosT"), (sinT, "sinT"), (mask, "mask"),
                         (bsp, "bsp"),
                         (brou, "brou"), (wrou, "w_router")):
                pool.dma_start(t[:], A[n]).then_inc(d_late, 16)
            pool.dma_start(zs[:, :, :, 0:2], A["stateT"]).then_inc(d_late, 16)
            pool.wait_ge(d_late, 16 * 9)
            pool.wait_ge(wgt[3], arrival(3, "late"))
            nc.gpsimd.affine_select(out=wspT, in_=wspT, compare_op=ALU.is_ge, fill=0.0, base=0,
                                    pattern=[[0, 8], [1, P]], channel_multiplier=-1).then_inc(s["wsp"], 1)
            pool.wait_ge(s["ckv"], 1)
            pool.dma_start(O["ckvT"], pT[:, T_KV:T_KV + KT_, :]).then_inc(d_out, 16)
            pool.wait_ge(s["krot"], 1)
            pool.dma_start(O["krT"], krT[NOPE:QK, 1, :]).then_inc(d_out, 16)
            for q in range(NS):
                pool.wait_ge(s["smx"], q + 1)
                nc.gpsimd.partition_all_reduce(samx[:], smx[:], P, RMAX).then_inc(s["allmx"], 1)
            pool.wait_ge(s["z"], 1)
            pool.dma_start(O["convP"], zp[:, :, NP_:NP_ + 2]).then_inc(d_out, 16)
            pool.dma_start(O["convS"], zs[:, :, :, 1:3]).then_inc(d_out, 16)
            pool.wait_ge(s["vn"], 1)
            pool.dma_start(O["vnP"], vn[:, :, P:NP_]).then_inc(d_vout, 16)
            pool.dma_start(O["vnS"], vn[:, :, NP_:NT]).then_inc(d_vout, 16)

        @block.tensor
        def _(pe):
            def enter(n, i=None, per=0):
                b, k = bank(n)
                if i is not None:
                    pe.wait_ge(free[b], i * (per // 4) + k)
                elif k:
                    pe.wait_ge(free[b], k)
                return bk[b]

            def through(n, b):
                pe.wait_ge(full[n % 4], n // 4 + 1)
                pe.sem_inc(used[b], 1)

            def mm(out, lhsT, rhs, start, stop):
                return nc.tensor.matmul(out, lhsT, rhs, start=start, stop=stop)

            def sumsq(stage, src, nt, kp=P):
                n = BASE[stage]
                t = enter(n)
                for k in range(nt):
                    last = mm(t[:, 0:NT], ones[0:kp, :], src[0:kp, k, :], k == 0, k == nt - 1)
                last.then_inc(full[n % 4], 1)

            pe.wait_ge(s["csilu"], 1)
            with pe.Fori(0, 3) as i:
                for b in range(4):
                    pe.wait_ge(wgt[b], i * 16 + 16)
                    w = ring[:, b, 0:DT * 512].rearrange("p (k c) -> p k c", k=DT)
                    for m in range(4):
                        for k in range(DT):
                            last = mm(pA[:, bass.ds(i * (16 * NC) + (4 * b + m) * NC, NC)],
                                      w[:, k, m * P:(m + 1) * P], csig[:, k, :], k == 0, k == DT - 1)
                    last.then_inc(used[b], 1)
            pe.wait_ge(s["consts"], 3)
            pe.wait_ge(s["sq1"], 1)
            sumsq("norm1", sq, DT)

            pe.wait_ge(s["h1"], 2)
            pe.wait_ge(wgt[0], arrival(0, "in0"))
            w = part(0, 0, DT, 672)
            for m in range(6):
                n = BASE["in0"] + m
                t = enter(n)
                for k in range(DT):
                    if m < 5:
                        last = mm(t[:, 0:NT], w[:, k, m * P:(m + 1) * P], hT[:, k, :], k == 0, k == DT - 1)
                    else:
                        last = mm(t[NOPE:QK, 0:NT], w[:, k, 640:672], hT[:, k, :], k == 0, k == DT - 1)
                last.then_inc(full[n % 4], 1)
            through(n, 0)
            for c, (b, name) in enumerate(((1, "cb"), (2, "cc"), (3, "ch"), (0, "u"), (1, "v"))):
                pe.wait_ge(wgt[b], arrival(b, name))
                w = part(b, 0, DT, 512)
                for m in range(4):
                    n = BASE["in1"] + 4 * c + m
                    t = enter(n)
                    for k in range(DT):
                        last = mm(t[:, 0:NT], w[:, k, m * P:(m + 1) * P], hT[:, k, :], k == 0, k == DT - 1)
                    last.then_inc(full[n % 4], 1)
                through(n, b)

            pe.wait_ge(s["sqq"], 1)
            sumsq("cqn", sq, QT)
            sumsq("kvn", sq[:, QT:QT + KT_, :], KT_)
            pe.wait_ge(d_late, 16 * 9)
            n = BASE["krs"]
            t = enter(n)
            mm(t[NOPE:QK, 0:NT], swapm[NOPE:QK, :], krT[NOPE:QK, 0, :], True, True).then_inc(full[n % 4], 1)
            pe.wait_ge(s["cqn"], 1)
            pe.wait_ge(wgt[2], arrival(2, "mla"))
            for h in range(H):
                n = BASE["q"] + h
                t = enter(n)
                for k in range(QT):
                    last = mm(t[0:QK, 0:NT], wuq[:, k, h * QK:(h + 1) * QK], pT[:, T_Q + k, :], k == 0, k == QT - 1)
                last.then_inc(full[n % 4], 1)
            for h in range(H):
                n = BASE["qswap"] + h
                t = enter(n)
                pe.wait_ge(s["qcopy"], h + 1)
                mm(t[NOPE:QK, 0:NT], swapm[NOPE:QK, :], qT[NOPE:QK, h, :], True, True).then_inc(full[n % 4], 1)
            pe.wait_ge(s["sqh"], 1)
            for h in range(H):
                n = BASE["qss"] + h
                t = enter(n)
                mm(t[:, 0:NT], ones[0:QK, :], sq[0:QK, h, :], True, True).then_inc(full[n % 4], 1)
            pe.wait_ge(s["ckv"], 1)
            for h in range(H):
                n = BASE["k"] + h
                t = enter(n)
                for k in range(KT_):
                    last = mm(t[0:NOPE, 0:NT], wuk[:, k, h * NOPE:(h + 1) * NOPE], pT[:, T_KV + k, :],
                              k == 0, k == KT_ - 1)
                last.then_inc(full[n % 4], 1)
            pe.wait_ge(s["sqh"], 2)
            for h in range(H):
                n = BASE["kss"] + h
                t = enter(n)
                mm(t[:, 0:NT], ones[0:QK, :], sq[0:QK, h, :], True, True).then_inc(full[n % 4], 1)
            for b in range(2):
                n = BASE["v"] + b
                t = enter(n)
                for k in range(KT_):
                    last = mm(t[:], pT[:, T_KV + k, b * P:(b + 1) * P], wuv[:, k, :], k == 0, k == KT_ - 1)
                last.then_inc(full[n % 4], 1)
            pe.wait_ge(s["prodself"], 1)
            n = BASE["self"]
            t = enter(n)
            mm(t[:, 0:H * NS], ones[0:QK, :], sq[0:QK, 0, 0:H * NS], True, True).then_inc(full[n % 4], 1)
            pe.wait_ge(s["qsg"], 1)
            pe.wait_ge(wgt[3], arrival(3, "late"))
            n = BASE["qlat"]
            t = enter(n)
            for k in range(KT_):
                for h in range(H):
                    last = mm(t[:, (k * H + h) * NS:(k * H + h + 1) * NS], wukT[:, h, k * P:(k + 1) * P],
                              qsg[0:NOPE, h, :], True, True)
            last.then_inc(full[n % 4], 1)
            for n in range(BASE["s_pad"], BASE["s_pad"] + 2):
                enter(n)
                mm(bk[n % 4][:, 0:NC], ones[:], csig[:, 0, :], True, True).then_inc(full[n % 4], 1)

            pe.wait_ge(s["qlat"], 2)
            sco = [pA, pB]
            olp = [pC, pD]

            def keys(q, b, i, first):
                pe.wait_ge(wgt[b], (q - b) * (16 * NPG) + arrival(b, "pages"))
                if not first:
                    pe.wait_ge(s["smx"], q - 1)
                for j in range(NPG):
                    n = BASE["know"] + NPG * b + j
                    k_ = bank(n)
                    pe.wait_ge(free[k_[0]], (q - b) * 2 + k_[1])
                    for k in range(KT_):
                        last = mm(bk[k_[0]][:], pgT[b][:, j, k, :], wuk[:, k, :], k == 0, k == KT_ - 1)
                    last.then_inc(full[k_[0]], 1)
                    for k in range(KT_):
                        mm(sco[b][:, j * H:(j + 1) * H], pgT[b][:, j, k, :],
                           qlat[:, k, bass.ds(q, 1), :].rearrange("p o h -> p (o h)"), k == 0, False)
                    last = mm(sco[b][:, j * H:(j + 1) * H], pgT[b][:, j, 2, :],
                              qrp[:, bass.ds(q, 1), :].rearrange("p o h -> p (o h)"), False, True)
                last.then_inc(s["s_mm"], 1)

            def values(q, b, first):
                pe.wait_ge(s["psumd"], q + 1)
                if not first:
                    pe.wait_ge(s["olat"], q - 1)
                mm(olp[b][:, 64:64 + H], ones[:], ssum[:], True, True)
                for k in range(KT_):
                    for j in range(NPG):
                        last = mm(olp[b][:, k * H:(k + 1) * H], pgR[b][:, j, k * P:(k + 1) * P], sp_[:, b, j, :],
                                  j == 0, j == NPG - 1)
                last.then_inc(s["pv"], 1)
                pe.wait_ge(s["pv"], q + 1)
                pe.sem_inc(used[b], 1)

            for q in range(NS):
                keys(q, q % 2, None, q < 2)
                if q:
                    values(q - 1, 1 - q % 2, q - 1 < 2)
            values(NS - 1, 1, False)

            pe.wait_ge(s["olat"], NS)
            for c in range(CT):
                n = BASE["uvs"] + c
                t = enter(n)
                for o in range(2):
                    h = 2 * c + o
                    for k in range(KT_):
                        last = mm(t[o * 64:(o + 1) * 64, 0:NS], wuv[:, k, h * NOPE:(h + 1) * NOPE], olat[:, k, h, :],
                                  k == 0, k == KT_ - 1)
                last.then_inc(full[n % 4], 1)

            def a_scores(h):
                n = BASE["att"] + 3 * h
                t = enter(n)
                mm(t[:, 0:P], qT[0:QK, h, 0:P], kT[0:QK, h, 0:P], True, True)
                mm(t[:, P:3 * P], qT[0:QK, h, P:NP_], kT[0:QK, h, 0:NP_], True, True).then_inc(full[n % 4], 1)

            def a_out(h):
                n = BASE["att"] + 3 * h + 1
                t = enter(n)
                pe.wait_ge(s["anorm"], h + 1)
                for j in range(3):
                    last = nc.tensor.transpose(t[:, j * P:(j + 1) * P], aP[:, j * P:(j + 1) * P], ident[:])
                last.then_inc(full[n % 4], 1)
                n = BASE["att"] + 3 * h + 2
                t = enter(n)
                o = 64 * (h % 2)
                pe.wait_ge(s["aPT"], h + 1)
                v = vtok[:, :, h * NOPE:(h + 1) * NOPE]
                mm(t[o:o + 64, 0:P], v[:, 0, :], aPT[:, 0:P], True, True)
                mm(t[o:o + 64, P:NP_], v[:, 0, :], aPT[:, P:2 * P], True, False)
                mm(t[o:o + 64, P:NP_], v[:, 1, :], aPT[:, 2 * P:3 * P], False, True).then_inc(full[n % 4], 1)

            pe.wait_ge(full[n % 4], n // 4 + 1)
            pe.sem_inc(used[2], 1)
            pe.wait_ge(s["kn"], 1)
            pe.wait_ge(s["vtok"], 2)
            for h in range(H):
                a_scores(h)
                a_out(h)

            n = BASE["vmean"]
            t = enter(n)
            for k in range(CT):
                last = mm(t[:, 0:NT], ones[:], pT[:, T_V + k, :], k == 0, k == CT - 1)
            last.then_inc(full[n % 4], 1)
            pe.wait_ge(s["sqv"], 1)
            sumsq("vvar", sq, CT)
            pe.wait_ge(s["vn"], 1)
            for b in range(2):
                n = BASE["vtr"] + b
                t = enter(n)
                for k in range(CT):
                    last = nc.tensor.transpose(t[:, k * P:(k + 1) * P], vn[:, k, b * P:(b + 1) * P], ident[:])
                last.then_inc(full[n % 4], 1)
            pe.wait_ge(s["wsp"], 1)
            pe.wait_ge(s["vntok"], 2)
            for c in range(CT):
                n = BASE["spat"] + c
                t = enter(n)
                for o in range(2):
                    for b in range(2):
                        g = 2 * c + o
                        last = mm(t[64 * o:64 * o + 64, b * P:(b + 1) * P], vntok[:, b, g * 64:(g + 1) * 64],
                                  wspT[:, g, :], True, True)
                last.then_inc(full[n % 4], 1)

            through(n, 3)

            pe.wait_ge(s["oa"], H)
            pe.wait_ge(s["oa_s"], CT)
            pe.wait_ge(s["conv"], 1)
            pe.wait_ge(s["sg"], 1)
            src = [oaT[:, :, :], pT[:, T_CB:T_CB + CT, :], pT[:, T_U:T_U + CT, :]]
            for hf in range(2):
                for b, x in enumerate("abc"):
                    pe.wait_ge(wgt[b], arrival(b, f"g{x}{hf}"))
                pe.wait_ge(wgt[3], arrival(3, f"br{hf}"))
                for m in range(4):
                    for b in range(3):
                        n = BASE["br"] + 6 * (4 * hf + m) + b
                        t = enter(n)
                        for k in range(DT):
                            last = mm(t[:, 0:NT], part(b, 0, DT, 512)[:, k, m * P:(m + 1) * P], hT[:, k, :],
                                      k == 0, k == DT - 1)
                        last.then_inc(full[n % 4], 1)
                    for b in range(3):
                        n = BASE["br"] + 6 * (4 * hf + m) + 3 + b
                        t = enter(n)
                        for k in range(CT):
                            last = mm(t[:, 0:NT], part(3, b * CT * 512, CT, 512)[:, k, m * P:(m + 1) * P],
                                      src[b][:, k, :], k == 0, k == CT - 1)
                        last.then_inc(full[n % 4], 1)
                for b in range(4):
                    through(n, b)
            pe.wait_ge(s["merged"], DT)
            for m in range(DT):
                b = m // 4
                if m % 4 == 0:
                    pe.wait_ge(wgt[b], arrival(b, f"out{b}"))
                n = BASE["out"] + m
                t = enter(n)
                for k in range(DT):
                    last = mm(t[:, 0:NT], part(b, 0, DT, 512)[:, k, (m % 4) * P:(m % 4 + 1) * P], mg[:, k, :],
                              k == 0, k == DT - 1)
                last.then_inc(full[n % 4], 1)
                if m % 4 == 3:
                    through(n, b)
            pe.wait_ge(s["sq2"], 1)
            sumsq("norm2", sq, DT)
            pe.wait_ge(s["h2"], 2)
            for j, m in enumerate((P, P, NS)):
                n = BASE["rout"] + j
                t = enter(n)
                for k in range(DT):
                    last = mm(t[0:m, 0:E], hT[:, k, j * P:j * P + m], wrou[:, k, :], k == 0, k == DT - 1)
                last.then_inc(full[n % 4], 1)
            pe.wait_ge(s["gates"], 1)
            n = BASE["gtr"]
            t = enter(n)
            for j, m in enumerate((P, P, NS)):
                last = nc.tensor.transpose(t[0:E, j * P:j * P + m], lg[0:m, j, :], ident[0:m, 0:m])
            last.then_inc(full[n % 4], 1)
            for n in range(BASE["e_pad"], BASE["e_pad"] + 3):
                enter(n)
                mm(bk[n % 4][:, 0:NC], ones[:], csig[:, 0, :], True, True).then_inc(full[n % 4], 1)

            def ffn(slot_, n0, par, i, shared, k_par):
                down = part(slot_, 2 * DT * FE, FT, D)
                for f in range(FT):
                    for u in range(2):
                        n = n0 + 2 * f + u
                        t = enter(n, i, 48)
                        w = part(slot_, u * DT * FE, DT, FE)
                        for k in range(DT):
                            last = mm(t[:, 0:NT], w[:, k, f * P:(f + 1) * P], hT[:, k, :], k == 0, k == DT - 1)
                        last.then_inc(full[n % 4], 1)
                if not shared:
                    gb = [pC, pD][par]
                    pe.wait_ge(s["gsel"], k_par + 1)
                    mm(gb[:, 0:NT], ones[0:E, :], gsel[:, par, :], True, True).then_inc(s["gbc"], 1)
                pe.wait_ge(s["act"], (k_par + 2) * 2 if not shared else 2)
                for m in range(DT):
                    n = n0 + 4 + m
                    t = enter(n, i, 48)
                    for f in range(FT):
                        last = mm(t[:, 0:NT], down[:, f, m * P:(m + 1) * P], actg[:, par, f, :], f == 0, f == FT - 1)
                    last.then_inc(full[n % 4], 1)
                if i is None:
                    pe.wait_ge(full[n % 4], n // 4 + 1)
                else:
                    pe.wait_ge(full[n % 4], i * 12 + (n // 4 + 1))
                pe.sem_inc(used[slot_], 1)

            pe.wait_ge(wgt[2], arrival(2, "shared"))
            ffn(2, BASE["shared"], 1, None, True, 0)
            with pe.Fori(0, E // 4) as i:
                for b in range(4):
                    sl = (b + 3) % 4
                    pe.wait_ge(wgt[sl], i * 48 + arrival(sl, "exp"))
                    ffn(sl, BASE["exp"] + 12 * b, b % 2, i, False, i * 4 + b)

        @block.scalar
        def _(act):
            chain = [0]

            def link(ins):
                chain[0] += 1
                ins.then_inc(c_act, 1)
                act.wait_ge(c_act, chain[0])

            def fulls(n):
                b, k = bank(n)
                act.wait_ge(full[b], k + 1)
                return bk[b]

            act.wait_ge(d_in, 16 * 3)
            nc.scalar.activation(csig[:], cT[:], ACT.Sigmoid).then_inc(s["csig"], 1)
            nc.scalar.activation(sq[:], xT[:], ACT.Square).then_inc(s["sq1"], 1)
            act.wait_ge(s["var1"], 1)
            nc.scalar.activation(rstd[:], rstd[:], ACT.Sqrt).then_inc(s["rs1"], 1)
            for m in range(5):
                n = BASE["in0"] + m
                t = fulls(n)
                nc.scalar.activation(pT[:, m, :], t[:, 0:NT], ACT.Copy).then_inc(free[n % 4], 1)
            n = BASE["in0"] + 5
            t = fulls(n)
            nc.scalar.activation(krT[NOPE:QK, 0, :], t[NOPE:QK, 0:NT], ACT.Copy).then_inc(free[n % 4], 1)
            for b in range(4):
                act.wait_ge(free[b], (BASE["in0"] + 5 - b) // 4 + 1)
            act.sem_inc(s["krin"], 1)
            act.wait_ge(s["var1"], 1)
            nc.scalar.activation(sq[:, 0:QT + KT_, :], pT[:, T_Q:T_Q + QT + KT_, :], ACT.Square).then_inc(s["sqq"], 1)
            for j in range(20):
                n = BASE["in1"] + j
                t = fulls(n)
                nc.scalar.activation(pT[:, T_CB + j, :], t[:, 0:NT], ACT.Copy).then_inc(free[n % 4], 1)
            for b in range(4):
                act.wait_ge(free[b], (n - b) // 4 + 1)
            act.sem_inc(s["in_done"], 1)
            act.wait_ge(s["varq"], 1)
            link(nc.scalar.activation(rstd[:], rstd[:], ACT.Sqrt))
            act.sem_inc(s["rsq"], 1)
            act.wait_ge(s["varkv"], 1)
            nc.scalar.activation(rstd[:], rstd[:], ACT.Sqrt).then_inc(s["rskv"], 1)
            for h in range(H):
                n = BASE["q"] + h
                t = fulls(n)
                nc.scalar.activation(qT[0:QK, h, :], t[0:QK, 0:NT], ACT.Copy).then_inc(s["qcopy"], 1)
                act.wait_ge(s["qcopy"], h + 1)
                act.sem_inc(free[n % 4], 1)
            act.wait_ge(s["qrot"], 1)
            nc.scalar.activation(sq[0:QK, :, :], qT[0:QK, :, :], ACT.Square).then_inc(s["sqh"], 1)
            act.wait_ge(s["varh"], 1)
            big = pT[0:QK, T_CC:T_CC + H, :]
            nc.scalar.activation(big, big, ACT.Sqrt).then_inc(s["rsh"], 1)
            for h in range(H):
                n = BASE["k"] + h
                t = fulls(n)
                nc.scalar.activation(kT[0:NOPE, h, :], t[0:NOPE, 0:NT], ACT.Copy).then_inc(free[n % 4], 1)
            for b in range(4):
                act.wait_ge(free[b], (n - b) // 4 + 1)
            act.wait_ge(s["kfull"], 1)
            nc.scalar.activation(sq[0:QK, :, :], kT[0:QK, :, :], ACT.Square).then_inc(s["sqh"], 1)
            act.wait_ge(s["varh"], 2)
            nc.scalar.activation(big, big, ACT.Sqrt).then_inc(s["rsh"], 1)
            for b in range(2):
                n = BASE["v"] + b
                t = fulls(n)
                nc.scalar.activation(vtok[:, b, :], t[:], ACT.Copy).then_inc(s["vtok"], 1)
                act.wait_ge(s["vtok"], b + 1)
                act.sem_inc(free[n % 4], 1)
            for n in range(BASE["s_pad"], BASE["s_pad"] + 2):
                act.wait_ge(full[n % 4], n // 4 + 1)
                act.sem_inc(free[n % 4], 1)

            def squares(q):
                for j in range(NPG):
                    n = BASE["know"] + NPG * q + j
                    t = fulls(n)
                    if NPG * q + j >= 2:
                        act.wait_ge(s["ksq_used"], NPG * q + j - 1)
                    nc.scalar.activation(ksq[:, j % 2, :], t[:], ACT.Square).then_inc(s["ksq"], 1)
                    act.wait_ge(s["ksq"], NPG * q + j + 1)
                    act.sem_inc(free[n % 4], 1)

            def softmax(q):
                act.wait_ge(s["kss"], q + 1)
                nc.scalar.activation(kss[:], kss[:], ACT.Sqrt).then_inc(s["rstds"], 1)
                act.wait_ge(s["ssub"], q + 1)
                nc.scalar.activation(eself[:], ssub[:], ACT.Exp)
                if q >= 2:
                    act.wait_ge(s["pv"], q - 1)
                nc.scalar.activation(sp_[:, q % 2, :, :], ssc[:], ACT.Exp).then_inc(s["pexp"], 1)

            for q in range(NS):
                squares(q)
                softmax(q)
            for c in range(CT):
                n = BASE["uvs"] + c
                t = fulls(n)
                nc.scalar.activation(oaT[:, c, NP_:NT], t[:, 0:NS], ACT.Copy).then_inc(s["oa_s"], 1)
                act.wait_ge(s["oa_s"], c + 1)
                act.sem_inc(free[n % 4], 1)
            for h in range(H):
                act.wait_ge(s["amx"], h + 1)
                nc.scalar.activation(aP[:, 0:P], am[:, 0:P], ACT.Exp, bias=amx[:, 0:1], accum_out=asum[:, 0:1])
                nc.scalar.activation(aP[:, P:3 * P], am[:, P:3 * P], ACT.Exp, bias=amx[:, 1:2],
                                     accum_out=asum[:, 1:2]).then_inc(s["aexp"], 1)
                n = BASE["att"] + 3 * h + 1
                t = fulls(n)
                nc.scalar.activation(aPT, t[:, 0:3 * P], ACT.Copy).then_inc(s["aPT"], 1)
                act.wait_ge(s["aPT"], h + 1)
                act.sem_inc(free[n % 4], 1)
                n = BASE["att"] + 3 * h + 2
                t = fulls(n)
                o = 64 * (h % 2)
                nc.scalar.activation(oaT[o:o + 64, h // 2, 0:NP_], t[o:o + 64, 0:NP_], ACT.Copy).then_inc(s["oa"], 1)
                act.wait_ge(s["oa"], h + 1)
                act.sem_inc(free[n % 4], 1)
            act.wait_ge(s["vcen"], 1)
            nc.scalar.activation(sq[:, 0:CT, :], vn[:], ACT.Square).then_inc(s["sqv"], 1)
            act.wait_ge(s["varv"], 1)
            nc.scalar.activation(rstd[:], rstd[:], ACT.Sqrt).then_inc(s["rsv"], 1)
            for b in range(2):
                n = BASE["vtr"] + b
                t = fulls(n)
                nc.scalar.activation(vntok[:, b, :], t[:], ACT.Copy).then_inc(s["vntok"], 1)
                act.wait_ge(s["vntok"], b + 1)
                act.sem_inc(free[n % 4], 1)
            for m in range(DT):
                for b in range(3):
                    n = BASE["br"] + 6 * m + b
                    t = fulls(n)
                    if m >= 2:
                        act.wait_ge(s["merged"], m - 1)
                    nc.scalar.activation(sq[:, 3 * (m % 2) + b, :], t[:, 0:NT], ACT.Sigmoid).then_inc(s["gsig"], 1)
                    act.wait_ge(s["gsig"], 3 * m + b + 1)
                    act.sem_inc(free[n % 4], 1)
            act.wait_ge(s["x1"], 1)
            nc.scalar.activation(sq[:], xT[:], ACT.Square).then_inc(s["sq2"], 1)
            act.wait_ge(s["var2"], 1)
            nc.scalar.activation(rstd[:], rstd[:], ACT.Sqrt).then_inc(s["rs2"], 1)
            for j, m in enumerate((P, P, NS)):
                n = BASE["rout"] + j
                t = fulls(n)
                nc.scalar.activation(lg[0:m, j, :], t[0:m, 0:E], ACT.Sigmoid).then_inc(s["lsig"], 1)
                act.wait_ge(s["lsig"], j + 1)
                act.sem_inc(free[n % 4], 1)
            n = BASE["gtr"]
            t = fulls(n)
            nc.scalar.activation(gatesT, t[0:E, 0:NT], ACT.Copy).then_inc(s["gatesT"], 1)
            act.wait_ge(s["gatesT"], 1)
            act.sem_inc(free[n % 4], 1)
            for n in range(BASE["e_pad"], BASE["e_pad"] + 3):
                act.wait_ge(full[n % 4], n // 4 + 1)
                act.sem_inc(free[n % 4], 1)

            def silu(n0, par, i, done):
                for f in range(FT):
                    n = n0 + 2 * f
                    b, k = bank(n)
                    if i is None:
                        act.wait_ge(full[b], k + 1)
                    else:
                        act.wait_ge(full[b], i * 12 + (k + 1))
                        act.wait_ge(s["act"], done - 1)
                    nc.scalar.activation(acts[:, par, f, :], bk[b][:, 0:NT], ACT.Silu).then_inc(s["silu"], 1)
                    act.wait_ge(s["silu"], done + (f + 1))
                    act.sem_inc(free[b], 1)

            act.wait_ge(d_vout, 16 * 2)
            silu(BASE["shared"], 1, None, 0)
            with act.Fori(0, E // 4) as i:
                for b in range(4):
                    silu(BASE["exp"] + 12 * b, b % 2, i, i * 8 + (2 + 2 * b))

        @block.vector
        def _(dve):
            chain = [0]

            def link(ins):
                chain[0] += 1
                ins.then_inc(c_dve, 1)
                dve.wait_ge(c_dve, chain[0])

            def fulls(n):
                b, k = bank(n)
                dve.wait_ge(full[b], k + 1)
                return bk[b]

            V = nc.vector

            def inv_var(stage, width, out, np_=P):
                n = BASE[stage]
                t = fulls(n)
                link(V.tensor_scalar(out, t[0:np_, 0:NT], 1.0 / width, EPS, ALU.mult, ALU.add))
                dve.sem_inc(free[n % 4], 1)
                link(V.reciprocal(out, out))

            def rows(ap, k):
                return ap.unsqueeze(1).broadcast_to([ap.shape[0], k, ap.shape[1]])

            def lanes(ap, t):
                return ap.unsqueeze(2).broadcast_to([ap.shape[0], ap.shape[1], t])

            dve.wait_ge(d_in, 16 * 3)
            dve.wait_ge(s["csig"], 1)
            link(V.tensor_tensor(csig[:], csig[:], cT[:], ALU.mult))
            dve.sem_inc(s["csilu"], 1)
            dve.wait_ge(s["consts"], 3)
            inv_var("norm1", D, rstd[:])
            dve.sem_inc(s["var1"], 1)
            for b in range(4):
                dve.wait_ge(used[b], 3)
            adf = ada[:].rearrange("p s k c -> p (s k) c")
            link(V.tensor_tensor(adf, pA[:, 0:48 * NC].rearrange("p (m c) -> p m c", c=NC),
                                 lanes(vec[:, V_BADA:V_BADA + 48], NC), ALU.add))
            for j, g in ((1, V_GMIX), (4, V_GFFN)):
                link(V.scalar_tensor_tensor(out=ada[:, j], in0=ada[:, j], scalar=1.0, in1=lanes(vec[:, g:g + DT], NC),
                                            op0=ALU.add, op1=ALU.mult))

            def modulate(dst, j, rs, done):
                dve.wait_ge(rs, 1)
                link(V.tensor_tensor(dst[:], xT[:], rows(rstd[:], DT), ALU.mult))
                for k in range(DT):
                    last = V.tensor_scalar(dst[:, k, 0:NP_], dst[:, k, 0:NP_], ada[:, j + 1, k, 0:1],
                                           ada[:, j, k, 0:1], ALU.mult, ALU.add)
                last.then_inc(done, 1)
                link(V.tensor_tensor(dst[:, :, NP_:NT], dst[:, :, NP_:NT], ada[:, j + 1, :, 1:NC], ALU.mult))
                V.tensor_tensor(dst[:, :, NP_:NT], dst[:, :, NP_:NT], ada[:, j, :, 1:NC], ALU.add).then_inc(done, 1)

            modulate(hT, 0, s["rs1"], s["h1"])

            inv_var("cqn", QL, rstd[:])
            dve.sem_inc(s["varq"], 1)
            dve.wait_ge(s["rsq"], 1)
            for k in range(QT):
                last = V.scalar_tensor_tensor(out=pT[:, T_Q + k, :], in0=pT[:, T_Q + k, :],
                                              scalar=vec[:, V_GQ + k:V_GQ + k + 1], in1=rstd[:],
                                              op0=ALU.mult, op1=ALU.mult)
            link(last)
            dve.sem_inc(s["cqn"], 1)
            inv_var("kvn", KL, rstd[:])
            dve.sem_inc(s["varkv"], 1)
            dve.wait_ge(s["rskv"], 1)
            for k in range(KT_):
                last = V.scalar_tensor_tensor(out=pT[:, T_KV + k, :], in0=pT[:, T_KV + k, :],
                                              scalar=vec[:, V_GKV + k:V_GKV + k + 1], in1=rstd[:],
                                              op0=ALU.mult, op1=ALU.mult)
            link(last)
            dve.sem_inc(s["ckv"], 1)
            dve.wait_ge(s["in_done"], 1)
            dve.wait_ge(d_late, 16 * 9)
            V.tensor_tensor(zp[:, :, 2:2 + NP_], pT[:, T_CC:T_CC + CT, 0:NP_], pT[:, T_CH:T_CH + CT, 0:NP_], ALU.mult)
            link(V.tensor_tensor(zs[:, :, :, 2:3].rearrange("p k s o -> p k (s o)"), pT[:, T_CC:T_CC + CT, NP_:NT],
                                 pT[:, T_CH:T_CH + CT, NP_:NT], ALU.mult))
            dve.sem_inc(s["z"], 1)
            n = BASE["krs"]
            t = fulls(n)
            R = slice(NOPE, QK)
            link(V.tensor_tensor(krT[R, 1, :], t[R, 0:NT], sinT[R, :], ALU.mult))
            dve.sem_inc(free[n % 4], 1)
            dve.wait_ge(s["krin"], 1)
            link(V.tensor_tensor(krT[R, 0, :], krT[R, 0, :], cosT[R, :], ALU.mult))
            link(V.tensor_tensor(krT[R, 1, :], krT[R, 0, :], krT[R, 1, :], ALU.add))
            dve.sem_inc(s["krot"], 1)
            big = pT[:, T_CC:T_CC + H, :]
            for h in range(H):
                n = BASE["qswap"] + h
                t = fulls(n)
                link(V.tensor_tensor(big[R, h, :], t[R, 0:NT], sinT[R, :], ALU.mult))
                dve.sem_inc(free[n % 4], 1)
            link(V.tensor_tensor(qT[R], qT[R], rows(cosT[R, :], H), ALU.mult))
            link(V.tensor_tensor(qT[R], qT[R], big[R], ALU.add))
            dve.sem_inc(s["qrot"], 1)
            link(V.tensor_scalar(gqp[:], vec[:, V_GQQ:V_GQQ + 1], QK ** -0.5, None, ALU.mult))

            def head_norm(stage, dst, g, turn):
                for h in range(H):
                    n = BASE[stage] + h
                    t = fulls(n)
                    link(V.tensor_scalar(big[0:QK, h, :], t[0:QK, 0:NT], 1.0 / QK, EPS, ALU.mult, ALU.add))
                    dve.sem_inc(free[n % 4], 1)
                link(V.reciprocal(big[0:QK], big[0:QK]))
                dve.sem_inc(s["varh"], 1)
                dve.wait_ge(s["rsh"], turn)
                link(V.scalar_tensor_tensor(out=dst[0:QK], in0=dst[0:QK], scalar=g, in1=big[0:QK],
                                            op0=ALU.mult, op1=ALU.mult))

            head_norm("qss", qT, gqp[0:QK, :], 1)
            dve.sem_inc(s["qn"], 1)
            V.tensor_copy(kT[R, :, :], rows(krT[R, 1, :], H)).then_inc(s["kfull"], 1)
            head_norm("kss", kT, vec[0:QK, V_GQK:V_GQK + 1], 2)
            dve.sem_inc(s["kn"], 1)
            link(V.tensor_tensor(sq[0:QK, 0, 0:H * NS].rearrange("p (h s) -> p h s", h=H), qT[0:QK, :, NP_:NT],
                                 kT[0:QK, :, NP_:NT], ALU.mult))
            dve.sem_inc(s["prodself"], 1)
            link(V.tensor_scalar(qsg[0:QK], qT[0:QK, :, NP_:NT], vec[0:QK, V_GQK:V_GQK + 1], None, ALU.mult))
            dve.sem_inc(s["qsg"], 1)
            link(V.tensor_copy(qrp[R].rearrange("p s h -> p h s"), qsg[R]))
            dve.sem_inc(s["qlat"], 1)
            n = BASE["self"]
            t = fulls(n)
            link(V.tensor_copy(sself[:].rearrange("p s h -> p h s"), t[:, 0:H * NS].rearrange("p (h s) -> p h s", h=H)))
            dve.sem_inc(free[n % 4], 1)
            n = BASE["qlat"]
            t = fulls(n)
            for k in range(KT_):
                last = V.tensor_copy(qlat[:, k].rearrange("p s h -> p h s"),
                                     t[:, k * H * NS:(k + 1) * H * NS].rearrange("p (h s) -> p h s", h=H))
            link(last)
            dve.sem_inc(free[n % 4], 1)
            dve.sem_inc(s["qlat"], 1)

            def finish(q):
                b = q % 2
                o = [pC, pD][b]
                dve.wait_ge(s["pv"], q + 1)
                link(V.tensor_tensor(stot[:], o[:, 64:64 + H], eself[:], ALU.add))
                link(V.reciprocal(stot[:], stot[:]))
                for k in range(KT_):
                    last = V.scalar_tensor_tensor(out=olt[:, k, :], in0=eself[:],
                                                  scalar=pT[:, T_KV + k, NP_ + q:NP_ + q + 1],
                                                  in1=o[:, k * H:(k + 1) * H], op0=ALU.mult, op1=ALU.add)
                link(last)
                link(V.tensor_tensor(olat[:, :, :, q], olt[:], rows(stot[:], KT_), ALU.mult))
                dve.sem_inc(s["olat"], 1)

            for q in range(NS):
                b = q % 2
                dve.wait_ge(wgt[b], (q // 2) * (16 * 2 * NPG) + arrival(b, "pages"))
                link(V.tensor_tensor(krsq[:], pgR[b][:, :, KL:KL + ROPE], pgR[b][:, :, KL:KL + ROPE], ALU.mult))
                link(V.tensor_reduce(out=krss[:], in_=krsq[:], op=ALU.add, axis=AX.X))
                for j in range(NPG):
                    dve.wait_ge(s["ksq"], NPG * q + j + 1)
                    V.tensor_reduce(out=kss[:, j, :], in_=ksq[:, j % 2, :].rearrange("p (h d) -> p h d", h=H),
                                    op=ALU.add, axis=AX.X).then_inc(s["ksq_used"], 1)
                dve.wait_ge(s["ksq_used"], NPG * (q + 1))
                link(V.tensor_tensor(kss[:], kss[:], lanes(krss[:], H), ALU.add))
                link(V.tensor_scalar(kss[:], kss[:], 1.0 / QK, EPS, ALU.mult, ALU.add))
                link(V.reciprocal(kss[:], kss[:]))
                dve.sem_inc(s["kss"], 1)
                dve.wait_ge(s["rstds"], q + 1)
                dve.wait_ge(s["s_mm"], q + 1)
                if q:
                    finish(q - 1)
                link(V.tensor_tensor(ssc[:], [pA, pB][b][:, 0:NPG * H].rearrange("p (j h) -> p j h", h=H), kss[:],
                                     ALU.mult))
                link(V.tensor_reduce(out=smx[:], in_=ssc[:].rearrange("p j h -> p h j"), op=ALU.max, axis=AX.X))
                dve.sem_inc(s["smx"], 1)
                dve.wait_ge(s["allmx"], q + 1)
                link(V.tensor_tensor(samx[:], samx[:], sself[:, q, :], ALU.max))
                V.tensor_tensor(ssub[:], sself[:, q, :], samx[:], ALU.subtract)
                link(V.tensor_tensor(ssc[:], ssc[:], rows(samx[:], NPG), ALU.subtract))
                dve.sem_inc(s["ssub"], 1)
                dve.wait_ge(s["pexp"], q + 1)
                link(V.tensor_reduce(out=ssum[:], in_=sp_[:, b].rearrange("p j h -> p h j"), op=ALU.add, axis=AX.X))
                dve.sem_inc(s["psumd"], 1)
            finish(NS - 1)

            for h in range(H):
                n = BASE["att"] + 3 * h
                t = fulls(n)
                if h:
                    dve.wait_ge(s["anorm"], h)
                link(V.tensor_tensor(am, t[:, 0:3 * P], mask[:], ALU.add))
                dve.sem_inc(free[n % 4], 1)
                V.tensor_reduce(out=amx[:, 0:1], in_=am[:, 0:P], op=ALU.max, axis=AX.X)
                link(V.tensor_reduce(out=amx[:, 1:2], in_=am[:, P:3 * P], op=ALU.max, axis=AX.X))
                link(V.tensor_scalar(amx[:], amx[:], -1.0, None, ALU.mult))
                dve.sem_inc(s["amx"], 1)
                dve.wait_ge(s["aexp"], h + 1)
                link(V.reciprocal(arc[:], asum[:]))
                V.tensor_scalar(aP[:, 0:P], aP[:, 0:P], arc[:, 0:1], None, ALU.mult)
                V.tensor_scalar(aP[:, P:3 * P], aP[:, P:3 * P], arc[:, 1:2], None, ALU.mult).then_inc(s["anorm"], 1)

            out = pT[:, T_CC:T_CC + CT, :]
            for k in range(CT):
                w = [vec[:, V_CONV + j * CT + k:V_CONV + j * CT + k + 1] for j in range(3)]
                V.tensor_scalar(out[:, k, 0:NP_], zp[:, k, 0:NP_], w[0], None, ALU.mult)
                link(V.tensor_scalar(out[:, k, NP_:NT], zs[:, k, :, 0], w[0], None, ALU.mult))
                for j in (1, 2):
                    V.scalar_tensor_tensor(out=out[:, k, 0:NP_], in0=zp[:, k, j:j + NP_], scalar=w[j],
                                           in1=out[:, k, 0:NP_], op0=ALU.mult, op1=ALU.add)
                    link(V.scalar_tensor_tensor(out=out[:, k, NP_:NT], in0=zs[:, k, :, j], scalar=w[j],
                                                in1=out[:, k, NP_:NT], op0=ALU.mult, op1=ALU.add))
            link(V.tensor_tensor(pT[:, T_CB:T_CB + CT, :], pT[:, T_CB:T_CB + CT, :], out, ALU.mult))
            dve.sem_inc(s["conv"], 1)

            n = BASE["vmean"]
            t = fulls(n)
            link(V.tensor_scalar(rstd[:], t[:, 0:NT], 1.0 / CW, None, ALU.mult))
            dve.sem_inc(free[n % 4], 1)
            link(V.tensor_tensor(vn[:], pT[:, T_V:T_V + CT, :], rows(rstd[:], CT), ALU.subtract))
            dve.sem_inc(s["vcen"], 1)
            inv_var("vvar", CW, rstd[:])
            dve.sem_inc(s["varv"], 1)
            dve.wait_ge(s["rsv"], 1)
            for k in range(CT):
                last = V.scalar_tensor_tensor(out=vn[:, k, :], in0=vn[:, k, :],
                                              scalar=vec[:, V_GV + k:V_GV + k + 1], in1=rstd[:],
                                              op0=ALU.mult, op1=ALU.mult)
            link(last)
            dve.sem_inc(s["vn"], 1)
            for c in range(CT):
                n = BASE["spat"] + c
                t = fulls(n)
                link(V.tensor_tensor(big[:, c, 0:NP_].rearrange("p (b t) -> p b t", b=2),
                                     t[:, 0:NP_].rearrange("p (b t) -> p b t", b=2), rows(bsp[:, c, :], 2), ALU.add))
                dve.sem_inc(free[n % 4], 1)
                link(V.tensor_scalar(big[:, c, NP_:NT], vn[:, c, NP_:NT], vec[:, V_W00 + c:V_W00 + c + 1],
                                     bsp[:, c, 0:1], ALU.mult, ALU.add))
            link(V.tensor_tensor(pT[:, T_U:T_U + CT, :], pT[:, T_U:T_U + CT, :], big[:, 0:CT, :], ALU.mult))
            dve.sem_inc(s["sg"], 1)

            for m in range(DT):
                for b in range(3):
                    n = BASE["br"] + 6 * m + 3 + b
                    t = fulls(n)
                    dve.wait_ge(s["gsig"], 3 * m + b + 1)
                    gs = sq[:, 3 * (m % 2):3 * (m % 2) + 3, :]
                    link(V.tensor_tensor(gs[:, b, :], t[:, 0:NT], gs[:, b, :], ALU.mult))
                    dve.sem_inc(free[n % 4], 1)
                link(V.tensor_tensor(gs[:, 0, :], gs[:, 0, :], gs[:, 1, :], ALU.add))
                link(V.tensor_tensor(mg[:, m, :], gs[:, 0, :], gs[:, 2, :], ALU.add))
                dve.sem_inc(s["merged"], 1)

            def residual(dst, ps, j, m):
                V.scalar_tensor_tensor(out=dst[:, m, 0:NP_], in0=ps[:, 0:NP_], scalar=ada[:, j, m, 0:1],
                                       in1=xT[:, m, 0:NP_], op0=ALU.mult, op1=ALU.add)
                link(V.tensor_tensor(sq[:, 7, 0:NS], ps[:, NP_:NT], ada[:, j, m, 1:NC], ALU.mult))
                link(V.tensor_tensor(dst[:, m, NP_:NT], sq[:, 7, 0:NS], xT[:, m, NP_:NT], ALU.add))

            for m in range(DT):
                n = BASE["out"] + m
                t = fulls(n)
                residual(xT, t, 2, m)
                dve.sem_inc(free[n % 4], 1)
            dve.sem_inc(s["x1"], 1)
            inv_var("norm2", D, rstd[:])
            dve.sem_inc(s["var2"], 1)
            modulate(hT, 3, s["rs2"], s["h2"])

            dve.wait_ge(s["lsig"], 3)
            for j, m in enumerate((P, P, NS)):
                link(V.tensor_tensor(ch[0:m, j], lg[0:m, j], brou[0:m], ALU.add))
                for g in range(8):
                    last = V.max(top[0:m, j, g, :], ch[0:m, j, g * 8:(g + 1) * 8])
                link(last)
                link(V.tensor_tensor(gsc[0:m, j, 0:8], top[0:m, j, :, 0], top[0:m, j, :, 1], ALU.add))
                link(V.max(gtop[0:m, j], gsc[0:m, j, 0:8]))
                V.memset(gsc[0:m, j, 8:12], 3 * BIG)
                link(V.memset(gtop[0:m, j, 4:8], 3 * BIG))
                link(V.match_replace(out=gms[0:m, j], in_to_replace=gtop[0:m, j], in_values=gsc[0:m, j],
                                     imm_value=-BIG))
                link(V.tensor_scalar(gms[0:m, j], gms[0:m, j], -BIG, BIG, ALU.is_equal, ALU.mult))
                link(V.tensor_scalar(gms[0:m, j], gms[0:m, j], BIG, None, ALU.subtract))
                g3 = lanes(gms[0:m, j, 0:8], 8)
                c3 = ch[0:m, j].rearrange("p (g e) -> p g e", g=8)
                m3 = cm[0:m, j].rearrange("p (g e) -> p g e", g=8)
                link(V.tensor_tensor(m3, c3, g3, ALU.add))
                link(V.max(gtop[0:m, j], cm[0:m, j]))
                link(V.match_replace(out=ch[0:m, j], in_to_replace=gtop[0:m, j], in_values=cm[0:m, j],
                                     imm_value=-3 * BIG))
                link(V.tensor_scalar(ch[0:m, j], ch[0:m, j], -3 * BIG, None, ALU.is_equal))
                link(V.tensor_tensor(lg[0:m, j], lg[0:m, j], ch[0:m, j], ALU.mult))
                link(V.tensor_reduce(out=wsum[0:m, j:j + 1], in_=lg[0:m, j], op=ALU.add, axis=AX.X))
                link(V.reciprocal(wsum[0:m, j:j + 1], wsum[0:m, j:j + 1]))
                link(V.tensor_scalar(lg[0:m, j], lg[0:m, j], wsum[0:m, j:j + 1], ROUTED, ALU.mult, ALU.mult))
            dve.sem_inc(s["gates"], 1)
            dve.wait_ge(s["gatesT"], 1)

            n0 = BASE["shared"]
            for f in range(FT):
                n = n0 + 2 * f + 1
                t = fulls(n)
                dve.wait_ge(s["silu"], f + 1)
                V.tensor_tensor(actg[:, 1, f, :], acts[:, 1, f, :], t[:, 0:NT], ALU.mult).then_inc(s["act"], 1)
                dve.wait_ge(s["act"], f + 1)
                dve.sem_inc(free[n % 4], 1)
            for m in range(DT):
                n = n0 + 4 + m
                t = fulls(n)
                link(V.tensor_copy(yacc[:, m, :], t[:, 0:NT]))
                dve.sem_inc(free[n % 4], 1)
            base = chain[0]
            PER = 13

            with dve.Fori(0, E // 4) as i:
                for b in range(4):
                    at = [PER * b]

                    def step(ins):
                        at[0] += 1
                        ins.then_inc(c_dve, 1)
                        dve.wait_ge(c_dve, i * (4 * PER) + (base + at[0]))

                    par = b % 2
                    n0 = BASE["exp"] + 12 * b
                    step(V.tensor_scalar(gsel[:, par, :], gatesT, ident[0:E, bass.ds(i * 4 + b, 1)], None, ALU.mult))
                    dve.sem_inc(s["gsel"], 1)
                    for f in range(FT):
                        n = n0 + 2 * f + 1
                        dve.wait_ge(full[n % 4], i * 12 + (n // 4 + 1))
                        dve.wait_ge(s["silu"], i * 8 + (2 * b + f + 3))
                        step(V.tensor_tensor(actg[:, par, f, :], acts[:, par, f, :], bk[n % 4][:, 0:NT], ALU.mult))
                        dve.sem_inc(free[n % 4], 1)
                    dve.wait_ge(s["gbc"], i * 4 + (b + 1))
                    g = [pC, pD][par]
                    for f in range(FT):
                        step(V.tensor_tensor(actg[:, par, f, :], actg[:, par, f, :], g[:, 0:NT], ALU.mult))
                        dve.sem_inc(s["act"], 1)
                    for m in range(DT):
                        n = n0 + 4 + m
                        dve.wait_ge(full[n % 4], i * 12 + (n // 4 + 1))
                        step(V.tensor_tensor(yacc[:, m, :], yacc[:, m, :], bk[n % 4][:, 0:NT], ALU.add))
                        dve.sem_inc(free[n % 4], 1)
                    assert at[0] == PER * (b + 1)
            chain[0] = base + PER * E
            for m in range(DT):
                residual(hT, yacc[:, m, :], 5, m)
            dve.sem_inc(s["yout"], 1)


def _constants():
    pos = np.concatenate([np.arange(NP_), np.full(NS, NPG * P)]).astype(np.float32)
    inv = (np.float32(10000.0) ** (-np.arange(0, ROPE, 2, dtype=np.float32) / np.float32(ROPE))).astype(np.float32)
    ang = (pos[:, None] * inv[None, :]).astype(np.float32).T
    cos, sin = np.zeros((P, NT), np.float32), np.zeros((P, NT), np.float32)
    cos[NOPE:QK] = np.concatenate([np.cos(ang), np.cos(ang)])
    sin[NOPE:QK] = np.concatenate([np.sin(ang), np.sin(ang)])
    swap = np.zeros((P, ROPE), np.float32)
    h = ROPE // 2
    for j in range(h):
        swap[NOPE + h + j, j] = -1.0
        swap[NOPE + j, h + j] = 1.0
    t = np.arange(P)
    tri = np.where(t[None, :] <= t[:, None], 0.0, -BIG).astype(np.float32)
    mask = np.concatenate([tri, np.zeros((P, P), np.float32), tri], axis=1)
    return {"ident": np.eye(P, dtype=np.float32), "swapm": swap, "cosT": cos, "sinT": sin, "mask": mask}


_OUTS = {"yT": (P, DT, NT), "ckvT": (P, KT_, NT), "krT": (ROPE, NT), "convP": (P, CT, 2), "convS": (P, CT, NS, 2),
         "vnP": (P, CT, P), "vnS": (P, CT, NS)}


def kernel(**inputs):
    import concourse.bacc as _bacc
    from concourse.bass_utils import run_bass_kernel_spmd as _run

    a = {k: np.asarray(v) for k, v in inputs.items()}
    a = {k: (v[0] if v.ndim > 1 and k not in ("x_prompt", "x_sample", "page_table", "c_prompt", "c_sample") else v)
         for k, v in a.items()}

    def feat(v, t):
        return v.T.reshape(t, P, -1).transpose(1, 0, 2)

    def wrows(w):
        return w.reshape(-1, P, w.shape[-1]).transpose(1, 0, 2)

    x = np.concatenate([a["x_prompt"][0], a["x_sample"][:, 0]], axis=0)
    c = np.concatenate([a["c_prompt"], a["c_sample"]], axis=0)
    vecs = [v.reshape(-1, P).T for v in (a["b_ada"], a["g_norm_mix"], a["g_norm_ffn"], a["g_q_lat"], a["g_kv_lat"],
                                         a["g_v_ln"], a["w_conv"].reshape(-1), np.repeat(a["w_spatial"][:, 0, 0], 64))]
    vecs += [np.pad(a[g], (0, P - QK))[:, None] for g in ("g_qk_q", "g_qk_k")]
    lat = a["cache_kv_latent"]
    kr = a["cache_k_rope"]
    latT = lat.transpose(0, 2, 1).reshape(NPOOL, KT_, P, P).transpose(0, 2, 1, 3)
    krT = np.pad(kr.transpose(0, 2, 1), ((0, 0), (NOPE, P - QK), (0, 0)))[:, :, None, :]
    arrays = {
        "xT": feat(x, DT), "cT": feat(c, DT), "vec": np.concatenate(vecs, axis=1),
        "ptab": a["page_table"].reshape(1, -1).astype(np.int32),
        "poolR": np.concatenate([lat, kr], axis=2), "poolT": np.concatenate([latT, krT], axis=2),
        "stateT": a["state_conv"].transpose(2, 0, 1).reshape(CT, P, NS, 2).transpose(1, 0, 2, 3),
        "w_uq": wrows(a["w_uq"].reshape(QL, -1)), "w_uk": wrows(a["w_uk"].reshape(KL, -1)),
        "w_uv": wrows(a["w_uv"].reshape(KL, -1)), "w_ukT": a["w_uk"].transpose(2, 1, 0),
        "wspT": a["w_spatial"].transpose(2, 0, 1), "w_router": wrows(a["w_router"]),
        "bsp": np.repeat(a["b_spatial"].reshape(CT, 2, 1, P), 64, axis=2).reshape(CT, P, P).transpose(1, 0, 2),
        "brou": np.broadcast_to(a["b_router"], (P, E)),
    }
    for k in ("w_ada", "w_in", "w_br_a", "w_br_b", "w_br_c", "w_out", "w_sh_gate", "w_sh_up", "w_sh_down",
              "w_e_gate", "w_e_up", "w_e_down"):
        arrays[k] = a[k]
    arrays.update(_constants())
    arrays = {k: np.ascontiguousarray(v) for k, v in arrays.items()}

    nc = _bacc.Bacc("TRN2", target_bir_lowering=False, num_devices=1)
    A = {k: nc.dram_tensor(f"in_{k}", v.shape, mybir.dt.from_np(v.dtype), kind="ExternalInput").ap()
         for k, v in arrays.items()}
    O = {k: nc.dram_tensor(f"out_{k}", v, F32, kind="ExternalOutput").ap() for k, v in _OUTS.items()}
    build(nc, A, O)
    r = _run(nc, [{f"in_{k}": v for k, v in arrays.items()}], core_ids=[0]).results[0]
    o = {k: np.asarray(r[f"out_{k}"]) for k in _OUTS}

    def tokens(v):
        return v.transpose(1, 0, 2).reshape(-1, v.shape[2]).T

    y, ckv, krope = tokens(o["yT"]), tokens(o["ckvT"]), o["krT"].T
    conv_p, vn_p, vn_s = tokens(o["convP"]), tokens(o["vnP"]), tokens(o["vnS"])
    conv_s = o["convS"].transpose(2, 3, 1, 0).reshape(NS, 2, CW)
    c_ = np.ascontiguousarray
    return (c_(y[None, :NP_]), c_(y[NP_:, None]), c_(ckv[None, None, :NP_]), c_(krope[None, None, :NP_]),
            c_(conv_p[None, None]), c_(vn_p[None, None]), c_(ckv[None, NP_:, None]), c_(krope[None, NP_:, None]),
            c_(conv_s[None]), c_(vn_s[None, :, None]))
```

```python
from contextlib import ExitStack

import numpy as np
import concourse.bass as bass
from concourse import mybir

ALU = mybir.AluOpType
ACT = mybir.ActivationFunctionType
AX = mybir.AxisListType
F32 = mybir.dt.float32
I32 = mybir.dt.int32
RMAX = bass.bass_isa.ReduceOp.max

P = 128
D = 1024
DT = D // P
NP_ = 256
NS = 8
NT = NP_ + NS
NC = 1 + NS
H = 8
NOPE, ROPE = 64, 32
QK = NOPE + ROPE
QL, KL = 384, 256
QT, KT_ = QL // P, KL // P
CW = 512
CT = CW // P
NPG = 8
NPOOL = 80
E = 64
FE = 256
FT = FE // P
EPS = 1e-6
ROUTED = 2.5
BIG = 1e30
GATE0 = 672 + 5 * CW
SLOT = 8 * 768
NSLOT = 4

V_BADA, V_GMIX, V_GFFN, V_GQ, V_GKV, V_GV, V_CONV, V_W00, V_GQQ, V_GQK = 0, 48, 56, 64, 67, 69, 73, 85, 89, 90
NVEC = 91
T_Q, T_KV, T_CB, T_CC, T_CH, T_U, T_V = 0, 3, 5, 9, 13, 17, 21
NTILE = 25
STAGES = [("norm1", 1), ("in0", 6), ("in1", 20), ("cqn", 1), ("kvn", 1), ("krs", 1),
          ("q", 8), ("qswap", 8), ("qss", 8), ("k", 8), ("kss", 8), ("v", 2), ("self", 1), ("qlat", 1), ("s_pad", 2),
          ("know", 64), ("uvs", 4), ("att", 3 * H), ("vmean", 1), ("vvar", 1), ("vtr", 2), ("spat", 4),
          ("br", 48), ("out", 8), ("norm2", 1), ("rout", 3), ("h2tr", 6), ("shgu", 4), ("pos", 1), ("shdn", 8), ("pad", 1),
          ("moe", 8 + 12 * (E // 2 - 3) + 11 + 9 + 8), ("fgates", 4), ("fexp", 12 * E)]
BASE = {}
_n = 0
for _s, _c in STAGES:
    BASE[_s] = _n
    _n += _c
for _s in ("know", "moe", "fgates", "fexp"):
    assert BASE[_s] % 4 == 0, (_s, BASE[_s])

CAP = 64
LIMIT = 64
NPAIR = E // 2
USE = {}
_n = BASE["moe"]


def _use(*key):
    global _n
    USE[key] = _n
    _n += 1


_use("G", 0)
_use("G", 1)
_use("X", 0, 0)
_use("X", 0, 1)
for _p in range(NPAIR):
    if _p + 2 < NPAIR:
        _use("G", _p + 2)
    if _p + 1 < NPAIR:
        _use("X", _p + 1, 0)
        _use("X", _p + 1, 1)
    for _m in range(4 if _p else 0):
        _use("C", _p - 1, _m)
    _use("T", _p)
    for _m in range(4 if _p else 0):
        _use("C", _p - 1, _m + 4)
for _m in range(8):
    _use("C", NPAIR - 1, _m)
assert _n == BASE["fgates"]


def turn(i, n, per):
    return n if i is None else i * (4 * per) + n


PAGES = [("pages", 2 * NPG)] * 4
ITEMS = [[("ada", 1)] * 3 + [("in0", 1), ("u", 1)] + PAGES + [("ga0", 1), ("ga1", 1), ("out0", 1), ("exp", 3)],
         [("ada", 1)] * 3 + [("cb", 1), ("v", 1)] + PAGES + [("gb0", 1), ("gb1", 1), ("out1", 1), ("exp", 3)],
         [("ada", 1)] * 3 + [("cc", 1), ("mla", 3), ("gc0", 1), ("gc1", 1), ("shared", 3), ("exp", 3)],
         [("ada", 1)] * 3 + [("ch", 1), ("late", 2), ("br0", 3), ("br1", 3), ("exp", 3)]]


def before(b, name):
    return [n for n, _ in ITEMS[b]].index(name)


def arrival(b, name):
    return 16 * sum(d for _, d in ITEMS[b][:before(b, name) + 1])


def build(nc, A, O):
    with ExitStack() as ctx:
        def sb(name, shape, dt=F32):
            return ctx.enter_context(nc.sbuf_tensor(name, shape, dt))

        def sem(name):
            return ctx.enter_context(nc.semaphore(name))

        ring = sb("ring", [P, NSLOT, SLOT])
        xT = sb("xT", [P, DT, NT])
        hT = sb("hT", [P, DT, NT])
        sq = sb("sq", [P, DT, NT])
        pT = sb("pT", [P, NTILE, NT])
        vec = sb("vec", [P, NVEC])
        cT = sb("cT", [P, DT, NC])
        csig = sb("csig", [P, DT, NC])
        ada = sb("ada", [P, 6, DT, NC])
        ones = sb("ones", [P, P])
        ident = sb("ident", [P, P])
        swapm = sb("swapm", [P, ROPE])
        cosT = sb("cosT", [P, NT])
        sinT = sb("sinT", [P, NT])
        mask = sb("mask", [P, 3 * P])
        rstd = sb("rstd", [P, NT])
        krT = sb("krT", [P, 2, NT])
        bsp = sb("bsp", [P, CT, P])
        brou = sb("brou", [P, E])
        wrou = sb("wrou", [P, DT, E])
        gqp = sb("gqp", [P, 1])
        qT = sb("qT", [P, H, NT])
        kT = sb("kT", [P, H, NT])
        vtok = sb("vtok", [P, 2, CW])
        oaT = sb("oaT", [P, CT, NT])
        ptab = sb("ptab", [1, NS * NPG], I32)
        qlat = sb("qlat", [P, KT_, NS, H])
        qrp = sb("qrp", [P, NS, H])
        qsg = sb("qsg", [P, H, NS])
        sself = sb("sself", [P, NS, H])
        ksq = sb("ksq", [P, 2, H * NOPE])
        krss = sb("krss", [P, NPG])
        kss = sb("kss", [P, NPG, H])
        ssc = sb("ssc", [P, NPG, H])
        sp_ = sb("sp_", [P, 2, NPG, H])
        smx = sb("smx", [P, H])
        samx = sb("samx", [P, H])
        ssub = sb("ssub", [P, H])
        eself = sb("eself", [P, H])
        ssum = sb("ssum", [P, H])
        stot = sb("stot", [P, H])
        olat = sb("olat", [P, KT_, H, NS])
        olt = sb("olt", [P, KT_, H])
        abuf = sb("abuf", [P, 9 * P])
        krsq = abuf[:, 0:NPG * ROPE].rearrange("p (j d) -> p j d", j=NPG)
        am, aP, aPT = (abuf[:, j * 3 * P:(j + 1) * 3 * P] for j in range(3))
        amx = sb("amx", [P, 2])
        asum = sb("asum", [P, 2])
        arc = sb("arc", [P, 2])
        zp = sb("zp", [P, CT, 2 + NP_])
        zs = sb("zs", [P, CT, NS, 3])
        lg = sb("lg", [P, 3, E])
        ch = sb("ch", [P, 3, E])
        cm = sb("cm", [P, 3, E])
        top = sb("top", [P, 3, 8, 8])
        gsc = sb("gsc", [P, 3, 12])
        gtop = sb("gtop", [P, 3, 8])
        gms = sb("gms", [P, 3, 12])
        wsum = sb("wsum", [P, 3])
        gatesT = abuf[0:E, 0:NT]
        gsel = abuf[0:E, NT:3 * NT].rearrange("p (a t) -> p a t", a=2)
        kTf = kT[:].rearrange("p h t -> p (h t)")
        acts = kTf[:, 0:4 * NT].rearrange("p (a f t) -> p a f t", a=2, f=2)
        tri = sb("tri", [P, P])
        iota = sb("iota", [P, CAP])
        toki = sb("toki", [P, NT])
        posm = abuf[:, 3 * NT:3 * NT + 3 * E].rearrange("p (j e) -> p j e", j=3)
        pmax = sb("pmax", [P, 1])
        pall = sb("pall", [P, 1])
        flag = sb("flag", [P, 1], I32)
        idxf = sb("idxf", [P, 2])
        idx = sb("idx", [P, 2], mybir.dt.uint32)
        sqf = sq[:].rearrange("p h t -> p (h t)")
        xs = sqf[:, 0:2 * D].rearrange("p (a c) -> p a c", a=2)
        qTf = qT[:].rearrange("p h t -> p (h t)")
        xTs = qTf[:, 0:2 * D].rearrange("p (a k c) -> p a k c", a=2, k=DT)
        yrow = vtok[:].rearrange("p a c -> p (a c)")
        free_p = pT[:].rearrange("p t n -> p (t n)")[:, DT * NT:NTILE * NT]
        h2tok = free_p[:, 0:3 * D].rearrange("p (j c) -> p j c", j=3)
        gm = [free_p[:, 3 * D + a * NT:3 * D + (a + 1) * NT] for a in range(4)]
        oaf = oaT[:].rearrange("p k t -> p (k t)")
        silu_s, act_s = oaf[:, 0:FE], oaf[:, FE:2 * FE]
        actT = oaf[:, 2 * FE:3 * FE].rearrange("p (f c) -> p f c", f=FT)
        idw = oaf[:, 3 * FE:3 * FE + NT]
        gtm = ksq[:].rearrange("p a c -> p (a c)")[:, 0:3 * P].rearrange("p (j c) -> p j c", j=3)
        actg = kTf[:, 4 * NT:8 * NT].rearrange("p (a f t) -> p a f t", a=2, f=2)
        vn = kTf[:, 0:CT * NT].rearrange("p (k t) -> p k t", k=CT)
        vntok = kTf[:, CT * NT:CT * NT + 2 * CW].rearrange("p (b c) -> p b c", b=2)
        mg = qT
        yacc = pT[:, 0:DT, :]

        def part(b, at, *dims):
            n = int(np.prod(dims))
            ap = ring[:, b, at:at + n]
            if len(dims) == 2:
                return ap.rearrange("p (a b) -> p a b", a=dims[0])
            return ap.rearrange("p (a b c) -> p a b c", a=dims[0], b=dims[1])

        wuq = part(2, 0, QT, H * QK)
        wuk = part(2, QT * H * QK, KT_, H * NOPE)
        wuv = part(2, QT * H * QK + KT_ * H * NOPE, KT_, H * NOPE)
        wukT = part(3, 0, H, KL)[0:NOPE]
        wspT = part(3, H * KL, 8, P)
        pgR = [part(b, 0, NPG, KL + ROPE) for b in range(2)]
        pgT = [part(b, NPG * (KL + ROPE), NPG, 3, P) for b in range(2)]

        bk = [ctx.enter_context(nc.psum_tensor(f"bank{i}", [P, 512], F32)) for i in range(4)]
        pA = ctx.enter_context(nc.psum_tensor("pA", [P, 512], F32))
        pB = ctx.enter_context(nc.psum_tensor("pB", [P, 512], F32))
        pC = ctx.enter_context(nc.psum_tensor("pC", [P, 512], F32))
        pD = ctx.enter_context(nc.psum_tensor("pD", [P, 512], F32))

        full = [sem(f"bank_full{i}") for i in range(4)]
        free = [sem(f"bank_free{i}") for i in range(4)]
        wgt = [sem(f"slot_filled{i}") for i in range(NSLOT)]
        used = [sem(f"slot_used{i}") for i in range(NSLOT)]
        d_in = sem("small_inputs")
        d_late = sem("late_inputs")
        d_ptab = sem("page_table")
        d_out = sem("outputs")
        d_vout = sem("v_outputs")
        d_y = sem("y_output")
        c_dve = sem("vector_chain")
        c_act = sem("scalar_chain")
        s = {n: sem(n) for n in (
            "consts", "csig", "csilu", "ada_mm", "ada", "sq1", "var1", "rs1", "h1", "in_done", "gsig",
            "sqq", "varq", "rsq", "cqn", "sqkv", "varkv", "rskv", "ckv", "kvout", "krin", "krot",
            "qcopy", "qrot", "sqh", "varh", "rsh", "qn", "kcopy", "kfull", "kn", "vtok", "prodself", "sself",
            "qsg", "qlat", "s_mm", "ksq", "ksq_used", "kss", "rstds", "smx", "allmx", "ssub", "pexp", "psumd", "tot_mm",
            "pg_used", "pv", "olat", "oa_s",
            "amx", "aexp", "anorm", "aPT", "oa", "z", "conv", "vcen", "sqv", "varv", "rsv", "vn", "vntok", "sg", "wsp",
            "merged", "x1", "sq2", "var2", "rs2", "h2", "lsig", "gates", "gatesT", "gsel", "gbc", "gbc_used",
            "silu", "act", "act_used", "yout",
            "h2tok", "posm", "pmax", "pall", "flag", "gt", "idx", "gu", "silu_s", "act_s", "dn0", "dn1", "y0", "y1",
            "fgates", "turn")}
        d_tok = sem("h2_stored")
        d_x = [sem("tokens_gathered0"), sem("tokens_gathered1")]
        c_f = sem("vector_chain_dense")
        c_end = sem("vector_chain_end")
        h2rows = nc.dram_tensor("h2_rows", (NT, D), F32, kind="Internal").ap()

        def bank(n):
            return n % 4, n // 4

        block = ctx.enter_context(nc.Block())

        @block.sync
        def _(sp):
            sp.dma_start(cT[:], A["cT"]).then_inc(d_in, 16)
            sp.dma_start(vec[:], A["vec"]).then_inc(d_in, 16)
            sp.dma_start(xT[:], A["xT"]).then_inc(d_in, 16)
            sp.dma_start(ptab[:], A["ptab"]).then_inc(d_ptab, 16)

            def cols(w, c0, nc_):
                return w.rearrange("(k p) c -> p k c", p=P)[:, :, c0:c0 + nc_]

            def reuse(b, name):
                sp.wait_ge(used[b], before(b, name))

            ada_w = A["w_ada"].rearrange("(k p) (n c) -> n p k c", p=P, c=512)
            for b in range(4):
                sp.dma_start(part(b, 0, DT, 512), ada_w[b]).then_inc(wgt[b], 16)
            with sp.Fori(1, 3) as i:
                for b in range(4):
                    sp.wait_ge(used[b], i)
                    sp.dma_start(part(b, 0, DT, 512), ada_w[bass.ds(i * 4 + b, 1)].rearrange("o p k c -> (o p) k c")
                                 ).then_inc(wgt[b], 16)
            reuse(0, "in0")
            sp.dma_start(part(0, 0, DT, 672), cols(A["w_in"], 0, 672)).then_inc(wgt[0], 16)
            for j, (b, name) in enumerate(((1, "cb"), (2, "cc"), (3, "ch"), (0, "u"), (1, "v"))):
                reuse(b, name)
                sp.dma_start(part(b, 0, DT, 512), cols(A["w_in"], 672 + j * 512, 512)).then_inc(wgt[b], 16)
            reuse(2, "mla")
            sp.dma_start(wuq, A["w_uq"]).then_inc(wgt[2], 16)
            sp.dma_start(wuk, A["w_uk"]).then_inc(wgt[2], 16)
            sp.dma_start(wuv, A["w_uv"]).then_inc(wgt[2], 16)
            reuse(3, "late")
            sp.dma_start(wukT, A["w_ukT"]).then_inc(wgt[3], 16)
            sp.dma_start(wspT, A["wspT"]).then_inc(wgt[3], 16)
            sp.wait_ge(d_ptab, 16)
            with sp.Fori(0, NS // 2) as i:
                for b in range(2):
                    sp.wait_ge(used[b], i + before(b, "pages"))
                    for j in range(NPG):
                        pg = sp.value_load(ptab[0:1, bass.ds(i * (2 * NPG) + (b * NPG + j), 1)],
                                           min_val=0, max_val=NPOOL - 1)
                        sp.dma_start(pgR[b][:, j, :], A["poolR"][bass.ds(pg, 1)].rearrange("o r c -> (o r) c")
                                     ).then_inc(wgt[b], 16)
                        sp.dma_start(pgT[b][:, j], A["poolT"][bass.ds(pg, 1)].rearrange("o p k c -> (o p) k c")
                                     ).then_inc(wgt[b], 16)
            for hf in range(2):
                for b, x in enumerate("abc"):
                    reuse(b, f"g{x}{hf}")
                    sp.dma_start(part(b, 0, DT, 512), cols(A["w_in"], GATE0 + b * D + hf * 512, 512)).then_inc(wgt[b], 16)
                reuse(3, f"br{hf}")
                for b, x in enumerate("abc"):
                    sp.dma_start(part(3, b * CT * 512, CT, 512), A[f"w_br_{x}"].rearrange("(k p) c -> p k c", p=P)
                                 [:, :, hf * 512:(hf + 1) * 512]).then_inc(wgt[3], 16)
            for b in range(2):
                reuse(b, f"out{b}")
                sp.dma_start(part(b, 0, DT, 512), cols(A["w_out"], b * 512, 512)).then_inc(wgt[b], 16)

            def expert(b, g, u, d):
                gu = part(b, 0, DT, 2 * FE)
                sp.dma_start(gu[:, :, 0:FE], g.rearrange("(k p) c -> p k c", p=P)).then_inc(wgt[b], 16)
                sp.dma_start(gu[:, :, FE:2 * FE], u.rearrange("(k p) c -> p k c", p=P)).then_inc(wgt[b], 16)
                sp.dma_start(part(b, 2 * DT * FE, FT, D), d.rearrange("(k p) c -> p k c", p=P)).then_inc(wgt[b], 16)

            reuse(2, "shared")
            expert(2, A["w_sh_gate"], A["w_sh_up"], A["w_sh_down"])

            def one(w, e):
                return A[w][bass.ds(e, 1)].rearrange("o r c -> (o r) c")

            with sp.Fori(0, E // 4) as i:
                for b in range(4):
                    sp.wait_ge(used[b], i + before(b, "exp"))
                    expert(b, *(one(w, i * 4 + b) for w in ("w_e_gate", "w_e_up", "w_e_down")))
            sp.wait_ge(s["flag"], 1)
            with sp.If(sp.value_load(flag[0:1, 0:1], min_val=0, max_val=1) >= 1):
                with sp.Fori(0, E // 4) as i:
                    for b in range(4):
                        sp.wait_ge(used[b], i + (before(b, "exp") + E // 4))
                        expert(b, *(one(w, i * 4 + b) for w in ("w_e_gate", "w_e_up", "w_e_down")))
            sp.wait_ge(s["yout"], 1)
            sp.dma_start(O["yT"], hT[:]).then_inc(d_y, 16)
            sp.wait_ge(d_y, 16)
            sp.wait_ge(d_out, 16 * 4)
            sp.wait_ge(d_vout, 16 * 2)

        @block.gpsimd
        def _(pool):
            nc.gpsimd.memset(ones[:], 1.0).then_inc(s["consts"], 1)
            nc.gpsimd.memset(qrp[:], 0.0).then_inc(s["consts"], 1)
            nc.gpsimd.memset(zp[:, :, 0:2], 0.0).then_inc(s["consts"], 1)
            for t, n in ((ident, "ident"), (swapm, "swapm"), (cosT, "cosT"), (sinT, "sinT"), (mask, "mask"),
                         (bsp, "bsp"),
                         (brou, "brou"), (wrou, "w_router"), (tri, "tri"), (iota, "iota"), (toki, "toki")):
                pool.dma_start(t[:], A[n]).then_inc(d_late, 16)
            pool.dma_start(zs[:, :, :, 0:2], A["stateT"]).then_inc(d_late, 16)
            pool.wait_ge(d_late, 16 * 12)
            pool.wait_ge(wgt[3], arrival(3, "late"))
            nc.gpsimd.affine_select(out=wspT, in_=wspT, compare_op=ALU.is_ge, fill=0.0, base=0,
                                    pattern=[[0, 8], [1, P]], channel_multiplier=-1).then_inc(s["wsp"], 1)
            pool.wait_ge(s["ckv"], 1)
            pool.dma_start(O["ckvT"], pT[:, T_KV:T_KV + KT_, :]).then_inc(d_out, 16)
            pool.wait_ge(s["krot"], 1)
            pool.dma_start(O["krT"], krT[NOPE:QK, 1, :]).then_inc(d_out, 16)
            for q in range(NS):
                pool.wait_ge(s["smx"], q + 1)
                nc.gpsimd.partition_all_reduce(samx[:], smx[:], P, RMAX).then_inc(s["allmx"], 1)
            pool.wait_ge(s["z"], 1)
            pool.dma_start(O["convP"], zp[:, :, NP_:NP_ + 2]).then_inc(d_out, 16)
            pool.dma_start(O["convS"], zs[:, :, :, 1:3]).then_inc(d_out, 16)
            pool.wait_ge(s["vn"], 1)
            pool.dma_start(O["vnP"], vn[:, :, P:NP_]).then_inc(d_vout, 16)
            pool.dma_start(O["vnS"], vn[:, :, NP_:NT]).then_inc(d_vout, 16)
            pool.wait_ge(s["h2tok"], 6)
            for j, m in enumerate((P, P, NS)):
                pool.dma_start(h2rows[j * P:j * P + m, :], h2tok[0:m, j, :]).then_inc(d_tok, 16)
            pool.wait_ge(s["pmax"], 1)
            nc.gpsimd.partition_all_reduce(pall[:], pmax[:], P, RMAX).then_inc(s["pall"], 1)
            pool.wait_ge(d_tok, 16 * 3)

            def gather(q, i):
                pool.wait_ge(s["idx"], turn(i, q + 1, 1))
                if q >= 2:
                    n = USE["X", q - 2, 1]
                    pool.wait_ge(full[n % 4], turn(i, n // 4 + 1, 3))
                pool.sem_inc(s["turn"], 1)
                nc.gpsimd.indirect_dma_start(
                    out=xs[:, q % 2, :], out_offset=None, in_=h2rows,
                    in_offset=bass.IndirectOffsetOnAxis(ap=idx[:, q % 2:q % 2 + 1], axis=0)).then_inc(d_x[q % 2], 16)

            for q in range(3):
                gather(q, None)
            with pool.Fori(0, 7) as i:
                for b in range(4):
                    gather(3 + b, i)
            gather(NPAIR - 1, None)

        @block.tensor
        def _(pe):
            def enter(n, i=None, per=0):
                b, k = bank(n)
                if i is not None:
                    pe.wait_ge(free[b], i * (per // 4) + k)
                elif k:
                    pe.wait_ge(free[b], k)
                return bk[b]

            def through(n, b):
                pe.wait_ge(full[n % 4], n // 4 + 1)
                pe.sem_inc(used[b], 1)

            def mm(out, lhsT, rhs, start, stop):
                return nc.tensor.matmul(out, lhsT, rhs, start=start, stop=stop)

            def sumsq(stage, src, nt, kp=P):
                n = BASE[stage]
                t = enter(n)
                for k in range(nt):
                    last = mm(t[:, 0:NT], ones[0:kp, :], src[0:kp, k, :], k == 0, k == nt - 1)
                last.then_inc(full[n % 4], 1)

            pe.wait_ge(s["csilu"], 1)
            with pe.Fori(0, 3) as i:
                for b in range(4):
                    pe.wait_ge(wgt[b], i * 16 + 16)
                    w = ring[:, b, 0:DT * 512].rearrange("p (k c) -> p k c", k=DT)
                    for m in range(4):
                        for k in range(DT):
                            last = mm(pA[:, bass.ds(i * (16 * NC) + (4 * b + m) * NC, NC)],
                                      w[:, k, m * P:(m + 1) * P], csig[:, k, :], k == 0, k == DT - 1)
                    last.then_inc(used[b], 1)
            pe.wait_ge(s["consts"], 3)
            pe.wait_ge(s["sq1"], 1)
            sumsq("norm1", sq, DT)

            pe.wait_ge(s["h1"], 2)
            pe.wait_ge(wgt[0], arrival(0, "in0"))
            w = part(0, 0, DT, 672)
            for m in range(6):
                n = BASE["in0"] + m
                t = enter(n)
                for k in range(DT):
                    if m < 5:
                        last = mm(t[:, 0:NT], w[:, k, m * P:(m + 1) * P], hT[:, k, :], k == 0, k == DT - 1)
                    else:
                        last = mm(t[NOPE:QK, 0:NT], w[:, k, 640:672], hT[:, k, :], k == 0, k == DT - 1)
                last.then_inc(full[n % 4], 1)
            through(n, 0)
            for c, (b, name) in enumerate(((1, "cb"), (2, "cc"), (3, "ch"), (0, "u"), (1, "v"))):
                pe.wait_ge(wgt[b], arrival(b, name))
                w = part(b, 0, DT, 512)
                for m in range(4):
                    n = BASE["in1"] + 4 * c + m
                    t = enter(n)
                    for k in range(DT):
                        last = mm(t[:, 0:NT], w[:, k, m * P:(m + 1) * P], hT[:, k, :], k == 0, k == DT - 1)
                    last.then_inc(full[n % 4], 1)
                through(n, b)

            pe.wait_ge(s["sqq"], 1)
            sumsq("cqn", sq, QT)
            sumsq("kvn", sq[:, QT:QT + KT_, :], KT_)
            pe.wait_ge(d_late, 16 * 12)
            n = BASE["krs"]
            t = enter(n)
            mm(t[NOPE:QK, 0:NT], swapm[NOPE:QK, :], krT[NOPE:QK, 0, :], True, True).then_inc(full[n % 4], 1)
            pe.wait_ge(s["cqn"], 1)
            pe.wait_ge(wgt[2], arrival(2, "mla"))
            for h in range(H):
                n = BASE["q"] + h
                t = enter(n)
                for k in range(QT):
                    last = mm(t[0:QK, 0:NT], wuq[:, k, h * QK:(h + 1) * QK], pT[:, T_Q + k, :], k == 0, k == QT - 1)
                last.then_inc(full[n % 4], 1)
            for h in range(H):
                n = BASE["qswap"] + h
                t = enter(n)
                pe.wait_ge(s["qcopy"], h + 1)
                mm(t[NOPE:QK, 0:NT], swapm[NOPE:QK, :], qT[NOPE:QK, h, :], True, True).then_inc(full[n % 4], 1)
            pe.wait_ge(s["sqh"], 1)
            for h in range(H):
                n = BASE["qss"] + h
                t = enter(n)
                mm(t[:, 0:NT], ones[0:QK, :], sq[0:QK, h, :], True, True).then_inc(full[n % 4], 1)
            pe.wait_ge(s["ckv"], 1)
            for h in range(H):
                n = BASE["k"] + h
                t = enter(n)
                for k in range(KT_):
                    last = mm(t[0:NOPE, 0:NT], wuk[:, k, h * NOPE:(h + 1) * NOPE], pT[:, T_KV + k, :],
                              k == 0, k == KT_ - 1)
                last.then_inc(full[n % 4], 1)
            pe.wait_ge(s["sqh"], 2)
            for h in range(H):
                n = BASE["kss"] + h
                t = enter(n)
                mm(t[:, 0:NT], ones[0:QK, :], sq[0:QK, h, :], True, True).then_inc(full[n % 4], 1)
            for b in range(2):
                n = BASE["v"] + b
                t = enter(n)
                for k in range(KT_):
                    last = mm(t[:], pT[:, T_KV + k, b * P:(b + 1) * P], wuv[:, k, :], k == 0, k == KT_ - 1)
                last.then_inc(full[n % 4], 1)
            pe.wait_ge(s["prodself"], 1)
            n = BASE["self"]
            t = enter(n)
            mm(t[:, 0:H * NS], ones[0:QK, :], sq[0:QK, 0, 0:H * NS], True, True).then_inc(full[n % 4], 1)
            pe.wait_ge(s["qsg"], 1)
            pe.wait_ge(wgt[3], arrival(3, "late"))
            n = BASE["qlat"]
            t = enter(n)
            for k in range(KT_):
                for h in range(H):
                    last = mm(t[:, (k * H + h) * NS:(k * H + h + 1) * NS], wukT[:, h, k * P:(k + 1) * P],
                              qsg[0:NOPE, h, :], True, True)
            last.then_inc(full[n % 4], 1)
            for n in range(BASE["s_pad"], BASE["s_pad"] + 2):
                enter(n)
                mm(bk[n % 4][:, 0:NC], ones[:], csig[:, 0, :], True, True).then_inc(full[n % 4], 1)

            pe.wait_ge(s["qlat"], 2)
            sco = [pA, pB]
            olp = [pC, pD]

            def keys(q, b, i, first):
                pe.wait_ge(wgt[b], (q - b) * (16 * NPG) + arrival(b, "pages"))
                if not first:
                    pe.wait_ge(s["smx"], q - 1)
                for j in range(NPG):
                    n = BASE["know"] + NPG * b + j
                    k_ = bank(n)
                    pe.wait_ge(free[k_[0]], (q - b) * 2 + k_[1])
                    for k in range(KT_):
                        last = mm(bk[k_[0]][:], pgT[b][:, j, k, :], wuk[:, k, :], k == 0, k == KT_ - 1)
                    last.then_inc(full[k_[0]], 1)
                    for k in range(KT_):
                        mm(sco[b][:, j * H:(j + 1) * H], pgT[b][:, j, k, :],
                           qlat[:, k, bass.ds(q, 1), :].rearrange("p o h -> p (o h)"), k == 0, False)
                    last = mm(sco[b][:, j * H:(j + 1) * H], pgT[b][:, j, 2, :],
                              qrp[:, bass.ds(q, 1), :].rearrange("p o h -> p (o h)"), False, True)
                last.then_inc(s["s_mm"], 1)

            def values(q, b, first):
                pe.wait_ge(s["psumd"], q + 1)
                if not first:
                    pe.wait_ge(s["olat"], q - 1)
                mm(olp[b][:, 64:64 + H], ones[:], ssum[:], True, True)
                for k in range(KT_):
                    for j in range(NPG):
                        last = mm(olp[b][:, k * H:(k + 1) * H], pgR[b][:, j, k * P:(k + 1) * P], sp_[:, b, j, :],
                                  j == 0, j == NPG - 1)
                last.then_inc(s["pv"], 1)
                pe.wait_ge(s["pv"], q + 1)
                pe.sem_inc(used[b], 1)

            for q in range(NS):
                keys(q, q % 2, None, q < 2)
                if q:
                    values(q - 1, 1 - q % 2, q - 1 < 2)
            values(NS - 1, 1, False)

            pe.wait_ge(s["olat"], NS)
            for c in range(CT):
                n = BASE["uvs"] + c
                t = enter(n)
                for o in range(2):
                    h = 2 * c + o
                    for k in range(KT_):
                        last = mm(t[o * 64:(o + 1) * 64, 0:NS], wuv[:, k, h * NOPE:(h + 1) * NOPE], olat[:, k, h, :],
                                  k == 0, k == KT_ - 1)
                last.then_inc(full[n % 4], 1)

            def a_scores(h):
                n = BASE["att"] + 3 * h
                t = enter(n)
                mm(t[:, 0:P], qT[0:QK, h, 0:P], kT[0:QK, h, 0:P], True, True)
                mm(t[:, P:3 * P], qT[0:QK, h, P:NP_], kT[0:QK, h, 0:NP_], True, True).then_inc(full[n % 4], 1)

            def a_out(h):
                n = BASE["att"] + 3 * h + 1
                t = enter(n)
                pe.wait_ge(s["anorm"], h + 1)
                for j in range(3):
                    last = nc.tensor.transpose(t[:, j * P:(j + 1) * P], aP[:, j * P:(j + 1) * P], ident[:])
                last.then_inc(full[n % 4], 1)
                n = BASE["att"] + 3 * h + 2
                t = enter(n)
                o = 64 * (h % 2)
                pe.wait_ge(s["aPT"], h + 1)
                v = vtok[:, :, h * NOPE:(h + 1) * NOPE]
                mm(t[o:o + 64, 0:P], v[:, 0, :], aPT[:, 0:P], True, True)
                mm(t[o:o + 64, P:NP_], v[:, 0, :], aPT[:, P:2 * P], True, False)
                mm(t[o:o + 64, P:NP_], v[:, 1, :], aPT[:, 2 * P:3 * P], False, True).then_inc(full[n % 4], 1)

            pe.wait_ge(full[n % 4], n // 4 + 1)
            pe.sem_inc(used[2], 1)
            pe.wait_ge(s["kn"], 1)
            pe.wait_ge(s["vtok"], 2)
            for h in range(H):
                a_scores(h)
                a_out(h)

            n = BASE["vmean"]
            t = enter(n)
            for k in range(CT):
                last = mm(t[:, 0:NT], ones[:], pT[:, T_V + k, :], k == 0, k == CT - 1)
            last.then_inc(full[n % 4], 1)
            pe.wait_ge(s["sqv"], 1)
            sumsq("vvar", sq, CT)
            pe.wait_ge(s["vn"], 1)
            for b in range(2):
                n = BASE["vtr"] + b
                t = enter(n)
                for k in range(CT):
                    last = nc.tensor.transpose(t[:, k * P:(k + 1) * P], vn[:, k, b * P:(b + 1) * P], ident[:])
                last.then_inc(full[n % 4], 1)
            pe.wait_ge(s["wsp"], 1)
            pe.wait_ge(s["vntok"], 2)
            for c in range(CT):
                n = BASE["spat"] + c
                t = enter(n)
                for o in range(2):
                    for b in range(2):
                        g = 2 * c + o
                        last = mm(t[64 * o:64 * o + 64, b * P:(b + 1) * P], vntok[:, b, g * 64:(g + 1) * 64],
                                  wspT[:, g, :], True, True)
                last.then_inc(full[n % 4], 1)

            through(n, 3)

            pe.wait_ge(s["oa"], H)
            pe.wait_ge(s["oa_s"], CT)
            pe.wait_ge(s["conv"], 1)
            pe.wait_ge(s["sg"], 1)
            src = [oaT[:, :, :], pT[:, T_CB:T_CB + CT, :], pT[:, T_U:T_U + CT, :]]
            for hf in range(2):
                for b, x in enumerate("abc"):
                    pe.wait_ge(wgt[b], arrival(b, f"g{x}{hf}"))
                pe.wait_ge(wgt[3], arrival(3, f"br{hf}"))
                for m in range(4):
                    for b in range(3):
                        n = BASE["br"] + 6 * (4 * hf + m) + b
                        t = enter(n)
                        for k in range(DT):
                            last = mm(t[:, 0:NT], part(b, 0, DT, 512)[:, k, m * P:(m + 1) * P], hT[:, k, :],
                                      k == 0, k == DT - 1)
                        last.then_inc(full[n % 4], 1)
                    for b in range(3):
                        n = BASE["br"] + 6 * (4 * hf + m) + 3 + b
                        t = enter(n)
                        for k in range(CT):
                            last = mm(t[:, 0:NT], part(3, b * CT * 512, CT, 512)[:, k, m * P:(m + 1) * P],
                                      src[b][:, k, :], k == 0, k == CT - 1)
                        last.then_inc(full[n % 4], 1)
                for b in range(4):
                    through(n, b)
            pe.wait_ge(s["merged"], DT)
            for m in range(DT):
                b = m // 4
                if m % 4 == 0:
                    pe.wait_ge(wgt[b], arrival(b, f"out{b}"))
                n = BASE["out"] + m
                t = enter(n)
                for k in range(DT):
                    last = mm(t[:, 0:NT], part(b, 0, DT, 512)[:, k, (m % 4) * P:(m % 4 + 1) * P], mg[:, k, :],
                              k == 0, k == DT - 1)
                last.then_inc(full[n % 4], 1)
                if m % 4 == 3:
                    through(n, b)
            pe.wait_ge(s["sq2"], 1)
            sumsq("norm2", sq, DT)
            pe.wait_ge(s["h2"], 2)
            for j, m in enumerate((P, P, NS)):
                n = BASE["rout"] + j
                t = enter(n)
                for k in range(DT):
                    last = mm(t[0:m, 0:E], hT[:, k, j * P:j * P + m], wrou[:, k, :], k == 0, k == DT - 1)
                last.then_inc(full[n % 4], 1)
            for j, m in enumerate((P, P, NS)):
                for hf in range(2):
                    n = BASE["h2tr"] + 2 * j + hf
                    t = enter(n)
                    for k in range(4):
                        last = nc.tensor.transpose(t[0:m, k * P:(k + 1) * P], hT[:, 4 * hf + k, j * P:j * P + m], ident[:])
                    last.then_inc(full[n % 4], 1)

            def dense_up(b, n0, i):
                w = part(b, 0, DT, 2 * FE)
                for f in range(FT):
                    for u in range(2):
                        n = n0 + 2 * f + u
                        t = enter(n, i, 48)
                        for k in range(DT):
                            c0 = u * FE + f * P
                            last = mm(t[:, 0:NT], w[:, k, c0:c0 + P], hT[:, k, :], k == 0, k == DT - 1)
                        last.then_inc(full[n % 4], 1)

            def dense_down(b, n0, i, par):
                w = part(b, 2 * DT * FE, FT, D)
                for m in range(DT):
                    n = n0 + m
                    t = enter(n, i, 48)
                    for f in range(FT):
                        last = mm(t[:, 0:NT], w[:, f, m * P:(m + 1) * P], actg[:, par, f, :], f == 0, f == FT - 1)
                    last.then_inc(full[n % 4], 1)
                if i is None:
                    pe.wait_ge(full[n % 4], n // 4 + 1)
                else:
                    pe.wait_ge(full[n % 4], i * 12 + (n // 4 + 1))
                pe.sem_inc(used[b], 1)

            pe.wait_ge(wgt[2], arrival(2, "shared"))
            dense_up(2, BASE["shgu"], None)
            pe.wait_ge(s["gates"], 1)
            n = BASE["pos"]
            t = enter(n)
            for j, m in enumerate((P, P, NS)):
                for i in range(j + 1):
                    kk = (P, P, NS)[i]
                    last = mm(t[0:m, j * E:(j + 1) * E], (ones if i < j else tri)[0:kk, 0:m], ch[0:kk, i, :],
                              i == 0, i == j)
            last.then_inc(full[n % 4], 1)
            pe.wait_ge(s["act"], 2)
            dense_down(2, BASE["shdn"], None, 1)
            for n in range(BASE["pad"], BASE["pad"] + 1):
                enter(n)
                mm(bk[n % 4][:, 0:NC], ones[:], csig[:, 0, :], True, True).then_inc(full[n % 4], 1)

            def use(n, i):
                pe.wait_ge(free[n % 4], turn(i, n // 4, 3))
                return bk[n % 4]

            def emptied(n, i):
                pe.wait_ge(free[n % 4], turn(i, n // 4 + 1, 3))

            def gates_tr(q, i):
                n = USE["G", q]
                t = use(n, i)
                pe.wait_ge(s["gt"], turn(i, q + 1, 1))
                for j, m in enumerate((P, P, NS)):
                    last = nc.tensor.transpose(t[:, j * P:j * P + m], gtm[0:m, j, :], ident[0:m, 0:m])
                last.then_inc(full[n % 4], 1)

            def tokens_tr(q, i):
                pe.wait_ge(d_x[q % 2], turn(i, 16 * (q // 2 + 1), 8))
                for hf in range(2):
                    n = USE["X", q, hf]
                    t = use(n, i)
                    for k in range(4):
                        c0 = (4 * hf + k) * P
                        last = nc.tensor.transpose(t[:, k * P:(k + 1) * P], xs[:, q % 2, c0:c0 + P], ident[:])
                    last.then_inc(full[n % 4], 1)

            def up(p, i):
                for hf in range(2):
                    emptied(USE["X", p, hf], i)
                sl = [2 * (p % 2) + x for x in range(2)]
                for b in sl:
                    pe.wait_ge(wgt[b], turn(i, arrival(b, "exp") + 48 * (p // 2), 24))
                for k in range(DT):
                    for x in range(2):
                        last = mm(pA[CAP * x:CAP * (x + 1), :], xTs[:, p % 2, k, CAP * x:CAP * (x + 1)],
                                  part(sl[x], 0, DT, 2 * FE)[:, k, :], k == 0, k == DT - 1)
                last.then_inc(s["gu"], 1)

            def act_tr(p, i):
                n = USE["T", p]
                t = use(n, i)
                pe.wait_ge(s["act_s"], turn(i, p + 1, 1))
                for f in range(FT):
                    last = nc.tensor.transpose(t[:, f * P:(f + 1) * P], act_s[:, f * P:(f + 1) * P], ident[:])
                last.then_inc(full[n % 4], 1)

            def down(p, i):
                emptied(USE["T", p], i)
                sl = [2 * (p % 2) + x for x in range(2)]
                for hf in range(2):
                    for f in range(FT):
                        for x in range(2):
                            last = mm([pB, pC][hf][CAP * x:CAP * (x + 1), :], actT[:, f, CAP * x:CAP * (x + 1)],
                                      part(sl[x], 2 * DT * FE, FT, D)[:, f, hf * 512:(hf + 1) * 512],
                                      f == 0, f == FT - 1)
                    last.then_inc(s[f"dn{hf}"], 1)
                pe.wait_ge(s["dn1"], turn(i, p + 1, 1))
                for b in sl:
                    pe.sem_inc(used[b], 1)

            def spread(q, i, ms):
                if ms[0] == 0:
                    emptied(USE["G", q], i)
                    pe.wait_ge(s["y0"], turn(i, q + 1, 1))
                    pe.wait_ge(s["y1"], turn(i, q + 1, 1))
                for m in ms:
                    n = USE["C", q, m]
                    t = use(n, i)
                    mm(t[:, 0:NT], yrow[:, m * P:(m + 1) * P], gm[q % 4], True, True).then_inc(full[n % 4], 1)

            def pair(p, i=None):
                if p + 2 < NPAIR:
                    gates_tr(p + 2, i)
                if p + 1 < NPAIR:
                    tokens_tr(p + 1, i)
                up(p, i)
                if p:
                    spread(p - 1, i, range(4))
                act_tr(p, i)
                if p:
                    spread(p - 1, i, range(4, 8))
                down(p, i)

            gates_tr(0, None)
            gates_tr(1, None)
            tokens_tr(0, None)
            pair(0)
            with pe.Fori(0, 7) as i:
                for b in range(4):
                    pair(1 + b, i)
            for p in range(29, NPAIR):
                pair(p)
            spread(NPAIR - 1, None, range(8))

            pe.wait_ge(s["flag"], 1)
            with pe.If(pe.value_load(flag[0:1, 0:1], min_val=0, max_val=1) >= 1):
                pe.wait_ge(s["fgates"], 1)
                n = BASE["fgates"]
                t = enter(n)
                for j, m in enumerate((P, P, NS)):
                    last = nc.tensor.transpose(t[0:E, j * P:j * P + m], ch[0:m, j, :], ident[0:m, 0:m])
                last.then_inc(full[n % 4], 1)
                for n in range(BASE["fgates"] + 1, BASE["fexp"]):
                    enter(n)
                    mm(bk[n % 4][:, 0:NC], ones[:], csig[:, 0, :], True, True).then_inc(full[n % 4], 1)
                with pe.Fori(0, E // 4) as i:
                    for b in range(4):
                        par = b % 2
                        n0 = BASE["fexp"] + 12 * b
                        pe.wait_ge(wgt[b], i * 48 + (arrival(b, "exp") + 48 * (E // 4)))
                        dense_up(b, n0, i)
                        pe.wait_ge(s["gsel"], i * 4 + (b + 1))
                        mm([pC, pD][par][:, 0:NT], ones[0:E, :], gsel[:, par, :], True, True).then_inc(s["gbc"], 1)
                        pe.wait_ge(s["act"], i * 8 + (2 * b + 4))
                        dense_down(b, n0 + 4, i, par)

        @block.scalar
        def _(act):
            chain = [0]

            def link(ins):
                chain[0] += 1
                ins.then_inc(c_act, 1)
                act.wait_ge(c_act, chain[0])

            def fulls(n):
                b, k = bank(n)
                act.wait_ge(full[b], k + 1)
                return bk[b]

            act.wait_ge(d_in, 16 * 3)
            nc.scalar.activation(csig[:], cT[:], ACT.Sigmoid).then_inc(s["csig"], 1)
            nc.scalar.activation(sq[:], xT[:], ACT.Square).then_inc(s["sq1"], 1)
            act.wait_ge(s["var1"], 1)
            nc.scalar.activation(rstd[:], rstd[:], ACT.Sqrt).then_inc(s["rs1"], 1)
            for m in range(5):
                n = BASE["in0"] + m
                t = fulls(n)
                nc.scalar.activation(pT[:, m, :], t[:, 0:NT], ACT.Copy).then_inc(free[n % 4], 1)
            n = BASE["in0"] + 5
            t = fulls(n)
            nc.scalar.activation(krT[NOPE:QK, 0, :], t[NOPE:QK, 0:NT], ACT.Copy).then_inc(free[n % 4], 1)
            for b in range(4):
                act.wait_ge(free[b], (BASE["in0"] + 5 - b) // 4 + 1)
            act.sem_inc(s["krin"], 1)
            act.wait_ge(s["var1"], 1)
            nc.scalar.activation(sq[:, 0:QT + KT_, :], pT[:, T_Q:T_Q + QT + KT_, :], ACT.Square).then_inc(s["sqq"], 1)
            for j in range(20):
                n = BASE["in1"] + j
                t = fulls(n)
                nc.scalar.activation(pT[:, T_CB + j, :], t[:, 0:NT], ACT.Copy).then_inc(free[n % 4], 1)
            for b in range(4):
                act.wait_ge(free[b], (n - b) // 4 + 1)
            act.sem_inc(s["in_done"], 1)
            act.wait_ge(s["varq"], 1)
            link(nc.scalar.activation(rstd[:], rstd[:], ACT.Sqrt))
            act.sem_inc(s["rsq"], 1)
            act.wait_ge(s["varkv"], 1)
            nc.scalar.activation(rstd[:], rstd[:], ACT.Sqrt).then_inc(s["rskv"], 1)
            for h in range(H):
                n = BASE["q"] + h
                t = fulls(n)
                nc.scalar.activation(qT[0:QK, h, :], t[0:QK, 0:NT], ACT.Copy).then_inc(s["qcopy"], 1)
                act.wait_ge(s["qcopy"], h + 1)
                act.sem_inc(free[n % 4], 1)
            act.wait_ge(s["qrot"], 1)
            nc.scalar.activation(sq[0:QK, :, :], qT[0:QK, :, :], ACT.Square).then_inc(s["sqh"], 1)
            act.wait_ge(s["varh"], 1)
            big = pT[0:QK, T_CC:T_CC + H, :]
            nc.scalar.activation(big, big, ACT.Sqrt).then_inc(s["rsh"], 1)
            for h in range(H):
                n = BASE["k"] + h
                t = fulls(n)
                nc.scalar.activation(kT[0:NOPE, h, :], t[0:NOPE, 0:NT], ACT.Copy).then_inc(free[n % 4], 1)
            for b in range(4):
                act.wait_ge(free[b], (n - b) // 4 + 1)
            act.wait_ge(s["kfull"], 1)
            nc.scalar.activation(sq[0:QK, :, :], kT[0:QK, :, :], ACT.Square).then_inc(s["sqh"], 1)
            act.wait_ge(s["varh"], 2)
            nc.scalar.activation(big, big, ACT.Sqrt).then_inc(s["rsh"], 1)
            for b in range(2):
                n = BASE["v"] + b
                t = fulls(n)
                nc.scalar.activation(vtok[:, b, :], t[:], ACT.Copy).then_inc(s["vtok"], 1)
                act.wait_ge(s["vtok"], b + 1)
                act.sem_inc(free[n % 4], 1)
            for n in range(BASE["s_pad"], BASE["s_pad"] + 2):
                act.wait_ge(full[n % 4], n // 4 + 1)
                act.sem_inc(free[n % 4], 1)

            def squares(q):
                for j in range(NPG):
                    n = BASE["know"] + NPG * q + j
                    t = fulls(n)
                    if NPG * q + j >= 2:
                        act.wait_ge(s["ksq_used"], NPG * q + j - 1)
                    nc.scalar.activation(ksq[:, j % 2, :], t[:], ACT.Square).then_inc(s["ksq"], 1)
                    act.wait_ge(s["ksq"], NPG * q + j + 1)
                    act.sem_inc(free[n % 4], 1)

            def softmax(q):
                act.wait_ge(s["kss"], q + 1)
                nc.scalar.activation(kss[:], kss[:], ACT.Sqrt).then_inc(s["rstds"], 1)
                act.wait_ge(s["ssub"], q + 1)
                nc.scalar.activation(eself[:], ssub[:], ACT.Exp)
                if q >= 2:
                    act.wait_ge(s["pv"], q - 1)
                nc.scalar.activation(sp_[:, q % 2, :, :], ssc[:], ACT.Exp).then_inc(s["pexp"], 1)

            for q in range(NS):
                squares(q)
                softmax(q)
            for c in range(CT):
                n = BASE["uvs"] + c
                t = fulls(n)
                nc.scalar.activation(oaT[:, c, NP_:NT], t[:, 0:NS], ACT.Copy).then_inc(s["oa_s"], 1)
                act.wait_ge(s["oa_s"], c + 1)
                act.sem_inc(free[n % 4], 1)
            for h in range(H):
                act.wait_ge(s["amx"], h + 1)
                nc.scalar.activation(aP[:, 0:P], am[:, 0:P], ACT.Exp, bias=amx[:, 0:1], accum_out=asum[:, 0:1])
                nc.scalar.activation(aP[:, P:3 * P], am[:, P:3 * P], ACT.Exp, bias=amx[:, 1:2],
                                     accum_out=asum[:, 1:2]).then_inc(s["aexp"], 1)
                n = BASE["att"] + 3 * h + 1
                t = fulls(n)
                nc.scalar.activation(aPT, t[:, 0:3 * P], ACT.Copy).then_inc(s["aPT"], 1)
                act.wait_ge(s["aPT"], h + 1)
                act.sem_inc(free[n % 4], 1)
                n = BASE["att"] + 3 * h + 2
                t = fulls(n)
                o = 64 * (h % 2)
                nc.scalar.activation(oaT[o:o + 64, h // 2, 0:NP_], t[o:o + 64, 0:NP_], ACT.Copy).then_inc(s["oa"], 1)
                act.wait_ge(s["oa"], h + 1)
                act.sem_inc(free[n % 4], 1)
            act.wait_ge(s["vcen"], 1)
            nc.scalar.activation(sq[:, 0:CT, :], vn[:], ACT.Square).then_inc(s["sqv"], 1)
            act.wait_ge(s["varv"], 1)
            nc.scalar.activation(rstd[:], rstd[:], ACT.Sqrt).then_inc(s["rsv"], 1)
            for b in range(2):
                n = BASE["vtr"] + b
                t = fulls(n)
                nc.scalar.activation(vntok[:, b, :], t[:], ACT.Copy).then_inc(s["vntok"], 1)
                act.wait_ge(s["vntok"], b + 1)
                act.sem_inc(free[n % 4], 1)
            for m in range(DT):
                for b in range(3):
                    n = BASE["br"] + 6 * m + b
                    t = fulls(n)
                    if m >= 2:
                        act.wait_ge(s["merged"], m - 1)
                    nc.scalar.activation(sq[:, 3 * (m % 2) + b, :], t[:, 0:NT], ACT.Sigmoid).then_inc(s["gsig"], 1)
                    act.wait_ge(s["gsig"], 3 * m + b + 1)
                    act.sem_inc(free[n % 4], 1)
            act.wait_ge(s["x1"], 1)
            nc.scalar.activation(sq[:], xT[:], ACT.Square).then_inc(s["sq2"], 1)
            act.wait_ge(s["var2"], 1)
            nc.scalar.activation(rstd[:], rstd[:], ACT.Sqrt).then_inc(s["rs2"], 1)
            for j, m in enumerate((P, P, NS)):
                n = BASE["rout"] + j
                t = fulls(n)
                nc.scalar.activation(lg[0:m, j, :], t[0:m, 0:E], ACT.Sigmoid).then_inc(s["lsig"], 1)
                act.wait_ge(s["lsig"], j + 1)
                act.sem_inc(free[n % 4], 1)
            for j, m in enumerate((P, P, NS)):
                for hf in range(2):
                    n = BASE["h2tr"] + 2 * j + hf
                    t = fulls(n)
                    nc.scalar.activation(h2tok[0:m, j, hf * 512:(hf + 1) * 512], t[0:m, :], ACT.Copy
                                         ).then_inc(s["h2tok"], 1)
                    act.wait_ge(s["h2tok"], 2 * j + hf + 1)
                    act.sem_inc(free[n % 4], 1)

            def silu(n0, par, i, done):
                for f in range(FT):
                    n = n0 + 2 * f
                    b, k = bank(n)
                    if i is None:
                        act.wait_ge(full[b], k + 1)
                    else:
                        act.wait_ge(full[b], i * 12 + (k + 1))
                        act.wait_ge(s["act"], done - 1)
                    nc.scalar.activation(acts[:, par, f, :], bk[b][:, 0:NT], ACT.Silu).then_inc(s["silu"], 1)
                    act.wait_ge(s["silu"], done + (f + 1))
                    act.sem_inc(free[b], 1)

            act.wait_ge(d_vout, 16 * 2)
            silu(BASE["shgu"], 1, None, 0)
            for n in range(BASE["pad"], BASE["pad"] + 1):
                act.wait_ge(full[n % 4], n // 4 + 1)
                act.sem_inc(free[n % 4], 1)

            def empty(n, i, dst, rows_):
                act.wait_ge(full[n % 4], turn(i, n // 4 + 1, 3))
                nc.scalar.activation(dst, rows_, ACT.Copy).then_inc(free[n % 4], 1)

            def gates_e(q, i):
                n = USE["G", q]
                empty(n, i, gm[q % 4], bk[n % 4][:, 0:NT])

            def tokens_e(q, i):
                for hf in range(2):
                    n = USE["X", q, hf]
                    empty(n, i, xTs[:, q % 2, 4 * hf:4 * hf + 4, :], bk[n % 4][:].rearrange("p (k c) -> p k c", k=4))

            def pair(p, i=None):
                if p + 2 < NPAIR:
                    gates_e(p + 2, i)
                if p + 1 < NPAIR:
                    tokens_e(p + 1, i)
                act.wait_ge(s["gu"], turn(i, p + 1, 1))
                nc.scalar.activation(silu_s, pA[:, 0:FE], ACT.Silu).then_inc(s["silu_s"], 1)
                n = USE["T", p]
                empty(n, i, actT, bk[n % 4][:, 0:2 * P].rearrange("p (f c) -> p f c", f=FT))
                act.wait_ge(s["dn1"], turn(i, p + 1, 1))
                nc.scalar.activation(yrow[:, 512:], pC[:], ACT.Copy).then_inc(s["y1"], 1)

            gates_e(0, None)
            gates_e(1, None)
            tokens_e(0, None)
            pair(0)
            with act.Fori(0, 7) as i:
                for b in range(4):
                    pair(1 + b, i)
            for p in range(29, NPAIR):
                pair(p)

            act.wait_ge(s["flag"], 1)
            with act.If(act.value_load(flag[0:1, 0:1], min_val=0, max_val=1) >= 1):
                n = BASE["fgates"]
                t = fulls(n)
                nc.scalar.activation(gatesT, t[0:E, 0:NT], ACT.Copy).then_inc(s["gatesT"], 1)
                act.wait_ge(s["gatesT"], 1)
                act.sem_inc(free[n % 4], 1)
                for n in range(BASE["fgates"] + 1, BASE["fexp"]):
                    act.wait_ge(full[n % 4], n // 4 + 1)
                    act.sem_inc(free[n % 4], 1)
                with act.Fori(0, E // 4) as i:
                    for b in range(4):
                        silu(BASE["fexp"] + 12 * b, b % 2, i, i * 8 + (2 + 2 * b))

        @block.vector
        def _(dve):
            chain = [0, c_dve]

            def link(ins):
                chain[0] += 1
                ins.then_inc(chain[1], 1)
                dve.wait_ge(chain[1], chain[0])

            def fulls(n):
                b, k = bank(n)
                dve.wait_ge(full[b], k + 1)
                return bk[b]

            V = nc.vector

            def inv_var(stage, width, out, np_=P):
                n = BASE[stage]
                t = fulls(n)
                link(V.tensor_scalar(out, t[0:np_, 0:NT], 1.0 / width, EPS, ALU.mult, ALU.add))
                dve.sem_inc(free[n % 4], 1)
                link(V.reciprocal(out, out))

            def rows(ap, k):
                return ap.unsqueeze(1).broadcast_to([ap.shape[0], k, ap.shape[1]])

            def lanes(ap, t):
                return ap.unsqueeze(2).broadcast_to([ap.shape[0], ap.shape[1], t])

            dve.wait_ge(d_in, 16 * 3)
            dve.wait_ge(s["csig"], 1)
            link(V.tensor_tensor(csig[:], csig[:], cT[:], ALU.mult))
            dve.sem_inc(s["csilu"], 1)
            dve.wait_ge(s["consts"], 3)
            inv_var("norm1", D, rstd[:])
            dve.sem_inc(s["var1"], 1)
            for b in range(4):
                dve.wait_ge(used[b], 3)
            adf = ada[:].rearrange("p s k c -> p (s k) c")
            link(V.tensor_tensor(adf, pA[:, 0:48 * NC].rearrange("p (m c) -> p m c", c=NC),
                                 lanes(vec[:, V_BADA:V_BADA + 48], NC), ALU.add))
            for j, g in ((1, V_GMIX), (4, V_GFFN)):
                link(V.scalar_tensor_tensor(out=ada[:, j], in0=ada[:, j], scalar=1.0, in1=lanes(vec[:, g:g + DT], NC),
                                            op0=ALU.add, op1=ALU.mult))

            def modulate(dst, j, rs, done):
                dve.wait_ge(rs, 1)
                link(V.tensor_tensor(dst[:], xT[:], rows(rstd[:], DT), ALU.mult))
                for k in range(DT):
                    last = V.tensor_scalar(dst[:, k, 0:NP_], dst[:, k, 0:NP_], ada[:, j + 1, k, 0:1],
                                           ada[:, j, k, 0:1], ALU.mult, ALU.add)
                last.then_inc(done, 1)
                link(V.tensor_tensor(dst[:, :, NP_:NT], dst[:, :, NP_:NT], ada[:, j + 1, :, 1:NC], ALU.mult))
                V.tensor_tensor(dst[:, :, NP_:NT], dst[:, :, NP_:NT], ada[:, j, :, 1:NC], ALU.add).then_inc(done, 1)

            modulate(hT, 0, s["rs1"], s["h1"])

            inv_var("cqn", QL, rstd[:])
            dve.sem_inc(s["varq"], 1)
            dve.wait_ge(s["rsq"], 1)
            for k in range(QT):
                last = V.scalar_tensor_tensor(out=pT[:, T_Q + k, :], in0=pT[:, T_Q + k, :],
                                              scalar=vec[:, V_GQ + k:V_GQ + k + 1], in1=rstd[:],
                                              op0=ALU.mult, op1=ALU.mult)
            link(last)
            dve.sem_inc(s["cqn"], 1)
            inv_var("kvn", KL, rstd[:])
            dve.sem_inc(s["varkv"], 1)
            dve.wait_ge(s["rskv"], 1)
            for k in range(KT_):
                last = V.scalar_tensor_tensor(out=pT[:, T_KV + k, :], in0=pT[:, T_KV + k, :],
                                              scalar=vec[:, V_GKV + k:V_GKV + k + 1], in1=rstd[:],
                                              op0=ALU.mult, op1=ALU.mult)
            link(last)
            dve.sem_inc(s["ckv"], 1)
            dve.wait_ge(s["in_done"], 1)
            dve.wait_ge(d_late, 16 * 12)
            V.tensor_tensor(zp[:, :, 2:2 + NP_], pT[:, T_CC:T_CC + CT, 0:NP_], pT[:, T_CH:T_CH + CT, 0:NP_], ALU.mult)
            link(V.tensor_tensor(zs[:, :, :, 2:3].rearrange("p k s o -> p k (s o)"), pT[:, T_CC:T_CC + CT, NP_:NT],
                                 pT[:, T_CH:T_CH + CT, NP_:NT], ALU.mult))
            dve.sem_inc(s["z"], 1)
            n = BASE["krs"]
            t = fulls(n)
            R = slice(NOPE, QK)
            link(V.tensor_tensor(krT[R, 1, :], t[R, 0:NT], sinT[R, :], ALU.mult))
            dve.sem_inc(free[n % 4], 1)
            dve.wait_ge(s["krin"], 1)
            link(V.tensor_tensor(krT[R, 0, :], krT[R, 0, :], cosT[R, :], ALU.mult))
            link(V.tensor_tensor(krT[R, 1, :], krT[R, 0, :], krT[R, 1, :], ALU.add))
            dve.sem_inc(s["krot"], 1)
            big = pT[:, T_CC:T_CC + H, :]
            for h in range(H):
                n = BASE["qswap"] + h
                t = fulls(n)
                link(V.tensor_tensor(big[R, h, :], t[R, 0:NT], sinT[R, :], ALU.mult))
                dve.sem_inc(free[n % 4], 1)
            link(V.tensor_tensor(qT[R], qT[R], rows(cosT[R, :], H), ALU.mult))
            link(V.tensor_tensor(qT[R], qT[R], big[R], ALU.add))
            dve.sem_inc(s["qrot"], 1)
            link(V.tensor_scalar(gqp[:], vec[:, V_GQQ:V_GQQ + 1], QK ** -0.5, None, ALU.mult))

            def head_norm(stage, dst, g, turn):
                for h in range(H):
                    n = BASE[stage] + h
                    t = fulls(n)
                    link(V.tensor_scalar(big[0:QK, h, :], t[0:QK, 0:NT], 1.0 / QK, EPS, ALU.mult, ALU.add))
                    dve.sem_inc(free[n % 4], 1)
                link(V.reciprocal(big[0:QK], big[0:QK]))
                dve.sem_inc(s["varh"], 1)
                dve.wait_ge(s["rsh"], turn)
                link(V.scalar_tensor_tensor(out=dst[0:QK], in0=dst[0:QK], scalar=g, in1=big[0:QK],
                                            op0=ALU.mult, op1=ALU.mult))

            head_norm("qss", qT, gqp[0:QK, :], 1)
            dve.sem_inc(s["qn"], 1)
            V.tensor_copy(kT[R, :, :], rows(krT[R, 1, :], H)).then_inc(s["kfull"], 1)
            head_norm("kss", kT, vec[0:QK, V_GQK:V_GQK + 1], 2)
            dve.sem_inc(s["kn"], 1)
            link(V.tensor_tensor(sq[0:QK, 0, 0:H * NS].rearrange("p (h s) -> p h s", h=H), qT[0:QK, :, NP_:NT],
                                 kT[0:QK, :, NP_:NT], ALU.mult))
            dve.sem_inc(s["prodself"], 1)
            link(V.tensor_scalar(qsg[0:QK], qT[0:QK, :, NP_:NT], vec[0:QK, V_GQK:V_GQK + 1], None, ALU.mult))
            dve.sem_inc(s["qsg"], 1)
            link(V.tensor_copy(qrp[R].rearrange("p s h -> p h s"), qsg[R]))
            dve.sem_inc(s["qlat"], 1)
            n = BASE["self"]
            t = fulls(n)
            link(V.tensor_copy(sself[:].rearrange("p s h -> p h s"), t[:, 0:H * NS].rearrange("p (h s) -> p h s", h=H)))
            dve.sem_inc(free[n % 4], 1)
            n = BASE["qlat"]
            t = fulls(n)
            for k in range(KT_):
                last = V.tensor_copy(qlat[:, k].rearrange("p s h -> p h s"),
                                     t[:, k * H * NS:(k + 1) * H * NS].rearrange("p (h s) -> p h s", h=H))
            link(last)
            dve.sem_inc(free[n % 4], 1)
            dve.sem_inc(s["qlat"], 1)

            def finish(q):
                b = q % 2
                o = [pC, pD][b]
                dve.wait_ge(s["pv"], q + 1)
                link(V.tensor_tensor(stot[:], o[:, 64:64 + H], eself[:], ALU.add))
                link(V.reciprocal(stot[:], stot[:]))
                for k in range(KT_):
                    last = V.scalar_tensor_tensor(out=olt[:, k, :], in0=eself[:],
                                                  scalar=pT[:, T_KV + k, NP_ + q:NP_ + q + 1],
                                                  in1=o[:, k * H:(k + 1) * H], op0=ALU.mult, op1=ALU.add)
                link(last)
                link(V.tensor_tensor(olat[:, :, :, q], olt[:], rows(stot[:], KT_), ALU.mult))
                dve.sem_inc(s["olat"], 1)

            for q in range(NS):
                b = q % 2
                dve.wait_ge(wgt[b], (q // 2) * (16 * 2 * NPG) + arrival(b, "pages"))
                link(V.tensor_tensor(krsq, pgR[b][:, :, KL:KL + ROPE], pgR[b][:, :, KL:KL + ROPE], ALU.mult))
                link(V.tensor_reduce(out=krss[:], in_=krsq, op=ALU.add, axis=AX.X))
                for j in range(NPG):
                    dve.wait_ge(s["ksq"], NPG * q + j + 1)
                    V.tensor_reduce(out=kss[:, j, :], in_=ksq[:, j % 2, :].rearrange("p (h d) -> p h d", h=H),
                                    op=ALU.add, axis=AX.X).then_inc(s["ksq_used"], 1)
                dve.wait_ge(s["ksq_used"], NPG * (q + 1))
                link(V.tensor_tensor(kss[:], kss[:], lanes(krss[:], H), ALU.add))
                link(V.tensor_scalar(kss[:], kss[:], 1.0 / QK, EPS, ALU.mult, ALU.add))
                link(V.reciprocal(kss[:], kss[:]))
                dve.sem_inc(s["kss"], 1)
                dve.wait_ge(s["rstds"], q + 1)
                dve.wait_ge(s["s_mm"], q + 1)
                if q:
                    finish(q - 1)
                link(V.tensor_tensor(ssc[:], [pA, pB][b][:, 0:NPG * H].rearrange("p (j h) -> p j h", h=H), kss[:],
                                     ALU.mult))
                link(V.tensor_reduce(out=smx[:], in_=ssc[:].rearrange("p j h -> p h j"), op=ALU.max, axis=AX.X))
                dve.sem_inc(s["smx"], 1)
                dve.wait_ge(s["allmx"], q + 1)
                link(V.tensor_tensor(samx[:], samx[:], sself[:, q, :], ALU.max))
                V.tensor_tensor(ssub[:], sself[:, q, :], samx[:], ALU.subtract)
                link(V.tensor_tensor(ssc[:], ssc[:], rows(samx[:], NPG), ALU.subtract))
                dve.sem_inc(s["ssub"], 1)
                dve.wait_ge(s["pexp"], q + 1)
                link(V.tensor_reduce(out=ssum[:], in_=sp_[:, b].rearrange("p j h -> p h j"), op=ALU.add, axis=AX.X))
                dve.sem_inc(s["psumd"], 1)
            finish(NS - 1)

            for h in range(H):
                n = BASE["att"] + 3 * h
                t = fulls(n)
                if h:
                    dve.wait_ge(s["anorm"], h)
                link(V.tensor_tensor(am, t[:, 0:3 * P], mask[:], ALU.add))
                dve.sem_inc(free[n % 4], 1)
                V.tensor_reduce(out=amx[:, 0:1], in_=am[:, 0:P], op=ALU.max, axis=AX.X)
                link(V.tensor_reduce(out=amx[:, 1:2], in_=am[:, P:3 * P], op=ALU.max, axis=AX.X))
                link(V.tensor_scalar(amx[:], amx[:], -1.0, None, ALU.mult))
                dve.sem_inc(s["amx"], 1)
                dve.wait_ge(s["aexp"], h + 1)
                link(V.reciprocal(arc[:], asum[:]))
                V.tensor_scalar(aP[:, 0:P], aP[:, 0:P], arc[:, 0:1], None, ALU.mult)
                V.tensor_scalar(aP[:, P:3 * P], aP[:, P:3 * P], arc[:, 1:2], None, ALU.mult).then_inc(s["anorm"], 1)

            out = pT[:, T_CC:T_CC + CT, :]
            for k in range(CT):
                w = [vec[:, V_CONV + j * CT + k:V_CONV + j * CT + k + 1] for j in range(3)]
                V.tensor_scalar(out[:, k, 0:NP_], zp[:, k, 0:NP_], w[0], None, ALU.mult)
                link(V.tensor_scalar(out[:, k, NP_:NT], zs[:, k, :, 0], w[0], None, ALU.mult))
                for j in (1, 2):
                    V.scalar_tensor_tensor(out=out[:, k, 0:NP_], in0=zp[:, k, j:j + NP_], scalar=w[j],
                                           in1=out[:, k, 0:NP_], op0=ALU.mult, op1=ALU.add)
                    link(V.scalar_tensor_tensor(out=out[:, k, NP_:NT], in0=zs[:, k, :, j], scalar=w[j],
                                                in1=out[:, k, NP_:NT], op0=ALU.mult, op1=ALU.add))
            link(V.tensor_tensor(pT[:, T_CB:T_CB + CT, :], pT[:, T_CB:T_CB + CT, :], out, ALU.mult))
            dve.sem_inc(s["conv"], 1)

            n = BASE["vmean"]
            t = fulls(n)
            link(V.tensor_scalar(rstd[:], t[:, 0:NT], 1.0 / CW, None, ALU.mult))
            dve.sem_inc(free[n % 4], 1)
            link(V.tensor_tensor(vn[:], pT[:, T_V:T_V + CT, :], rows(rstd[:], CT), ALU.subtract))
            dve.sem_inc(s["vcen"], 1)
            inv_var("vvar", CW, rstd[:])
            dve.sem_inc(s["varv"], 1)
            dve.wait_ge(s["rsv"], 1)
            for k in range(CT):
                last = V.scalar_tensor_tensor(out=vn[:, k, :], in0=vn[:, k, :],
                                              scalar=vec[:, V_GV + k:V_GV + k + 1], in1=rstd[:],
                                              op0=ALU.mult, op1=ALU.mult)
            link(last)
            dve.sem_inc(s["vn"], 1)
            for c in range(CT):
                n = BASE["spat"] + c
                t = fulls(n)
                link(V.tensor_tensor(big[:, c, 0:NP_].rearrange("p (b t) -> p b t", b=2),
                                     t[:, 0:NP_].rearrange("p (b t) -> p b t", b=2), rows(bsp[:, c, :], 2), ALU.add))
                dve.sem_inc(free[n % 4], 1)
                link(V.tensor_scalar(big[:, c, NP_:NT], vn[:, c, NP_:NT], vec[:, V_W00 + c:V_W00 + c + 1],
                                     bsp[:, c, 0:1], ALU.mult, ALU.add))
            link(V.tensor_tensor(pT[:, T_U:T_U + CT, :], pT[:, T_U:T_U + CT, :], big[:, 0:CT, :], ALU.mult))
            dve.sem_inc(s["sg"], 1)

            for m in range(DT):
                for b in range(3):
                    n = BASE["br"] + 6 * m + 3 + b
                    t = fulls(n)
                    dve.wait_ge(s["gsig"], 3 * m + b + 1)
                    gs = sq[:, 3 * (m % 2):3 * (m % 2) + 3, :]
                    link(V.tensor_tensor(gs[:, b, :], t[:, 0:NT], gs[:, b, :], ALU.mult))
                    dve.sem_inc(free[n % 4], 1)
                link(V.tensor_tensor(gs[:, 0, :], gs[:, 0, :], gs[:, 1, :], ALU.add))
                link(V.tensor_tensor(mg[:, m, :], gs[:, 0, :], gs[:, 2, :], ALU.add))
                dve.sem_inc(s["merged"], 1)

            def residual(dst, ps, j, m):
                V.scalar_tensor_tensor(out=dst[:, m, 0:NP_], in0=ps[:, 0:NP_], scalar=ada[:, j, m, 0:1],
                                       in1=xT[:, m, 0:NP_], op0=ALU.mult, op1=ALU.add)
                link(V.tensor_tensor(sq[:, 7, 0:NS], ps[:, NP_:NT], ada[:, j, m, 1:NC], ALU.mult))
                link(V.tensor_tensor(dst[:, m, NP_:NT], sq[:, 7, 0:NS], xT[:, m, NP_:NT], ALU.add))

            for m in range(DT):
                n = BASE["out"] + m
                t = fulls(n)
                residual(xT, t, 2, m)
                dve.sem_inc(free[n % 4], 1)
            dve.sem_inc(s["x1"], 1)
            inv_var("norm2", D, rstd[:])
            dve.sem_inc(s["var2"], 1)
            modulate(hT, 3, s["rs2"], s["h2"])

            dve.wait_ge(s["lsig"], 3)
            for j, m in enumerate((P, P, NS)):
                link(V.tensor_tensor(ch[0:m, j], lg[0:m, j], brou[0:m], ALU.add))
                for g in range(8):
                    last = V.max(top[0:m, j, g, :], ch[0:m, j, g * 8:(g + 1) * 8])
                link(last)
                link(V.tensor_tensor(gsc[0:m, j, 0:8], top[0:m, j, :, 0], top[0:m, j, :, 1], ALU.add))
                link(V.max(gtop[0:m, j], gsc[0:m, j, 0:8]))
                V.memset(gsc[0:m, j, 8:12], 3 * BIG)
                link(V.memset(gtop[0:m, j, 4:8], 3 * BIG))
                link(V.match_replace(out=gms[0:m, j], in_to_replace=gtop[0:m, j], in_values=gsc[0:m, j],
                                     imm_value=-BIG))
                link(V.tensor_scalar(gms[0:m, j], gms[0:m, j], -BIG, BIG, ALU.is_equal, ALU.mult))
                link(V.tensor_scalar(gms[0:m, j], gms[0:m, j], BIG, None, ALU.subtract))
                g3 = lanes(gms[0:m, j, 0:8], 8)
                c3 = ch[0:m, j].rearrange("p (g e) -> p g e", g=8)
                m3 = cm[0:m, j].rearrange("p (g e) -> p g e", g=8)
                link(V.tensor_tensor(m3, c3, g3, ALU.add))
                link(V.max(gtop[0:m, j], cm[0:m, j]))
                link(V.match_replace(out=ch[0:m, j], in_to_replace=gtop[0:m, j], in_values=cm[0:m, j],
                                     imm_value=-3 * BIG))
                link(V.tensor_scalar(ch[0:m, j], ch[0:m, j], -3 * BIG, None, ALU.is_equal))
                link(V.tensor_tensor(lg[0:m, j], lg[0:m, j], ch[0:m, j], ALU.mult))
                link(V.tensor_reduce(out=wsum[0:m, j:j + 1], in_=lg[0:m, j], op=ALU.add, axis=AX.X))
                link(V.reciprocal(wsum[0:m, j:j + 1], wsum[0:m, j:j + 1]))
                link(V.tensor_scalar(lg[0:m, j], lg[0:m, j], wsum[0:m, j:j + 1], ROUTED, ALU.mult, ALU.mult))
            dve.sem_inc(s["gates"], 1)

            for f in range(FT):
                n = BASE["shgu"] + 2 * f + 1
                t = fulls(n)
                dve.wait_ge(s["silu"], f + 1)
                V.tensor_tensor(actg[:, 1, f, :], acts[:, 1, f, :], t[:, 0:NT], ALU.mult).then_inc(s["act"], 1)
                dve.wait_ge(s["act"], f + 1)
                dve.sem_inc(free[n % 4], 1)
            link(V.memset(posm, -1.0))
            n = BASE["pos"]
            t = fulls(n)
            for j, m in enumerate((P, P, NS)):
                link(V.tensor_tensor(posm[0:m, j], t[0:m, j * E:(j + 1) * E], ch[0:m, j], ALU.mult))
                link(V.tensor_scalar(posm[0:m, j], posm[0:m, j], 1.0, None, ALU.subtract))
            dve.sem_inc(free[n % 4], 1)
            link(V.tensor_reduce(out=pmax[:], in_=posm.rearrange("p j e -> p (j e)"), op=ALU.max, axis=AX.X))
            dve.sem_inc(s["pmax"], 1)

            at = [0, None, c_dve]

            def step(ins):
                at[0] += 1
                ins.then_inc(c_dve, 1)
                dve.wait_ge(c_dve, at[0] if at[1] is None else at[1] + at[0])

            def build_gates(q, i):
                e = 2 * q if i is None else i * 8 + 2 * q
                for x in range(2):
                    for j, m in enumerate((P, P, NS)):
                        last = V.tensor_scalar(gtm[0:m, j, CAP * x:CAP * (x + 1)], iota[0:m, :],
                                               posm[0:m, j, bass.ds(e + x, 1)], lg[0:m, j, bass.ds(e + x, 1)],
                                               ALU.is_equal, ALU.mult)
                last.then_inc(s["gt"], 1)

            def index(q, i):
                n = USE["G", q]
                dve.wait_ge(free[n % 4], turn(i, n // 4 + 1, 3))
                step(V.scalar_tensor_tensor(out=idw, in0=gm[q % 4], scalar=0.0, in1=toki[:], op0=ALU.is_gt,
                                            op1=ALU.mult, accum_out=idxf[:, q % 2:q % 2 + 1]))
                V.tensor_copy(idx[:, q % 2:q % 2 + 1], idxf[:, q % 2:q % 2 + 1]).then_inc(s["idx"], 1)

            def add(q, i, ms):
                for m in ms:
                    n = USE["C", q, m]
                    dve.wait_ge(full[n % 4], turn(i, n // 4 + 1, 3))
                    V.tensor_tensor(yacc[:, m, :], yacc[:, m, :], bk[n % 4][:, 0:NT], ALU.add).then_inc(free[n % 4], 1)

            def pair(p, i=None):
                if p + 2 < NPAIR:
                    index(p + 2, i)
                if p + 3 < NPAIR:
                    build_gates(p + 3, i)
                dve.wait_ge(s["silu_s"], turn(i, p + 1, 1))
                V.tensor_tensor(act_s, silu_s, pA[:, FE:2 * FE], ALU.mult).then_inc(s["act_s"], 1)
                if p:
                    add(p - 1, i, range(8))
                dve.wait_ge(s["dn0"], turn(i, p + 1, 1))
                V.tensor_copy(yrow[:, 0:512], pB[:]).then_inc(s["y0"], 1)

            build_gates(0, None)
            dve.wait_ge(s["pall"], 1)
            V.tensor_scalar(flag[:], pall[:], float(LIMIT), None, ALU.is_ge).then_inc(s["flag"], 1)
            for m in range(DT):
                n = BASE["shdn"] + m
                t = fulls(n)
                link(V.tensor_copy(yacc[:, m, :], t[:, 0:NT]))
                dve.sem_inc(free[n % 4], 1)
            at[0] = chain[0]
            index(0, None)
            build_gates(1, None)
            index(1, None)
            build_gates(2, None)
            pair(0)
            first = at[0]
            with dve.Fori(0, 7) as i:
                for b in range(4):
                    at[1] = i * 4
                    at[0] = first + b
                    pair(1 + b, i)
            at[0], at[1] = first + 28, None
            for p in range(29, NPAIR):
                pair(p)
            add(NPAIR - 1, None, range(8))

            dve.wait_ge(s["flag"], 1)
            with dve.If(dve.value_load(flag[0:1, 0:1], min_val=0, max_val=1) >= 1):
                for j, m in enumerate((P, P, NS)):
                    last = V.scalar_tensor_tensor(out=ch[0:m, j], in0=posm[0:m, j], scalar=float(LIMIT), in1=lg[0:m, j],
                                                  op0=ALU.is_ge, op1=ALU.mult)
                last.then_inc(s["fgates"], 1)
                dve.wait_ge(s["gatesT"], 1)
                per = 13
                with dve.Fori(0, E // 4) as i:
                    for b in range(4):
                        nth = [per * b]

                        def fstep(ins):
                            nth[0] += 1
                            ins.then_inc(c_f, 1)
                            dve.wait_ge(c_f, i * (4 * per) + nth[0])

                        par = b % 2
                        n0 = BASE["fexp"] + 12 * b
                        fstep(V.tensor_scalar(gsel[:, par, :], gatesT, ident[0:E, bass.ds(i * 4 + b, 1)], None, ALU.mult))
                        dve.sem_inc(s["gsel"], 1)
                        for f in range(FT):
                            n = n0 + 2 * f + 1
                            dve.wait_ge(full[n % 4], i * 12 + (n // 4 + 1))
                            dve.wait_ge(s["silu"], i * 8 + (2 * b + f + 3))
                            fstep(V.tensor_tensor(actg[:, par, f, :], acts[:, par, f, :], bk[n % 4][:, 0:NT], ALU.mult))
                            dve.sem_inc(free[n % 4], 1)
                        dve.wait_ge(s["gbc"], i * 4 + (b + 1))
                        for f in range(FT):
                            fstep(V.tensor_tensor(actg[:, par, f, :], actg[:, par, f, :], [pC, pD][par][:, 0:NT],
                                                  ALU.mult))
                            dve.sem_inc(s["act"], 1)
                        for m in range(DT):
                            n = n0 + 4 + m
                            dve.wait_ge(full[n % 4], i * 12 + (n // 4 + 1))
                            fstep(V.tensor_tensor(yacc[:, m, :], yacc[:, m, :], bk[n % 4][:, 0:NT], ALU.add))
                            dve.sem_inc(free[n % 4], 1)
                        assert nth[0] == per * (b + 1)
            V.memset(idxf[:], 0.0).then_inc(c_end, 1)
            dve.wait_ge(c_end, 1)
            chain[0], chain[1] = 1, c_end
            for m in range(DT):
                residual(hT, yacc[:, m, :], 5, m)
            dve.sem_inc(s["yout"], 1)


def _constants():
    pos = np.concatenate([np.arange(NP_), np.full(NS, NPG * P)]).astype(np.float32)
    inv = (np.float32(10000.0) ** (-np.arange(0, ROPE, 2, dtype=np.float32) / np.float32(ROPE))).astype(np.float32)
    ang = (pos[:, None] * inv[None, :]).astype(np.float32).T
    cos, sin = np.zeros((P, NT), np.float32), np.zeros((P, NT), np.float32)
    cos[NOPE:QK] = np.concatenate([np.cos(ang), np.cos(ang)])
    sin[NOPE:QK] = np.concatenate([np.sin(ang), np.sin(ang)])
    swap = np.zeros((P, ROPE), np.float32)
    h = ROPE // 2
    for j in range(h):
        swap[NOPE + h + j, j] = -1.0
        swap[NOPE + j, h + j] = 1.0
    t = np.arange(P)
    slots = np.arange(CAP)
    tri = np.where(t[None, :] <= t[:, None], 0.0, -BIG).astype(np.float32)
    mask = np.concatenate([tri, np.zeros((P, P), np.float32), tri], axis=1)
    return {"ident": np.eye(P, dtype=np.float32), "swapm": swap, "cosT": cos, "sinT": sin, "mask": mask,
            "tri": (t[:, None] <= t[None, :]).astype(np.float32),
            "iota": np.tile(np.where(slots < LIMIT, slots, -7).astype(np.float32), (P, 1)),
            "toki": np.tile(np.arange(NT, dtype=np.float32), (P, 1))}


_OUTS = {"yT": (P, DT, NT), "ckvT": (P, KT_, NT), "krT": (ROPE, NT), "convP": (P, CT, 2), "convS": (P, CT, NS, 2),
         "vnP": (P, CT, P), "vnS": (P, CT, NS)}


def kernel(**inputs):
    import concourse.bacc as _bacc
    from concourse.bass_utils import run_bass_kernel_spmd as _run

    a = {k: np.asarray(v) for k, v in inputs.items()}
    a = {k: (v[0] if v.ndim > 1 and k not in ("x_prompt", "x_sample", "page_table", "c_prompt", "c_sample") else v)
         for k, v in a.items()}

    def feat(v, t):
        return v.T.reshape(t, P, -1).transpose(1, 0, 2)

    def wrows(w):
        return w.reshape(-1, P, w.shape[-1]).transpose(1, 0, 2)

    x = np.concatenate([a["x_prompt"][0], a["x_sample"][:, 0]], axis=0)
    c = np.concatenate([a["c_prompt"], a["c_sample"]], axis=0)
    vecs = [v.reshape(-1, P).T for v in (a["b_ada"], a["g_norm_mix"], a["g_norm_ffn"], a["g_q_lat"], a["g_kv_lat"],
                                         a["g_v_ln"], a["w_conv"].reshape(-1), np.repeat(a["w_spatial"][:, 0, 0], 64))]
    vecs += [np.pad(a[g], (0, P - QK))[:, None] for g in ("g_qk_q", "g_qk_k")]
    lat = a["cache_kv_latent"]
    kr = a["cache_k_rope"]
    latT = lat.transpose(0, 2, 1).reshape(NPOOL, KT_, P, P).transpose(0, 2, 1, 3)
    krT = np.pad(kr.transpose(0, 2, 1), ((0, 0), (NOPE, P - QK), (0, 0)))[:, :, None, :]
    arrays = {
        "xT": feat(x, DT), "cT": feat(c, DT), "vec": np.concatenate(vecs, axis=1),
        "ptab": a["page_table"].reshape(1, -1).astype(np.int32),
        "poolR": np.concatenate([lat, kr], axis=2), "poolT": np.concatenate([latT, krT], axis=2),
        "stateT": a["state_conv"].transpose(2, 0, 1).reshape(CT, P, NS, 2).transpose(1, 0, 2, 3),
        "w_uq": wrows(a["w_uq"].reshape(QL, -1)), "w_uk": wrows(a["w_uk"].reshape(KL, -1)),
        "w_uv": wrows(a["w_uv"].reshape(KL, -1)), "w_ukT": a["w_uk"].transpose(2, 1, 0),
        "wspT": a["w_spatial"].transpose(2, 0, 1), "w_router": wrows(a["w_router"]),
        "bsp": np.repeat(a["b_spatial"].reshape(CT, 2, 1, P), 64, axis=2).reshape(CT, P, P).transpose(1, 0, 2),
        "brou": np.broadcast_to(a["b_router"], (P, E)),
    }
    for k in ("w_ada", "w_in", "w_br_a", "w_br_b", "w_br_c", "w_out", "w_sh_gate", "w_sh_up", "w_sh_down",
              "w_e_gate", "w_e_up", "w_e_down"):
        arrays[k] = a[k]
    arrays.update(_constants())
    arrays = {k: np.ascontiguousarray(v) for k, v in arrays.items()}

    nc = _bacc.Bacc("TRN2", target_bir_lowering=False, num_devices=1)
    A = {k: nc.dram_tensor(f"in_{k}", v.shape, mybir.dt.from_np(v.dtype), kind="ExternalInput").ap()
         for k, v in arrays.items()}
    O = {k: nc.dram_tensor(f"out_{k}", v, F32, kind="ExternalOutput").ap() for k, v in _OUTS.items()}
    build(nc, A, O)
    r = _run(nc, [{f"in_{k}": v for k, v in arrays.items()}], core_ids=[0]).results[0]
    o = {k: np.asarray(r[f"out_{k}"]) for k in _OUTS}

    def tokens(v):
        return v.transpose(1, 0, 2).reshape(-1, v.shape[2]).T

    y, ckv, krope = tokens(o["yT"]), tokens(o["ckvT"]), o["krT"].T
    conv_p, vn_p, vn_s = tokens(o["convP"]), tokens(o["vnP"]), tokens(o["vnS"])
    conv_s = o["convS"].transpose(2, 3, 1, 0).reshape(NS, 2, CW)
    c_ = np.ascontiguousarray
    return (c_(y[None, :NP_]), c_(y[NP_:, None]), c_(ckv[None, None, :NP_]), c_(krope[None, None, :NP_]),
            c_(conv_p[None, None]), c_(vn_p[None, None]), c_(ckv[None, NP_:, None]), c_(krope[None, NP_:, None]),
            c_(conv_s[None]), c_(vn_s[None, :, None]))
```

```python
from contextlib import ExitStack

import numpy as np
import concourse.bass as bass
from concourse import mybir

ALU = mybir.AluOpType
ACT = mybir.ActivationFunctionType
AX = mybir.AxisListType
F32 = mybir.dt.float32
I32 = mybir.dt.int32
RMAX = bass.bass_isa.ReduceOp.max

P = 128
D = 1024
DT = D // P
NP_ = 256
NS = 8
NT = NP_ + NS
NC = 1 + NS
H = 8
NOPE, ROPE = 64, 32
QK = NOPE + ROPE
QL, KL = 384, 256
QT, KT_ = QL // P, KL // P
CW = 512
CT = CW // P
NPG = 8
NPOOL = 80
E = 64
FE = 256
FT = FE // P
EPS = 1e-6
ROUTED = 2.5
BIG = 1e30
GATE0 = 672 + 5 * CW
SLOT = 8 * 768
NSLOT = 4

V_BADA, V_GMIX, V_GFFN, V_GQ, V_GKV, V_GV, V_CONV, V_W00, V_GQQ, V_GQK = 0, 48, 56, 64, 67, 69, 73, 85, 89, 90
NVEC = 91
T_Q, T_KV, T_CB, T_CC, T_CH, T_U, T_V = 0, 3, 5, 9, 13, 17, 21
NTILE = 25
KNOW = []
for _q in range(NS):
    KNOW += [(f"ksc{_q + 1}", 1), (f"know{_q + 1}", NPG)] if _q + 1 < NS else []
    KNOW += {0: [("vmean", 1)], 1: [("vvar", 1)], 2: [("vtr", 2)], 3: [("spat", 4)]}.get(_q, [])
BRANCH = []
for _m in range(DT):
    BRANCH += ([(f"bg{_m + 2}", 3)] if _m + 2 < DT else []) + [(f"bo{_m}", 3)]
STAGES = [("ada0", 1), ("norm1", 1), ("ada1", 3), ("in0", 6), ("in1", 20), ("cqn", 1), ("kvn", 1), ("krs", 1), ("ada4", 2),
          ("q", 8), ("ada6", 2), ("k", 8), ("ada8", 2), ("ada10", 2), ("v", 2), ("qswap", 8), ("ksum", 1),
          ("know0", NPG // 2), ("kinv", 8), ("qsum", 1), ("know0b", NPG // 2), ("qinv", 8), ("self", 1), ("qlat", 1),
          ("ksc0", 1)] + KNOW + [
          ("bg0", 3), ("bg1", 3), ("otr", 2), ("uvs", 4)] + BRANCH + [
          ("out", 8), ("norm2", 1), ("rout", 3), ("h2tr", 6), ("shgu", 4), ("pos", 1), ("gt0", 1), ("shdn0", 4),
          ("gt1", 1), ("shdn4", 4),
          ("moe", 6 + 12 * (E // 2 - 3) + 11 + 9 + 8), ("fgates", 4), ("fexp", 12 * E)]
BASE = {}
_n = 0
for _s, _c in STAGES:
    BASE[_s] = _n
    _n += _c

CAP = 64
LIMIT = 64
NPAIR = E // 2
USE = {}
_n = BASE["moe"]


def _use(*key):
    global _n
    USE[key] = _n
    _n += 1


USE["G", 0], USE["G", 1] = BASE["gt0"], BASE["gt1"]
_use("X", 0, 0)
_use("X", 0, 1)
for _p in range(NPAIR):
    if _p + 2 < NPAIR:
        _use("G", _p + 2)
    if _p + 1 < NPAIR:
        _use("X", _p + 1, 0)
        _use("X", _p + 1, 1)
    for _m in range(4 if _p else 0):
        _use("C", _p - 1, _m)
    _use("T", _p)
    for _m in range(4 if _p else 0):
        _use("C", _p - 1, _m + 4)
for _m in range(8):
    _use("C", NPAIR - 1, _m)
assert _n == BASE["fgates"]


def turn(i, n, per):
    return n if i is None else i * (4 * per) + n


PAGES = [("pages", NPG)] * 4
ITEMS = [[(n, 1) for n in ("ada0", "in0", "u", "ada5", "ada8", "ada10")] + PAGES
         + [("rows0", 0), ("g1", 3), ("g3", 3), ("exp", 2)],
         [(n, 1) for n in ("ada1", "cb", "v", "ada6", "ada9", "ada11")] + PAGES
         + [("rows1", 3 * NPG), ("g2", 3), ("exp", 2)],
         [("ada2", 1), ("cc", 1), ("mla", 3), ("br0", 3), ("out0", 1), ("shared", 3), ("exp", 2)],
         [(n, 1) for n in ("ada3", "ch", "ada4", "ada7")] + [("late", 2), ("g0", 3), ("br1", 3), ("out1", 1),
                                                           ("exp", 2)]]
ADA_SLOT = (0, 1, 2, 3, 3, 0, 1, 3, 0, 1, 0, 1)


def before(b, name):
    return [n for n, _ in ITEMS[b]].index(name)


def arrival(b, name):
    return 16 * sum(d for _, d in ITEMS[b][:before(b, name) + 1])


def build(nc, A, O):
    with ExitStack() as ctx:
        def sb(name, shape, dt=F32):
            return ctx.enter_context(nc.sbuf_tensor(name, shape, dt))

        def sem(name):
            return ctx.enter_context(nc.semaphore(name))

        ring = sb("ring", [P, NSLOT, SLOT])
        xT = sb("xT", [P, DT, NT])
        hT = sb("hT", [P, DT, NT])
        sq = sb("sq", [P, DT, NT])
        pT = sb("pT", [P, NTILE, NT])
        vec = sb("vec", [P, NVEC])
        cT = sb("cT", [P, DT, NC])
        csig = sb("csig", [P, DT, 32])
        ada = sb("ada", [P, 6, DT, NC])
        ones = sb("ones", [P, P])
        ident = sb("ident", [P, P])
        swapm = sb("swapm", [P, ROPE])
        cosT = sb("cosT", [P, NT])
        sinT = sb("sinT", [P, NT])
        mask = sb("mask", [P, 3 * P])
        rstd = sb("rstd", [P, NT])
        krT = sb("krT", [P, 2, NT])
        bsp = sb("bsp", [P, CT, P])
        brou = sb("brou", [P, E])
        wrou = sb("wrou", [P, DT, E])
        gqp = sb("gqp", [P, 1])
        qT = sb("qT", [P, H, NT])
        kT = sb("kT", [P, H, NT])
        vtok = sb("vtok", [P, 2, CW])
        oaT = sb("oaT", [P, CT, NT])
        ptab = sb("ptab", [1, NS * NPG], I32)
        qlat = sb("qlat", [P, KT_, NS, 32])
        qsg = sb("qsg", [P, H, NS])
        sself = sb("sself", [P, NS, H])
        ksq = sb("ksq", [P, 2, H * NOPE])
        olat = sb("olat", [P, KT_, H, NS])
        abuf = sb("abuf", [P, 9 * P])
        fold = sb("fold", [P, NC])
        onecol = sb("onecol", [P, 2 * H - 1])
        hinv = abuf[0:H, 0:2 * NT].rearrange("p (x t) -> p x t", x=2)
        fold2 = sb("fold2", [P, 2 * H])
        scr = pT[:, 0:QT, :].rearrange("p t n -> p (t n)")[:, 0:512]
        qrp = pT[:, 0:QT, :].rearrange("p t n -> p (t n)")[:, 512:768].rearrange("p (q x) -> p q x", q=NS)
        krss = sb("krss", [P, NS, NPG])
        am, aP, aPT = (abuf[:, j * 3 * P:(j + 1) * 3 * P] for j in range(3))
        amx = sb("amx", [P, 2])
        asum = sb("asum", [P, 2])
        arc = sb("arc", [P, 2])
        zp = sb("zp", [P, CT, 2 + NP_])
        zs = sb("zs", [P, CT, NS, 3])
        lg = sb("lg", [P, 3, E])
        ch = sb("ch", [P, 3, E])
        cm = sb("cm", [P, 3, E])
        top = sb("top", [P, 3, 8, 8])
        gsc = sb("gsc", [P, 3, 12])
        gtop = sb("gtop", [P, 3, 8])
        gms = sb("gms", [P, 3, 12])
        wsum = sb("wsum", [P, 3])
        gatesT = abuf[0:E, 0:NT]
        gsel = abuf[0:E, NT:3 * NT].rearrange("p (a t) -> p a t", a=2)
        kTf = kT[:].rearrange("p h t -> p (h t)")
        acts = kTf[:, 0:4 * NT].rearrange("p (a f t) -> p a f t", a=2, f=2)
        tri, iota = sinT[:, 0:P], sinT[:, P:P + CAP]
        toki = cosT
        posm = abuf[:, 3 * NT:3 * NT + 3 * E].rearrange("p (j e) -> p j e", j=3)
        pmax = sb("pmax", [P, 1])
        pall = sb("pall", [P, 1])
        flag = sb("flag", [P, 1], I32)
        idxf = sb("idxf", [P, 2])
        idx = sb("idx", [P, 2], mybir.dt.uint32)
        sqf = sq[:].rearrange("p h t -> p (h t)")
        NG = NPG * H
        kss, ssc, sp_ = (sqf[:, NG + j * NS * NG:NG + (j + 1) * NS * NG].rearrange("p (q j h) -> p q j h", q=NS, j=NPG)
                         for j in range(3))
        krsq = sqf[:, NG + 2 * NS * NG:NG + 2 * NS * NG + NPG * ROPE].rearrange("p (j d) -> p j d", j=NPG)
        smx, samx, ssub, eself, ssum, stot = (
            sqf[:, NG + 3 * NS * NG + j * NG:NG + 3 * NS * NG + (j + 1) * NG].rearrange("p (q h) -> p q h", q=NS)
            for j in range(6))
        adb = ksq
        orow = ksq[:, :, 0:KL]
        otmp = ksq[:, :, KL:KL + NG]
        xs = sqf[:, 0:2 * D].rearrange("p (a c) -> p a c", a=2)
        qTf = qT[:].rearrange("p h t -> p (h t)")
        xTs = qTf[:, 0:2 * D].rearrange("p (a k c) -> p a k c", a=2, k=DT)
        yrow = vtok[:].rearrange("p a c -> p (a c)")
        free_p = pT[:].rearrange("p t n -> p (t n)")[:, DT * NT:NTILE * NT]
        h2tok = free_p[:, 0:3 * D].rearrange("p (j c) -> p j c", j=3)
        gm = [free_p[:, 3 * D + a * NT:3 * D + (a + 1) * NT] for a in range(4)]
        oaf = oaT[:].rearrange("p k t -> p (k t)")
        silu_s, act_s = oaf[:, 0:FE], oaf[:, FE:2 * FE]
        actT = oaf[:, 2 * FE:3 * FE].rearrange("p (f c) -> p f c", f=FT)
        idw = oaf[:, 3 * FE:3 * FE + NT]
        gtm = ksq[:].rearrange("p a c -> p (a c)")[:, 0:3 * P].rearrange("p (j c) -> p j c", j=3)
        actg = kTf[:, 4 * NT:8 * NT].rearrange("p (a f t) -> p a f t", a=2, f=2)
        vn = pT[:, T_V:T_V + CT, :]
        vsq = pT[:, T_CH:T_CH + CT, :]
        vntok = vsq.rearrange("p k t -> p (k t)")[:, 0:2 * CW].rearrange("p (b c) -> p b c", b=2)
        gs = [pT[:, T_CC:T_CC + 3, :], pT[:, T_CC + 3:T_CC + 6, :], sq[:, 0:3, :]]
        mg = qT
        yacc = pT[:, 0:DT, :]

        def part(b, at, *dims):
            n = int(np.prod(dims))
            ap = ring[:, b, at:at + n]
            if len(dims) == 2:
                return ap.rearrange("p (a b) -> p a b", a=dims[0])
            return ap.rearrange("p (a b c) -> p a b c", a=dims[0], b=dims[1])

        wuq = part(2, 0, QT, H * QK)
        wuk = part(2, QT * H * QK, KT_, H * NOPE)
        wuv = part(2, QT * H * QK + KT_ * H * NOPE, KT_, H * NOPE)
        wukT = part(3, 0, H, KL)[0:NOPE]
        wspT = part(3, H * KL, 8, P)
        PGW = (KT_ + 1) * P + ROPE
        pgT = [part(b, 0, NPG, PGW) for b in range(2)]
        RS = NPG * KL
        pgR = [part(q // 3, (q % 3) * RS, NPG, KL) for q in range(6)]
        pgR += [qTf[:, 0:RS].rearrange("p (j c) -> p j c", j=NPG), kTf[:, 0:RS].rearrange("p (j c) -> p j c", j=NPG)]

        bk = [ctx.enter_context(nc.psum_tensor(f"bank{i}", [P, 512], F32)) for i in range(4)]
        pA = ctx.enter_context(nc.psum_tensor("pA", [P, 512], F32))
        pB = ctx.enter_context(nc.psum_tensor("pB", [P, 512], F32))
        pC = ctx.enter_context(nc.psum_tensor("pC", [P, 512], F32))
        pD = ctx.enter_context(nc.psum_tensor("pD", [P, 512], F32))

        full = [sem(f"bank_full{i}") for i in range(4)]
        free = [sem(f"bank_free{i}") for i in range(4)]
        wgt = [sem(f"slot_filled{i}") for i in range(NSLOT)]
        used = [sem(f"slot_used{i}") for i in range(NSLOT)]
        d_in = sem("small_inputs")
        d_late = sem("late_inputs")
        d_ptab = sem("page_table")
        d_fold = sem("fold_input")
        d_c = sem("conditioning")
        d_rows = sem("latent_rows")
        d_tabs = sem("routing_tables")
        wgd = [sem(f"down_filled{i}") for i in range(NSLOT)]
        d_out = sem("outputs")
        d_vout = sem("v_outputs")
        d_y = sem("y_output")
        c_dve = sem("vector_chain")
        c_act = sem("scalar_chain")
        s = {n: sem(n) for n in (
            "consts", "onecol", "csig", "csilu", "ada_mm", "ada", "sq1", "var1", "rs1", "h1", "in_done", "gsig",
            "sqq", "varq", "rsq", "cqn", "varkv", "rskv", "ckv", "krin", "krot", "qcopy", "qrot", "sqh", "varh",
            "rsh", "kfull", "kn", "vtok", "prodself", "qsg", "qlat", "fold", "krd", "am", "ksq", "ksq_used",
            "kss", "rstds", "smx", "allmx", "ssub", "pexp", "psumd", "tot_mm", "pv", "orow", "olat", "oa_s",
            "asc", "atr", "aout", "amx", "aexp", "anorm", "aPT", "oa", "z", "conv", "vcen", "sqv", "varv",
            "rsv", "vn", "vntok", "sg", "wsp", "merged", "x1", "sq2", "var2", "rs2", "h2", "lsig", "gates",
            "gatesT", "gsel", "gbc", "silu", "act", "yout", "h2tok", "pmax", "pall", "flag", "gt", "idx", "gu",
            "silu_s", "act_s", "dn0", "dn1", "y0", "y1", "fgates", "turn")}
        d_tok = sem("h2_stored")
        d_x = [sem("tokens_gathered0"), sem("tokens_gathered1")]
        c_f = sem("vector_chain_dense")
        c_end = sem("vector_chain_end")
        h2rows = nc.dram_tensor("h2_rows", (NT, D), F32, kind="Internal").ap()

        def bank(n):
            return n % 4, n // 4

        block = ctx.enter_context(nc.Block())

        @block.sync
        def _(sp):
            sp.dma_start(cT[:], A["cT"]).then_inc(d_c, 16)

            def cols(w, c0, nc_):
                return w.rearrange("(k p) c -> p k c", p=P)[:, :, c0:c0 + nc_]

            def reuse(b, name):
                sp.wait_ge(used[b], before(b, name))

            def ada_item(x):
                b = ADA_SLOT[x]
                if x >= 4:
                    reuse(b, f"ada{x}")
                sp.dma_start(part(b, 0, DT, 512), cols(A["w_ada"], x * 512, 512)).then_inc(wgt[b], 16)

            ada_item(0)
            sp.dma_start(xT[:], A["xT"]).then_inc(d_in, 16)
            sp.dma_start(vec[:], A["vec"]).then_inc(d_in, 16)
            for x in range(1, 4):
                ada_item(x)
            sp.dma_start(ptab[:], A["ptab"]).then_inc(d_ptab, 16)
            reuse(0, "in0")
            sp.dma_start(part(0, 0, DT, 672), cols(A["w_in"], 0, 672)).then_inc(wgt[0], 16)
            for j, (b, name) in enumerate(((1, "cb"), (2, "cc"), (3, "ch"), (0, "u"), (1, "v"))):
                reuse(b, name)
                sp.dma_start(part(b, 0, DT, 512), cols(A["w_in"], 672 + j * 512, 512)).then_inc(wgt[b], 16)
            ada_item(4)
            reuse(2, "mla")
            sp.dma_start(wuq, A["w_uq"]).then_inc(wgt[2], 16)
            sp.dma_start(wuk, A["w_uk"]).then_inc(wgt[2], 16)
            sp.dma_start(wuv, A["w_uv"]).then_inc(wgt[2], 16)
            for x in range(5, 12):
                ada_item(x)
            reuse(3, "late")
            sp.dma_start(wukT, A["w_ukT"]).then_inc(wgt[3], 16)
            sp.dma_start(wspT, A["wspT"]).then_inc(wgt[3], 16)
            sp.wait_ge(d_ptab, 16)

            def page(x):
                return sp.value_load(ptab[0:1, bass.ds(x, 1)], min_val=0, max_val=NPOOL - 1)

            with sp.Fori(0, NS // 2) as i:
                for b in range(2):
                    sp.wait_ge(used[b], i + before(b, "pages"))
                    for j in range(NPG):
                        sp.dma_start(pgT[b][:, j], A["poolT"][bass.ds(page(i * (2 * NPG) + (b * NPG + j)), 1)]
                                     .rearrange("o p c -> (o p) c")).then_inc(wgt[b], 16)
            def gates_w(x):
                b = (3, 0, 1, 0)[x]
                reuse(b, f"g{x}")
                for y in range(3):
                    sp.dma_start(part(b, y * DT * 256, DT, 256), cols(A["w_in"], GATE0 + y * D + x * 256, 256)
                                 ).then_inc(wgt[b], 16)

            gates_w(0)
            reuse(1, "rows1")
            for x in range(3 * NPG):
                sp.dma_start(ring[:, 1, x * KL:(x + 1) * KL], A["poolR"][bass.ds(page(3 * NPG + x), 1)]
                             .rearrange("o r c -> (o r) c")).then_inc(wgt[1], 16)
            def branch_w(hf):
                reuse(2 + hf, f"br{hf}")
                for y, x in enumerate("abc"):
                    sp.dma_start(part(2 + hf, y * CT * 512, CT, 512), A[f"w_br_{x}"].rearrange("(k p) c -> p k c", p=P)
                                 [:, :, hf * 512:(hf + 1) * 512]).then_inc(wgt[2 + hf], 16)

            def out_w(hf):
                reuse(2 + hf, f"out{hf}")
                sp.dma_start(part(2 + hf, 0, DT, 512), cols(A["w_out"], hf * 512, 512)).then_inc(wgt[2 + hf], 16)

            gates_w(1)
            branch_w(0)
            branch_w(1)
            gates_w(2)
            gates_w(3)
            out_w(0)
            def expert(b, g, u, d, wd):
                gu = part(b, 0, DT, 2 * FE)
                sp.dma_start(gu[:, :, 0:FE], g.rearrange("(k p) c -> p k c", p=P)).then_inc(wgt[b], 16)
                sp.dma_start(gu[:, :, FE:2 * FE], u.rearrange("(k p) c -> p k c", p=P)).then_inc(wgt[b], 16)
                sp.dma_start(part(b, 2 * DT * FE, FT, D), d.rearrange("(k p) c -> p k c", p=P)).then_inc(wd, 16)

            def one(w, e):
                return A[w][bass.ds(e, 1)].rearrange("o r c -> (o r) c")

            def routed(b, e):
                expert(b, *(A[w][e] if isinstance(e, int) else one(w, e) for w in ("w_e_gate", "w_e_up", "w_e_down")), wgd[b])

            reuse(1, "exp")
            routed(1, 1)
            reuse(0, "exp")
            routed(0, 0)
            out_w(1)
            reuse(2, "shared")
            expert(2, A["w_sh_gate"], A["w_sh_up"], A["w_sh_down"], wgt[2])
            for b in (3, 2):
                reuse(b, "exp")
                routed(b, b)
            with sp.Fori(1, E // 4) as i:
                for b0 in (0, 2):
                    for b in (b0, b0 + 1):
                        sp.wait_ge(used[b], i * 2 + (before(b, "exp") - 1))
                        gu = part(b, 0, DT, 2 * FE)
                        for u, w in enumerate(("w_e_gate", "w_e_up")):
                            sp.dma_start(gu[:, :, u * FE:(u + 1) * FE], one(w, i * 4 + b)
                                         .rearrange("(k p) c -> p k c", p=P)).then_inc(wgt[b], 16)
                    for b in (b0, b0 + 1):
                        sp.wait_ge(used[b], i * 2 + before(b, "exp"))
                        sp.dma_start(part(b, 2 * DT * FE, FT, D), one("w_e_down", i * 4 + b)
                                     .rearrange("(k p) c -> p k c", p=P)).then_inc(wgd[b], 16)
            sp.wait_ge(s["flag"], 1)
            with sp.If(sp.value_load(flag[0:1, 0:1], min_val=0, max_val=1) >= 1):
                with sp.Fori(0, E // 4) as i:
                    for b in range(4):
                        sp.wait_ge(used[b], i + (before(b, "exp") + 2 * (E // 4)))
                        routed(b, i * 4 + b)
            for j in range(4):
                sp.wait_ge(s["yout"], j + 1)
                sp.dma_start(O["yT"][:, 2 * j:2 * j + 2], hT[:, 2 * j:2 * j + 2]).then_inc(d_y, 16)
            sp.wait_ge(d_y, 16 * 4)
            sp.wait_ge(d_out, 16 * 4)
            sp.wait_ge(d_vout, 16 * 2)

        @block.gpsimd
        def _(pool):
            nc.gpsimd.memset(csig[:], 0.0).then_inc(s["consts"], 1)
            pool.dma_start(fold[:], A["fold"]).then_inc(d_fold, 16)
            nc.gpsimd.memset(lg[:, 2, :], 1.0).then_inc(s["consts"], 1)
            nc.gpsimd.memset(ones[:], 1.0).then_inc(s["consts"], 1)
            nc.gpsimd.memset(onecol[:], 0.0).then_inc(s["onecol"], 1)
            pool.wait_ge(s["onecol"], 1)
            nc.gpsimd.memset(onecol[:, H - 1:H], 1.0).then_inc(s["consts"], 1)
            nc.gpsimd.memset(qlat[:], 0.0).then_inc(s["consts"], 1)
            nc.gpsimd.memset(zp[:, :, 0:2], 0.0).then_inc(s["consts"], 1)
            for t, n in ((ident, "ident"), (swapm, "swapm"), (cosT, "cosT"), (sinT, "sinT"), (mask, "mask"),
                         (bsp, "bsp"),
                         (brou, "brou"), (wrou, "w_router"), (fold2, "fold2")):
                pool.dma_start(t[:], A[n]).then_inc(d_late, 16)
            pool.dma_start(zs[:, :, :, 0:2], A["stateT"]).then_inc(d_late, 16)
            pool.wait_ge(d_late, 16 * 10)
            pool.wait_ge(wgt[3], arrival(3, "late"))
            nc.gpsimd.affine_select(out=wspT, in_=wspT, compare_op=ALU.is_ge, fill=0.0, base=0,
                                    pattern=[[0, 8], [1, P]], channel_multiplier=-1).then_inc(s["wsp"], 1)
            pool.wait_ge(s["ckv"], 1)
            pool.dma_start(O["ckvT"], pT[:, T_KV:T_KV + KT_, :]).then_inc(d_out, 16)
            pool.wait_ge(s["krot"], 1)
            pool.dma_start(O["krT"], krT[NOPE:QK, 1, :]).then_inc(d_out, 16)
            pool.wait_ge(s["qrot"], 1)
            for t, n in ((toki[:], "toki"), (tri, "tri"), (iota, "iota")):
                pool.dma_start(t, A[n]).then_inc(d_tabs, 16)
            pool.wait_ge(s["z"], 1)
            pool.dma_start(O["convP"], zp[:, :, NP_:NP_ + 2]).then_inc(d_out, 16)
            pool.dma_start(O["convS"], zs[:, :, :, 1:3]).then_inc(d_out, 16)
            pool.wait_ge(s["vn"], 1)
            pool.dma_start(O["vnP"], vn[:, :, P:NP_]).then_inc(d_vout, 16)
            pool.dma_start(O["vnS"], vn[:, :, NP_:NT]).then_inc(d_vout, 16)
            for at in [*range(3 * NPG), *range(6 * NPG, 8 * NPG)]:
                if at == 0:
                    pool.wait_ge(used[0], before(0, "rows0"))
                if at == 6 * NPG:
                    pool.wait_ge(s["asc"], H)
                pg = pool.value_load(ptab[0:1, at:at + 1], min_val=0, max_val=NPOOL - 1)
                pool.dma_start(pgR[at // NPG][:, at % NPG, :], A["poolR"][bass.ds(pg, 1)]
                               .rearrange("o r c -> (o r) c")).then_inc(d_rows, 16)
            pool.wait_ge(s["smx"], 1)
            nc.gpsimd.partition_all_reduce(samx.rearrange("p q h -> p (q h)"), smx.rearrange("p q h -> p (q h)"), P, RMAX
                                           ).then_inc(s["allmx"], 1)
            pool.wait_ge(s["h2tok"], 6)
            for j, m in enumerate((P, P, NS)):
                pool.dma_start(h2rows[j * P:j * P + m, :], h2tok[0:m, j, :]).then_inc(d_tok, 16)
            pool.wait_ge(d_tok, 16 * 3)

            def gather(q, i):
                pool.wait_ge(s["idx"], turn(i, q + 1, 1))
                if q >= 2:
                    n = USE["X", q - 2, 1]
                    pool.wait_ge(full[n % 4], turn(i, n // 4 + 1, 3))
                pool.sem_inc(s["turn"], 1)
                nc.gpsimd.indirect_dma_start(
                    out=xs[:, q % 2, :], out_offset=None, in_=h2rows,
                    in_offset=bass.IndirectOffsetOnAxis(ap=idx[:, q % 2:q % 2 + 1], axis=0)).then_inc(d_x[q % 2], 16)

            gather(0, None)
            gather(1, None)
            pool.wait_ge(s["pmax"], 1)
            nc.gpsimd.partition_all_reduce(pall[:], pmax[:], P, RMAX).then_inc(s["pall"], 1)
            gather(2, None)
            with pool.Fori(0, 7) as i:
                for b in range(4):
                    gather(3 + b, i)
            gather(NPAIR - 1, None)

        @block.tensor
        def _(pe):
            def enter(n, i=None, per=0):
                b, k = bank(n)
                if i is not None:
                    pe.wait_ge(free[b], i * (per // 4) + k)
                elif k:
                    pe.wait_ge(free[b], k)
                return bk[b]

            def through(n, b):
                pe.wait_ge(full[n % 4], n // 4 + 1)
                pe.sem_inc(used[b], 1)

            def mm(out, lhsT, rhs, start, stop):
                return nc.tensor.matmul(out, lhsT, rhs, start=start, stop=stop)

            def sumsq(stage, src, nt, ready=None):
                n = BASE[stage]
                t = enter(n)
                for k in range(nt):
                    if ready:
                        pe.wait_ge(ready, k + 1)
                    last = mm(t[:, 0:NT], ones[:], src[:, k, :], k == 0, k == nt - 1)
                last.then_inc(full[n % 4], 1)

            def ada_item(x):
                b = ADA_SLOT[x]
                n = BASE["ada0" if x == 0 else "ada1"] + max(x - 1, 0) if x < 4 else BASE[f"ada{x - x % 2}"] + x % 2
                t = enter(n)
                pe.wait_ge(wgt[b], arrival(b, f"ada{x}"))
                w = part(b, 0, DT, 512)
                for o in range(2):
                    for j in range(4):
                        last = mm(t[32 * j:32 * j + 32, :], csig[:, 2 * j + o, :], w[:, 2 * j + o, :], o == 0, o == 1)
                last.then_inc(full[n % 4], 1)
                through(n, b)
                return n

            def ada_fold(x, n):
                pe.wait_ge(free[n % 4], n // 4 + 1)
                for m in range(4):
                    last = mm(pA[:, (4 * x + m) * NC:(4 * x + m + 1) * NC], adb[:, x % 2, m * P:(m + 1) * P], fold[:],
                              True, True)
                last.then_inc(s["ada_mm"], 1)

            def ada_items(xs_):
                before_ = None
                for x in xs_:
                    n = ada_item(x)
                    if before_:
                        ada_fold(*before_)
                    before_ = (x, n)
                ada_fold(*before_)

            pe.wait_ge(s["csilu"], 1)
            pe.wait_ge(d_fold, 16)
            first = ada_item(0)
            pe.wait_ge(s["consts"], 6)
            pe.wait_ge(s["sq1"], 1)
            sumsq("norm1", sq, DT)
            ada_fold(0, first)
            ada_items(range(1, 4))

            pe.wait_ge(s["h1"], 2)
            pe.wait_ge(wgt[0], arrival(0, "in0"))
            w = part(0, 0, DT, 672)
            for m in range(6):
                n = BASE["in0"] + m
                t = enter(n)
                for k in range(DT):
                    if m < 5:
                        last = mm(t[:, 0:NT], w[:, k, m * P:(m + 1) * P], hT[:, k, :], k == 0, k == DT - 1)
                    else:
                        last = mm(t[NOPE:QK, 0:NT], w[:, k, 640:672], hT[:, k, :], k == 0, k == DT - 1)
                last.then_inc(full[n % 4], 1)
            through(n, 0)
            for c, (b, name) in enumerate(((1, "cb"), (2, "cc"), (3, "ch"), (0, "u"), (1, "v"))):
                pe.wait_ge(wgt[b], arrival(b, name))
                w = part(b, 0, DT, 512)
                for m in range(4):
                    n = BASE["in1"] + 4 * c + m
                    t = enter(n)
                    for k in range(DT):
                        last = mm(t[:, 0:NT], w[:, k, m * P:(m + 1) * P], hT[:, k, :], k == 0, k == DT - 1)
                    last.then_inc(full[n % 4], 1)
                through(n, b)

            pe.wait_ge(s["sqq"], 1)
            sumsq("cqn", sq, QT)
            sumsq("kvn", sq[:, QT:QT + KT_, :], KT_)
            pe.wait_ge(d_late, 16 * 10)
            n = BASE["krs"]
            t = enter(n)
            mm(t[NOPE:QK, 0:NT], swapm[NOPE:QK, :], krT[NOPE:QK, 0, :], True, True).then_inc(full[n % 4], 1)
            ada_items((4, 5))
            pe.wait_ge(s["cqn"], 1)
            pe.wait_ge(wgt[2], arrival(2, "mla"))
            for h in range(H):
                n = BASE["q"] + h
                t = enter(n)
                for k in range(QT):
                    last = mm(t[0:QK, 0:NT], wuq[:, k, h * QK:(h + 1) * QK], pT[:, T_Q + k, :], k == 0, k == QT - 1)
                last.then_inc(full[n % 4], 1)
            ada_items((6, 7))
            pe.wait_ge(s["ckv"], 1)
            for h in range(H):
                n = BASE["k"] + h
                t = enter(n)
                for k in range(KT_):
                    last = mm(t[0:NOPE, 0:NT], wuk[:, k, h * NOPE:(h + 1) * NOPE], pT[:, T_KV + k, :],
                              k == 0, k == KT_ - 1)
                last.then_inc(full[n % 4], 1)
            ada_items((8, 9))
            ada_items((10, 11))
            for b in range(2):
                n = BASE["v"] + b
                t = enter(n)
                for k in range(KT_):
                    last = mm(t[:], pT[:, T_KV + k, b * P:(b + 1) * P], wuv[:, k, :], k == 0, k == KT_ - 1)
                last.then_inc(full[n % 4], 1)
            for h in range(H):
                n = BASE["qswap"] + h
                t = enter(n)
                pe.wait_ge(s["qcopy"], h + 1)
                mm(t[NOPE:QK, 0:NT], swapm[NOPE:QK, :], qT[NOPE:QK, h, :], True, True).then_inc(full[n % 4], 1)

            def keys(q, js):
                b = q % 2
                pe.wait_ge(wgt[b], (q // 2) * (16 * NPG) + arrival(b, "pages"))
                for j in js:
                    n = BASE[f"know{q}"] + j if q or j < 4 else BASE["know0b"] + j - 4
                    t = enter(n)
                    for k in range(KT_):
                        last = mm(t[:], pgT[b][:, j, k * P:(k + 1) * P], wuk[:, k, :], k == 0, k == KT_ - 1)
                    last.then_inc(full[n % 4], 1)
                if q and j == NPG - 1:
                    pe.wait_ge(s["krd"], q + 1)
                    through(n, b)

            def head_sums(stage, src):
                n = BASE[stage]
                t = enter(n)
                for h in range(H):
                    last = mm(t[0:H, 0:NT], onecol[0:QK, H - 1 - h:2 * H - 1 - h], src[0:QK, h, :], h == 0, h == H - 1)
                last.then_inc(full[n % 4], 1)

            def head_rows(stage, x):
                pe.wait_ge(s["rsh"], x + 1)
                for h in range(H):
                    n = BASE[stage] + h
                    t = enter(n)
                    mm(t[0:QK, 0:NT], ident[0:H, h:h + 1].broadcast_to([H, QK]), hinv[:, x, :], True, True
                       ).then_inc(full[n % 4], 1)

            pe.wait_ge(s["sqh"], 1)
            head_sums("ksum", sq)
            keys(0, range(0, 4))
            head_rows("kinv", 0)
            pe.wait_ge(s["sqh"], 2)
            head_sums("qsum", pT[:, T_CC:T_CC + H, :])
            keys(0, range(4, NPG))
            head_rows("qinv", 1)
            pe.wait_ge(s["prodself"], 1)
            n = BASE["self"]
            t = enter(n)
            mm(t[:, 0:H * NS], ones[0:QK, :], sq[0:QK, 0, 0:H * NS], True, True).then_inc(full[n % 4], 1)
            pe.wait_ge(s["qsg"], 1)
            pe.wait_ge(wgt[3], arrival(3, "late"))
            n = BASE["qlat"]
            t = enter(n)
            for k in range(KT_):
                for h in range(H):
                    last = mm(t[:, (k * H + h) * NS:(k * H + h + 1) * NS], wukT[:, h, k * P:(k + 1) * P],
                              qsg[0:NOPE, h, :], True, True)
            last.then_inc(full[n % 4], 1)
            pe.wait_ge(s["qlat"], 2)
            pe.wait_ge(s["ada"], 2)
            pe.wait_ge(s["kn"], 1)
            pe.wait_ge(s["vtok"], 2)

            def scores(q):
                b = q % 2
                n = BASE[f"ksc{q}"]
                t = enter(n)
                pe.wait_ge(wgt[b], (q // 2) * (16 * NPG) + arrival(b, "pages"))
                for k in range(KT_):
                    for g in range(2):
                        mm(t[32 * (2 * k + g):32 * (2 * k + g) + 32, :], qlat[:, k, q, :],
                           pgT[b][:, 4 * g:4 * g + 4, k * P:(k + 1) * P], True, k == 1)
                for g in range(2):
                    last = mm(t[32 * g:32 * g + 32, :], qrp[:, q, :], pgT[b][:, 4 * g:4 * g + 4, 2 * P:3 * P], False, True)
                last.then_inc(full[n % 4], 1)

            def scores_fold(q):
                n = BASE[f"ksc{q}"]
                pe.wait_ge(free[n % 4], n // 4 + 1)
                out = pA[:, q * NPG * H:(q + 1) * NPG * H].rearrange("p (g j h) -> p g j h", g=2, j=4)
                for j in range(4):
                    last = mm(out[:, :, j, :], scr[:, j * P:(j + 1) * P], fold2[:].rearrange("p (g h) -> p g h", g=2),
                              True, True)
                last.then_inc(s["fold"], 1)

            def a_scores(h):
                if h:
                    pe.wait_ge(s["am"], h)
                mm(pB[:, 0:P], qT[0:QK, h, 0:P], kT[0:QK, h, 0:P], True, True)
                mm(pB[:, P:3 * P], qT[0:QK, h, P:NP_], kT[0:QK, h, 0:NP_], True, True).then_inc(s["asc"], 1)

            def a_transpose(h):
                pe.wait_ge(s["anorm"], h + 1)
                if h:
                    pe.wait_ge(s["aPT"], h)
                for j in range(3):
                    last = nc.tensor.transpose(pC[:, j * P:(j + 1) * P], aP[:, j * P:(j + 1) * P], ident[:])
                last.then_inc(s["atr"], 1)

            def a_values(h):
                o = 64 * (h % 2)
                pe.wait_ge(s["aPT"], h + 1)
                if h:
                    pe.wait_ge(s["oa"], h)
                v = vtok[:, :, h * NOPE:(h + 1) * NOPE]
                mm(pD[o:o + 64, 0:P], v[:, 0, :], aPT[:, 0:P], True, True)
                mm(pD[o:o + 64, P:NP_], v[:, 0, :], aPT[:, P:2 * P], True, False)
                mm(pD[o:o + 64, P:NP_], v[:, 1, :], aPT[:, 2 * P:3 * P], False, True).then_inc(s["aout"], 1)

            def gmlp(step_):
                n = BASE[step_]
                if step_ == "vmean":
                    t = enter(n)
                    for k in range(CT):
                        last = mm(t[:, 0:NT], ones[:], pT[:, T_V + k, :], k == 0, k == CT - 1)
                    last.then_inc(full[n % 4], 1)
                elif step_ == "vvar":
                    pe.wait_ge(s["sqv"], 1)
                    sumsq("vvar", vsq, CT)
                elif step_ == "vtr":
                    pe.wait_ge(s["vn"], 1)
                    for b in range(2):
                        n = BASE["vtr"] + b
                        t = enter(n)
                        for k in range(CT):
                            last = nc.tensor.transpose(t[:, k * P:(k + 1) * P], vn[:, k, b * P:(b + 1) * P], ident[:])
                        last.then_inc(full[n % 4], 1)
                else:
                    pe.wait_ge(s["wsp"], 1)
                    pe.wait_ge(s["vntok"], 2)
                    for c in range(CT):
                        n = BASE["spat"] + c
                        t = enter(n)
                        for o in range(2):
                            for b in range(2):
                                g = 2 * c + o
                                last = mm(t[64 * o:64 * o + 64, b * P:(b + 1) * P], vntok[:, b, g * 64:(g + 1) * 64],
                                          wspT[:, g, :], True, True)
                        last.then_inc(full[n % 4], 1)
                    through(n, 3)

            scores(0)
            scores_fold(0)
            pe.wait_ge(s["krd"], 1)
            pe.sem_inc(used[0], 1)
            for q in range(NS):
                a_scores(q)
                if q + 1 < NS:
                    scores(q + 1)
                    keys(q + 1, range(0, 4))
                    scores_fold(q + 1)
                a_transpose(q)
                if q + 1 < NS:
                    keys(q + 1, range(4, NPG))
                a_values(q)
                for step_ in {0: ("vmean",), 1: ("vvar",), 2: ("vtr",), 3: ("spat",)}.get(q, ()):
                    gmlp(step_)

            def gates(m):
                x = m // 2
                b = (3, 0, 1, 0)[x]
                pe.wait_ge(wgt[b], arrival(b, f"g{x}"))
                for y in range(3):
                    n = BASE[f"bg{m}"] + y
                    t = enter(n)
                    for k in range(DT):
                        last = mm(t[:, 0:NT], part(b, y * DT * 256, DT, 256)[:, k, (m % 2) * P:(m % 2 + 1) * P],
                                  hT[:, k, :], k == 0, k == DT - 1)
                    last.then_inc(full[n % 4], 1)
                if m % 2:
                    through(n, b)

            gates(0)
            gates(1)
            pe.wait_ge(s["psumd"], 1)
            mm(pB[:, 0:NS * H], ones[:], ssum.rearrange("p q h -> p (q h)"), True, True).then_inc(s["tot_mm"], 1)
            pe.wait_ge(s["oa"], H)
            pe.wait_ge(d_rows, 16 * 5 * NPG)
            pe.wait_ge(wgt[1], arrival(1, "rows1"))
            for g in range(2):
                for j in range(NPG):
                    for o in range(4):
                        q = 4 * g + o
                        last = mm([pC, pD][g][32 * o:32 * o + H, 0:KL], sp_[:, q, j, :], pgR[q][:, j, :],
                                  j == 0, j == NPG - 1)
                last.then_inc(s["pv"], 1)
            pe.wait_ge(s["pv"], 2)
            for b in (0, 1):
                pe.sem_inc(used[b], 1)
            for g in range(2):
                n = BASE["otr"] + g
                t = enter(n)
                pe.wait_ge(s["orow"], 4 * g + 4)
                for k in range(KT_):
                    last = nc.tensor.transpose(t[:, k * P:(k + 1) * P], orow[:, g, k * P:(k + 1) * P], ident[:])
                last.then_inc(full[n % 4], 1)

            pe.wait_ge(s["olat"], 2)
            for c in range(CT):
                n = BASE["uvs"] + c
                t = enter(n)
                for o in range(2):
                    h = 2 * c + o
                    for k in range(KT_):
                        last = mm(t[o * 64:(o + 1) * 64, 0:NS], wuv[:, k, h * NOPE:(h + 1) * NOPE], olat[:, k, h, :],
                                  k == 0, k == KT_ - 1)
                last.then_inc(full[n % 4], 1)
            through(n, 2)

            pe.wait_ge(s["conv"], 1)
            pe.wait_ge(s["sg"], 1)
            src = [oaT[:, :, :], pT[:, T_CB:T_CB + CT, :], pT[:, T_U:T_U + CT, :]]
            for m in range(DT):
                if m + 2 < DT:
                    gates(m + 2)
                if m == 0:
                    pe.wait_ge(s["oa_s"], CT)
                hf = m // 4
                if m % 4 == 0:
                    pe.wait_ge(wgt[2 + hf], arrival(2 + hf, f"br{hf}"))
                for b in range(3):
                    n = BASE[f"bo{m}"] + b
                    t = enter(n)
                    for k in range(CT):
                        last = mm(t[:, 0:NT], part(2 + hf, b * CT * 512, CT, 512)[:, k, (m % 4) * P:(m % 4 + 1) * P],
                                  src[b][:, k, :], k == 0, k == CT - 1)
                    last.then_inc(full[n % 4], 1)
                if m % 4 == 3:
                    through(n, 2 + hf)
            pe.wait_ge(s["merged"], DT)
            for m in range(DT):
                b = 2 + m // 4
                if m % 4 == 0:
                    pe.wait_ge(wgt[b], arrival(b, f"out{m // 4}"))
                n = BASE["out"] + m
                t = enter(n)
                for k in range(DT):
                    last = mm(t[:, 0:NT], part(b, 0, DT, 512)[:, k, (m % 4) * P:(m % 4 + 1) * P], mg[:, k, :],
                              k == 0, k == DT - 1)
                last.then_inc(full[n % 4], 1)
                if m % 4 == 3:
                    through(n, b)
            sumsq("norm2", sq, DT, s["sq2"])
            pe.wait_ge(s["h2"], 2)
            for j, m in enumerate((P, P, NS)):
                n = BASE["rout"] + j
                t = enter(n)
                for k in range(DT):
                    last = mm(t[0:m, 0:E], hT[:, k, j * P:j * P + m], wrou[:, k, :], k == 0, k == DT - 1)
                last.then_inc(full[n % 4], 1)
            for j, m in enumerate((P, P, NS)):
                for hf in range(2):
                    n = BASE["h2tr"] + 2 * j + hf
                    t = enter(n)
                    for k in range(4):
                        last = nc.tensor.transpose(t[0:m, k * P:(k + 1) * P], hT[:, 4 * hf + k, j * P:j * P + m], ident[:])
                    last.then_inc(full[n % 4], 1)

            def dense_up(b, n0, i):
                w = part(b, 0, DT, 2 * FE)
                for f in range(FT):
                    for u in range(2):
                        n = n0 + 2 * f + u
                        t = enter(n, i, 48)
                        for k in range(DT):
                            c0 = u * FE + f * P
                            last = mm(t[:, 0:NT], w[:, k, c0:c0 + P], hT[:, k, :], k == 0, k == DT - 1)
                        last.then_inc(full[n % 4], 1)

            def dense_down(b, n0, i, par):
                w = part(b, 2 * DT * FE, FT, D)
                for m in range(DT):
                    n = n0 + m
                    t = enter(n, i, 48)
                    for f in range(FT):
                        last = mm(t[:, 0:NT], w[:, f, m * P:(m + 1) * P], actg[:, par, f, :], f == 0, f == FT - 1)
                    last.then_inc(full[n % 4], 1)
                if i is None:
                    pe.wait_ge(full[n % 4], n // 4 + 1)
                else:
                    pe.wait_ge(full[n % 4], i * 12 + (n // 4 + 1))
                pe.sem_inc(used[b], 1)

            pe.wait_ge(wgt[2], arrival(2, "shared"))
            dense_up(2, BASE["shgu"], None)
            pe.wait_ge(s["gates"], 1)
            pe.wait_ge(d_tabs, 16 * 3)
            n = BASE["pos"]
            t = enter(n)
            for j, m in enumerate((P, P, NS)):
                for i in range(j + 1):
                    kk = (P, P, NS)[i]
                    last = mm(t[0:m, j * E:(j + 1) * E], (ones if i < j else tri)[0:kk, 0:m], ch[0:kk, i, :],
                              i == 0, i == j)
            last.then_inc(full[n % 4], 1)

            def shared_down(ms):
                w = part(2, 2 * DT * FE, FT, D)
                for m in ms:
                    n = BASE[f"shdn{m - m % 4}"] + m % 4
                    t = enter(n)
                    for f in range(FT):
                        last = mm(t[:, 0:NT], w[:, f, m * P:(m + 1) * P], actg[:, 1, f, :], f == 0, f == FT - 1)
                    last.then_inc(full[n % 4], 1)
                if m == DT - 1:
                    through(n, 2)

            def use(n, i):
                pe.wait_ge(free[n % 4], turn(i, n // 4, 3))
                return bk[n % 4]

            def emptied(n, i):
                pe.wait_ge(free[n % 4], turn(i, n // 4 + 1, 3))

            def gates_tr(q, i):
                n = USE["G", q]
                t = use(n, i)
                pe.wait_ge(s["gt"], turn(i, q + 1, 1))
                for j, m in enumerate((P, P, NS)):
                    last = nc.tensor.transpose(t[:, j * P:j * P + m], gtm[0:m, j, :], ident[0:m, 0:m])
                last.then_inc(full[n % 4], 1)

            def tokens_tr(q, i):
                pe.wait_ge(d_x[q % 2], turn(i, 16 * (q // 2 + 1), 8))
                for hf in range(2):
                    n = USE["X", q, hf]
                    t = use(n, i)
                    for k in range(4):
                        c0 = (4 * hf + k) * P
                        last = nc.tensor.transpose(t[:, k * P:(k + 1) * P], xs[:, q % 2, c0:c0 + P], ident[:])
                    last.then_inc(full[n % 4], 1)

            def up(p, i):
                for hf in range(2):
                    emptied(USE["X", p, hf], i)
                sl = [2 * (p % 2) + x for x in range(2)]
                for b in sl:
                    pe.wait_ge(wgt[b], turn(i, arrival(b, "exp") + 32 * (p // 2), 16))
                for k in range(DT):
                    for x in range(2):
                        last = mm(pA[CAP * x:CAP * (x + 1), :], xTs[:, p % 2, k, CAP * x:CAP * (x + 1)],
                                  part(sl[x], 0, DT, 2 * FE)[:, k, :], k == 0, k == DT - 1)
                last.then_inc(s["gu"], 1)

            def act_tr(p, i):
                n = USE["T", p]
                t = use(n, i)
                pe.wait_ge(s["act_s"], turn(i, p + 1, 1))
                for f in range(FT):
                    last = nc.tensor.transpose(t[:, f * P:(f + 1) * P], act_s[:, f * P:(f + 1) * P], ident[:])
                last.then_inc(full[n % 4], 1)

            def down(p, i):
                emptied(USE["T", p], i)
                sl = [2 * (p % 2) + x for x in range(2)]
                for b in sl:
                    pe.wait_ge(wgd[b], turn(i, 16 * (p // 2 + 1), 8))
                for hf in range(2):
                    for f in range(FT):
                        for x in range(2):
                            last = mm([pB, pC][hf][CAP * x:CAP * (x + 1), :], actT[:, f, CAP * x:CAP * (x + 1)],
                                      part(sl[x], 2 * DT * FE, FT, D)[:, f, hf * 512:(hf + 1) * 512],
                                      f == 0, f == FT - 1)
                    last.then_inc(s[f"dn{hf}"], 1)
                pe.wait_ge(s["dn1"], turn(i, p + 1, 1))
                for b in sl:
                    pe.sem_inc(used[b], 1)

            def spread(q, i, ms):
                if ms[0] == 0:
                    emptied(USE["G", q], i)
                    pe.wait_ge(s["y0"], turn(i, q + 1, 1))
                    pe.wait_ge(s["y1"], turn(i, q + 1, 1))
                for m in ms:
                    n = USE["C", q, m]
                    t = use(n, i)
                    mm(t[:, 0:NT], yrow[:, m * P:(m + 1) * P], gm[q % 4], True, True).then_inc(full[n % 4], 1)

            def pair(p, i=None):
                if p + 2 < NPAIR:
                    gates_tr(p + 2, i)
                if p + 1 < NPAIR:
                    tokens_tr(p + 1, i)
                up(p, i)
                if p:
                    spread(p - 1, i, range(4))
                pe.wait_ge(s["gu"], turn(i, p + 1, 1))
                for x in range(2):
                    pe.sem_inc(used[2 * (p % 2) + x], 1)
                act_tr(p, i)
                if p:
                    spread(p - 1, i, range(4, 8))
                down(p, i)

            gates_tr(0, None)
            pe.wait_ge(s["act"], 2)
            shared_down(range(0, 4))
            gates_tr(1, None)
            shared_down(range(4, 8))
            tokens_tr(0, None)
            pair(0)
            with pe.Fori(0, 7) as i:
                for b in range(4):
                    pair(1 + b, i)
            for p in range(29, NPAIR):
                pair(p)
            spread(NPAIR - 1, None, range(8))

            pe.wait_ge(s["flag"], 1)
            with pe.If(pe.value_load(flag[0:1, 0:1], min_val=0, max_val=1) >= 1):
                pe.wait_ge(s["fgates"], 1)
                n = BASE["fgates"]
                t = enter(n)
                for j, m in enumerate((P, P, NS)):
                    last = nc.tensor.transpose(t[0:E, j * P:j * P + m], ch[0:m, j, :], ident[0:m, 0:m])
                last.then_inc(full[n % 4], 1)
                for n in range(BASE["fgates"] + 1, BASE["fexp"]):
                    enter(n)
                    mm(bk[n % 4][:, 0:NC], ones[:], csig[:, 0, 0:NC], True, True).then_inc(full[n % 4], 1)
                with pe.Fori(0, E // 4) as i:
                    for b in range(4):
                        par = b % 2
                        n0 = BASE["fexp"] + 12 * b
                        pe.wait_ge(wgt[b], i * 32 + (arrival(b, "exp") + 32 * (E // 4)))
                        pe.wait_ge(wgd[b], i * 16 + 16 * (E // 4 + 1))
                        dense_up(b, n0, i)
                        pe.wait_ge(s["gsel"], i * 4 + (b + 1))
                        mm([pC, pD][par][:, 0:NT], ones[0:E, :], gsel[:, par, :], True, True).then_inc(s["gbc"], 1)
                        pe.wait_ge(s["act"], i * 8 + (2 * b + 4))
                        dense_down(b, n0 + 4, i, par)

        @block.scalar
        def _(act):
            chain = [0]

            def link(ins):
                chain[0] += 1
                ins.then_inc(c_act, 1)
                act.wait_ge(c_act, chain[0])

            def fulls(n):
                b, k = bank(n)
                act.wait_ge(full[b], k + 1)
                return bk[b]

            act.wait_ge(d_c, 16)
            act.wait_ge(s["consts"], 1)
            nc.scalar.activation(csig[:, :, 0:NC], cT[:], ACT.Sigmoid).then_inc(s["csig"], 1)
            act.wait_ge(d_in, 16 * 2)
            nc.scalar.activation(sq[:], xT[:], ACT.Square).then_inc(s["sq1"], 1)

            def ada_rows(xs_):
                for x in xs_:
                    n = BASE["ada0" if x == 0 else "ada1"] + max(x - 1, 0) if x < 4 else BASE[f"ada{x - x % 2}"] + x % 2
                    t = fulls(n)
                    if x >= 2:
                        act.wait_ge(s["ada_mm"], x - 1)
                    nc.scalar.activation(adb[:, x % 2, :], t[:], ACT.Copy).then_inc(free[n % 4], 1)

            ada_rows(range(1))
            act.wait_ge(s["var1"], 1)
            nc.scalar.activation(rstd[:], rstd[:], ACT.Sqrt).then_inc(s["rs1"], 1)
            ada_rows(range(1, 4))
            for m in range(5):
                n = BASE["in0"] + m
                t = fulls(n)
                nc.scalar.activation(pT[:, m, :], t[:, 0:NT], ACT.Copy).then_inc(free[n % 4], 1)
            n = BASE["in0"] + 5
            t = fulls(n)
            nc.scalar.activation(krT[NOPE:QK, 0, :], t[NOPE:QK, 0:NT], ACT.Copy).then_inc(free[n % 4], 1)
            for b in range(4):
                act.wait_ge(free[b], (BASE["in0"] + 5 - b) // 4 + 1)
            act.sem_inc(s["krin"], 1)
            act.wait_ge(s["var1"], 1)
            nc.scalar.activation(sq[:, 0:QT + KT_, :], pT[:, T_Q:T_Q + QT + KT_, :], ACT.Square).then_inc(s["sqq"], 1)
            for j in range(20):
                n = BASE["in1"] + j
                t = fulls(n)
                nc.scalar.activation(pT[:, T_CB + j, :], t[:, 0:NT], ACT.Copy).then_inc(free[n % 4], 1)
            for b in range(4):
                act.wait_ge(free[b], (n - b) // 4 + 1)
            act.sem_inc(s["in_done"], 1)
            act.wait_ge(s["varq"], 1)
            link(nc.scalar.activation(rstd[:], rstd[:], ACT.Sqrt))
            act.sem_inc(s["rsq"], 1)
            act.wait_ge(s["varkv"], 1)
            nc.scalar.activation(rstd[:], rstd[:], ACT.Sqrt).then_inc(s["rskv"], 1)
            ada_rows((4, 5))
            for h in range(H):
                n = BASE["q"] + h
                t = fulls(n)
                nc.scalar.activation(qT[0:QK, h, :], t[0:QK, 0:NT], ACT.Copy).then_inc(s["qcopy"], 1)
                act.wait_ge(s["qcopy"], h + 1)
                act.sem_inc(free[n % 4], 1)
            ada_rows((6, 7))
            for h in range(H):
                n = BASE["k"] + h
                t = fulls(n)
                nc.scalar.activation(kT[0:NOPE, h, :], t[0:NOPE, 0:NT], ACT.Copy).then_inc(free[n % 4], 1)
            for b in range(4):
                act.wait_ge(free[b], (n - b) // 4 + 1)
            ada_rows((8, 9))
            act.wait_ge(s["kfull"], 1)
            act.wait_ge(s["ckv"], 1)
            nc.scalar.activation(sq[0:QK, :, :], kT[0:QK, :, :], ACT.Square).then_inc(s["sqh"], 1)
            ada_rows((10, 11))
            for b in range(2):
                n = BASE["v"] + b
                t = fulls(n)
                nc.scalar.activation(vtok[:, b, :], t[:], ACT.Copy).then_inc(s["vtok"], 1)
                act.wait_ge(s["vtok"], b + 1)
                act.sem_inc(free[n % 4], 1)
            def squares(q, js):
                for j in js:
                    n = BASE[f"know{q}"] + j if q or j < 4 else BASE["know0b"] + j - 4
                    t = fulls(n)
                    if NPG * q + j >= 2:
                        act.wait_ge(s["ksq_used"], NPG * q + j - 1)
                    if NPG * q + j == 0:
                        act.wait_ge(s["ada_mm"], 12)
                    nc.scalar.activation(ksq[:, j % 2, :], t[:], ACT.Square).then_inc(s["ksq"], 1)
                    act.wait_ge(s["ksq"], NPG * q + j + 1)
                    act.sem_inc(free[n % 4], 1)

            act.wait_ge(s["varh"], 1)
            nc.scalar.activation(hinv[:, 0, :], hinv[:, 0, :], ACT.Sqrt).then_inc(s["rsh"], 1)
            act.wait_ge(s["qrot"], 1)
            nc.scalar.activation(pT[0:QK, T_CC:T_CC + H, :], qT[0:QK, :, :], ACT.Square).then_inc(s["sqh"], 1)
            squares(0, range(4))
            act.wait_ge(s["varh"], 2)
            nc.scalar.activation(hinv[:, 1, :], hinv[:, 1, :], ACT.Sqrt).then_inc(s["rsh"], 1)
            squares(0, range(4, NPG))

            def score_rows(q):
                n = BASE[f"ksc{q}"]
                t = fulls(n)
                if q:
                    act.wait_ge(s["fold"], q)
                nc.scalar.activation(scr, t[:], ACT.Copy).then_inc(free[n % 4], 1)

            score_rows(0)
            for q in range(NS):
                h = q
                if q + 1 < NS:
                    score_rows(q + 1)
                    squares(q + 1, (0, 1))
                act.wait_ge(s["amx"], h + 1)
                nc.scalar.activation(aP[:, 0:P], am[:, 0:P], ACT.Exp, bias=amx[:, 0:1], accum_out=asum[:, 0:1])
                nc.scalar.activation(aP[:, P:3 * P], am[:, P:3 * P], ACT.Exp, bias=amx[:, 1:2],
                                     accum_out=asum[:, 1:2]).then_inc(s["aexp"], 1)
                if q + 1 < NS:
                    squares(q + 1, (2, 3))
                act.wait_ge(s["atr"], h + 1)
                if h:
                    act.wait_ge(s["aout"], h)
                nc.scalar.activation(aPT, pC[:, 0:3 * P], ACT.Copy).then_inc(s["aPT"], 1)
                if q + 1 < NS:
                    squares(q + 1, (4, 5, 6, 7))
                act.wait_ge(s["aout"], h + 1)
                o = 64 * (h % 2)
                nc.scalar.activation(oaT[o:o + 64, h // 2, 0:NP_], pD[o:o + 64, 0:NP_], ACT.Copy).then_inc(s["oa"], 1)
                if q == 0:
                    act.wait_ge(s["vcen"], 1)
                    nc.scalar.activation(vsq, vn, ACT.Square).then_inc(s["sqv"], 1)
                if q == 1:
                    act.wait_ge(s["varv"], 1)
                    nc.scalar.activation(rstd[:], rstd[:], ACT.Sqrt).then_inc(s["rsv"], 1)
                if q == 2:
                    for b in range(2):
                        n = BASE["vtr"] + b
                        t = fulls(n)
                        nc.scalar.activation(vntok[:, b, :], t[:], ACT.Copy).then_inc(s["vntok"], 1)
                        act.wait_ge(s["vntok"], b + 1)
                        act.sem_inc(free[n % 4], 1)
            act.wait_ge(s["kss"], 1)
            nc.scalar.activation(kss, kss, ACT.Sqrt).then_inc(s["rstds"], 1)

            def gate_sigmoids(m):
                for b in range(3):
                    n = BASE[f"bg{m}"] + b
                    t = fulls(n)
                    if m >= 3:
                        act.wait_ge(s["merged"], m - 2)
                    nc.scalar.activation(gs[m % 3][:, b, :], t[:, 0:NT], ACT.Sigmoid).then_inc(s["gsig"], 1)
                    act.wait_ge(s["gsig"], 3 * m + b + 1)
                    act.sem_inc(free[n % 4], 1)

            act.wait_ge(s["sg"], 1)
            gate_sigmoids(0)
            act.wait_ge(s["ssub"], 1)
            nc.scalar.activation(sp_, ssc, ACT.Exp).then_inc(s["pexp"], 1)
            nc.scalar.activation(eself, ssub, ACT.Exp).then_inc(s["pexp"], 1)
            gate_sigmoids(1)
            for g in range(2):
                act.wait_ge(s["pv"], g + 1)
                for o in range(4):
                    nc.scalar.activation(orow[32 * o:32 * o + H, g, :], [pC, pD][g][32 * o:32 * o + H, 0:KL], ACT.Copy
                                         ).then_inc(s["orow"], 1)
            for c in range(CT):
                n = BASE["uvs"] + c
                t = fulls(n)
                nc.scalar.activation(oaT[:, c, NP_:NT], t[:, 0:NS], ACT.Copy).then_inc(s["oa_s"], 1)
                act.wait_ge(s["oa_s"], c + 1)
                act.sem_inc(free[n % 4], 1)
            act.wait_ge(s["olat"], 2)
            for m in range(2, DT):
                gate_sigmoids(m)
            for m in range(DT):
                act.wait_ge(s["x1"], m + 1)
                nc.scalar.activation(sq[:, m, :], xT[:, m, :], ACT.Square).then_inc(s["sq2"], 1)
            act.wait_ge(s["var2"], 1)
            nc.scalar.activation(rstd[:], rstd[:], ACT.Sqrt).then_inc(s["rs2"], 1)
            for j, m in enumerate((P, P, NS)):
                n = BASE["rout"] + j
                t = fulls(n)
                nc.scalar.activation(lg[0:m, j, :], t[0:m, 0:E], ACT.Sigmoid).then_inc(s["lsig"], 1)
                act.wait_ge(s["lsig"], j + 1)
                act.sem_inc(free[n % 4], 1)
            for j, m in enumerate((P, P, NS)):
                for hf in range(2):
                    n = BASE["h2tr"] + 2 * j + hf
                    t = fulls(n)
                    nc.scalar.activation(h2tok[0:m, j, hf * 512:(hf + 1) * 512], t[0:m, :], ACT.Copy
                                         ).then_inc(s["h2tok"], 1)
                    act.wait_ge(s["h2tok"], 2 * j + hf + 1)
                    act.sem_inc(free[n % 4], 1)

            def silu(n0, par, i, done):
                for f in range(FT):
                    n = n0 + 2 * f
                    b, k = bank(n)
                    if i is None:
                        act.wait_ge(full[b], k + 1)
                    else:
                        act.wait_ge(full[b], i * 12 + (k + 1))
                        act.wait_ge(s["act"], done - 1)
                    nc.scalar.activation(acts[:, par, f, :], bk[b][:, 0:NT], ACT.Silu).then_inc(s["silu"], 1)
                    act.wait_ge(s["silu"], done + (f + 1))
                    act.sem_inc(free[b], 1)

            act.wait_ge(d_vout, 16 * 2)
            silu(BASE["shgu"], 1, None, 0)

            def empty(n, i, dst, rows_):
                act.wait_ge(full[n % 4], turn(i, n // 4 + 1, 3))
                nc.scalar.activation(dst, rows_, ACT.Copy).then_inc(free[n % 4], 1)

            def gates_e(q, i):
                n = USE["G", q]
                empty(n, i, gm[q % 4], bk[n % 4][:, 0:NT])

            def tokens_e(q, i):
                for hf in range(2):
                    n = USE["X", q, hf]
                    empty(n, i, xTs[:, q % 2, 4 * hf:4 * hf + 4, :], bk[n % 4][:].rearrange("p (k c) -> p k c", k=4))

            def pair(p, i=None):
                if p + 2 < NPAIR:
                    gates_e(p + 2, i)
                if p + 1 < NPAIR:
                    tokens_e(p + 1, i)
                act.wait_ge(s["gu"], turn(i, p + 1, 1))
                nc.scalar.activation(silu_s, pA[:, 0:FE], ACT.Silu).then_inc(s["silu_s"], 1)
                n = USE["T", p]
                empty(n, i, actT, bk[n % 4][:, 0:2 * P].rearrange("p (f c) -> p f c", f=FT))
                act.wait_ge(s["dn1"], turn(i, p + 1, 1))
                nc.scalar.activation(yrow[:, 512:], pC[:], ACT.Copy).then_inc(s["y1"], 1)

            gates_e(0, None)
            gates_e(1, None)
            tokens_e(0, None)
            pair(0)
            with act.Fori(0, 7) as i:
                for b in range(4):
                    pair(1 + b, i)
            for p in range(29, NPAIR):
                pair(p)

            act.wait_ge(s["flag"], 1)
            with act.If(act.value_load(flag[0:1, 0:1], min_val=0, max_val=1) >= 1):
                n = BASE["fgates"]
                t = fulls(n)
                nc.scalar.activation(gatesT, t[0:E, 0:NT], ACT.Copy).then_inc(s["gatesT"], 1)
                act.wait_ge(s["gatesT"], 1)
                act.sem_inc(free[n % 4], 1)
                for n in range(BASE["fgates"] + 1, BASE["fexp"]):
                    act.wait_ge(full[n % 4], n // 4 + 1)
                    act.sem_inc(free[n % 4], 1)
                with act.Fori(0, E // 4) as i:
                    for b in range(4):
                        silu(BASE["fexp"] + 12 * b, b % 2, i, i * 8 + (2 + 2 * b))

        @block.vector
        def _(dve):
            chain = [0, c_dve]

            def link(ins):
                chain[0] += 1
                ins.then_inc(chain[1], 1)
                dve.wait_ge(chain[1], chain[0])

            def fulls(n):
                b, k = bank(n)
                dve.wait_ge(full[b], k + 1)
                return bk[b]

            V = nc.vector

            def inv_var(stage, width, out, np_=P):
                n = BASE[stage]
                t = fulls(n)
                link(V.tensor_scalar(out, t[0:np_, 0:NT], 1.0 / width, EPS, ALU.mult, ALU.add))
                dve.sem_inc(free[n % 4], 1)
                link(V.reciprocal(out, out))

            def rows(ap, k):
                return ap.unsqueeze(1).broadcast_to([ap.shape[0], k, ap.shape[1]])

            def lanes(ap, t):
                return ap.unsqueeze(2).broadcast_to([ap.shape[0], ap.shape[1], t])

            dve.wait_ge(d_c, 16)
            dve.wait_ge(s["csig"], 1)
            link(V.tensor_tensor(csig[:, :, 0:NC], csig[:, :, 0:NC], cT[:], ALU.mult))
            dve.sem_inc(s["csilu"], 1)
            dve.wait_ge(d_in, 16 * 2)
            dve.wait_ge(s["consts"], 6)
            inv_var("norm1", D, rstd[:])
            dve.sem_inc(s["var1"], 1)
            adf = ada[:].rearrange("p s k c -> p (s k) c")

            def modulation(x0, x1, j, g):
                dve.wait_ge(s["ada_mm"], x1)
                link(V.tensor_tensor(adf[:, 4 * x0:4 * x1], pA[:, 4 * x0 * NC:4 * x1 * NC]
                                     .rearrange("p (m c) -> p m c", c=NC),
                                     lanes(vec[:, V_BADA + 4 * x0:V_BADA + 4 * x1], NC), ALU.add))
                link(V.scalar_tensor_tensor(out=ada[:, j], in0=ada[:, j], scalar=1.0, in1=lanes(vec[:, g:g + DT], NC),
                                            op0=ALU.add, op1=ALU.mult))
                dve.sem_inc(s["ada"], 1)

            def modulate(dst, j, rs, done):
                dve.wait_ge(rs, 1)
                link(V.tensor_tensor(dst[:], xT[:], rows(rstd[:], DT), ALU.mult))
                if j == 0:
                    modulation(0, 4, 1, V_GMIX)
                for k in range(DT):
                    last = V.tensor_scalar(dst[:, k, 0:NP_], dst[:, k, 0:NP_], ada[:, j + 1, k, 0:1],
                                           ada[:, j, k, 0:1], ALU.mult, ALU.add)
                last.then_inc(done, 1)
                link(V.tensor_tensor(dst[:, :, NP_:NT], dst[:, :, NP_:NT], ada[:, j + 1, :, 1:NC], ALU.mult))
                V.tensor_tensor(dst[:, :, NP_:NT], dst[:, :, NP_:NT], ada[:, j, :, 1:NC], ALU.add).then_inc(done, 1)

            modulate(hT, 0, s["rs1"], s["h1"])

            inv_var("cqn", QL, rstd[:])
            dve.sem_inc(s["varq"], 1)
            dve.wait_ge(s["rsq"], 1)
            for k in range(QT):
                last = V.scalar_tensor_tensor(out=pT[:, T_Q + k, :], in0=pT[:, T_Q + k, :],
                                              scalar=vec[:, V_GQ + k:V_GQ + k + 1], in1=rstd[:],
                                              op0=ALU.mult, op1=ALU.mult)
            link(last)
            dve.sem_inc(s["cqn"], 1)
            inv_var("kvn", KL, rstd[:])
            dve.sem_inc(s["varkv"], 1)
            dve.wait_ge(s["rskv"], 1)
            for k in range(KT_):
                last = V.scalar_tensor_tensor(out=pT[:, T_KV + k, :], in0=pT[:, T_KV + k, :],
                                              scalar=vec[:, V_GKV + k:V_GKV + k + 1], in1=rstd[:],
                                              op0=ALU.mult, op1=ALU.mult)
            link(last)
            dve.sem_inc(s["ckv"], 1)
            dve.wait_ge(s["in_done"], 1)
            dve.wait_ge(d_late, 16 * 10)
            V.tensor_tensor(zp[:, :, 2:2 + NP_], pT[:, T_CC:T_CC + CT, 0:NP_], pT[:, T_CH:T_CH + CT, 0:NP_], ALU.mult)
            link(V.tensor_tensor(zs[:, :, :, 2:3].rearrange("p k s o -> p k (s o)"), pT[:, T_CC:T_CC + CT, NP_:NT],
                                 pT[:, T_CH:T_CH + CT, NP_:NT], ALU.mult))
            dve.sem_inc(s["z"], 1)
            n = BASE["krs"]
            t = fulls(n)
            R = slice(NOPE, QK)
            link(V.tensor_tensor(krT[R, 1, :], t[R, 0:NT], sinT[R, :], ALU.mult))
            dve.sem_inc(free[n % 4], 1)
            dve.wait_ge(s["krin"], 1)
            link(V.tensor_tensor(krT[R, 0, :], krT[R, 0, :], cosT[R, :], ALU.mult))
            link(V.tensor_tensor(krT[R, 1, :], krT[R, 0, :], krT[R, 1, :], ALU.add))
            dve.sem_inc(s["krot"], 1)
            V.tensor_copy(kT[R, :, :], rows(krT[R, 1, :], H)).then_inc(s["kfull"], 1)
            big = pT[:, T_CC:T_CC + H, :]
            for h in range(H):
                n = BASE["qswap"] + h
                t = fulls(n)
                link(V.tensor_tensor(big[R, h, :], t[R, 0:NT], sinT[R, :], ALU.mult))
                dve.sem_inc(free[n % 4], 1)
            link(V.tensor_tensor(qT[R], qT[R], rows(cosT[R, :], H), ALU.mult))
            link(V.tensor_tensor(qT[R], qT[R], big[R], ALU.add))
            dve.sem_inc(s["qrot"], 1)
            link(V.tensor_scalar(gqp[:], vec[:, V_GQQ:V_GQQ + 1], QK ** -0.5, None, ALU.mult))

            def page_sums(q, js):
                for j in js:
                    dve.wait_ge(s["ksq"], NPG * q + j + 1)
                    V.tensor_reduce(out=kss[:, q, j, :], in_=ksq[:, j % 2, :].rearrange("p (h d) -> p h d", h=H),
                                    op=ALU.add, axis=AX.X).then_inc(s["ksq_used"], 1)

            def head_var(stage, x):
                n = BASE[stage]
                t = fulls(n)
                link(V.tensor_scalar(hinv[:, x, :], t[0:H, 0:NT], 1.0 / QK, EPS, ALU.mult, ALU.add))
                dve.sem_inc(free[n % 4], 1)
                link(V.reciprocal(hinv[:, x, :], hinv[:, x, :]))
                dve.sem_inc(s["varh"], 1)

            def head_norm(stage, dst, g):
                for h in range(H):
                    n = BASE[stage] + h
                    t = fulls(n)
                    link(V.scalar_tensor_tensor(out=dst[0:QK, h, :], in0=dst[0:QK, h, :], scalar=g, in1=t[0:QK, 0:NT],
                                                op0=ALU.mult, op1=ALU.mult))
                    dve.sem_inc(free[n % 4], 1)

            head_var("ksum", 0)
            page_sums(0, range(4))
            head_norm("kinv", kT, vec[0:QK, V_GQK:V_GQK + 1])
            head_var("qsum", 1)
            page_sums(0, range(4, NPG))
            head_norm("qinv", qT, gqp[0:QK, :])
            dve.sem_inc(s["kn"], 1)
            modulation(4, 12, 4, V_GFFN)
            link(V.tensor_tensor(sq[0:QK, 0, 0:H * NS].rearrange("p (h s) -> p h s", h=H), qT[0:QK, :, NP_:NT],
                                 kT[0:QK, :, NP_:NT], ALU.mult))
            dve.sem_inc(s["prodself"], 1)
            link(V.tensor_scalar(qsg[0:QK], qT[0:QK, :, NP_:NT], vec[0:QK, V_GQK:V_GQK + 1], None, ALU.mult))
            dve.sem_inc(s["qsg"], 1)
            link(V.memset(qrp, 0.0))
            link(V.tensor_copy(qrp[R, :, 0:H].rearrange("p s h -> p h s"), qsg[R]))
            dve.sem_inc(s["qlat"], 1)
            n = BASE["self"]
            t = fulls(n)
            link(V.tensor_copy(sself[:].rearrange("p s h -> p h s"), t[:, 0:H * NS].rearrange("p (h s) -> p h s", h=H)))
            dve.sem_inc(free[n % 4], 1)
            n = BASE["qlat"]
            t = fulls(n)
            for k in range(KT_):
                last = V.tensor_copy(qlat[:, k, :, 0:H].rearrange("p s h -> p h s"),
                                     t[:, k * H * NS:(k + 1) * H * NS].rearrange("p (h s) -> p h s", h=H))
            link(last)
            dve.sem_inc(free[n % 4], 1)
            dve.sem_inc(s["qlat"], 1)

            def conv(k):
                out = pT[:, T_CC:T_CC + CT, :]
                w = [vec[:, V_CONV + j * CT + k:V_CONV + j * CT + k + 1] for j in range(3)]
                V.tensor_scalar(out[:, k, 0:NP_], zp[:, k, 0:NP_], w[0], None, ALU.mult)
                link(V.tensor_scalar(out[:, k, NP_:NT], zs[:, k, :, 0], w[0], None, ALU.mult))
                for j in (1, 2):
                    V.scalar_tensor_tensor(out=out[:, k, 0:NP_], in0=zp[:, k, j:j + NP_], scalar=w[j],
                                           in1=out[:, k, 0:NP_], op0=ALU.mult, op1=ALU.add)
                    link(V.scalar_tensor_tensor(out=out[:, k, NP_:NT], in0=zs[:, k, :, j], scalar=w[j],
                                                in1=out[:, k, NP_:NT], op0=ALU.mult, op1=ALU.add))
                link(V.tensor_tensor(pT[:, T_CB + k, :], pT[:, T_CB + k, :], out[:, k], ALU.mult))

            def rotary_squares(q):
                b = q % 2
                dve.wait_ge(wgt[b], (q // 2) * (16 * NPG) + arrival(b, "pages"))
                kr_ = pgT[b][:, :, (KT_ + 1) * P:PGW]
                link(V.tensor_tensor(krsq, kr_, kr_, ALU.mult))
                dve.sem_inc(s["krd"], 1)
                link(V.tensor_reduce(out=krss[:, q, :], in_=krsq, op=ALU.add, axis=AX.X))

            rotary_squares(0)
            for q in range(NS):
                h = q
                if q + 1 < NS:
                    rotary_squares(q + 1)
                dve.wait_ge(s["asc"], h + 1)
                link(V.tensor_tensor(am, pB[:, 0:3 * P], mask[:], ALU.add))
                dve.sem_inc(s["am"], 1)
                V.tensor_reduce(out=amx[:, 0:1], in_=am[:, 0:P], op=ALU.max, axis=AX.X)
                link(V.tensor_reduce(out=amx[:, 1:2], in_=am[:, P:3 * P], op=ALU.max, axis=AX.X))
                link(V.tensor_scalar(amx[:], amx[:], -1.0, None, ALU.mult))
                dve.sem_inc(s["amx"], 1)
                if q + 1 < NS:
                    page_sums(q + 1, (0, 1))
                dve.wait_ge(s["aexp"], h + 1)
                link(V.reciprocal(arc[:], asum[:]))
                V.tensor_scalar(aP[:, 0:P], aP[:, 0:P], arc[:, 0:1], None, ALU.mult)
                V.tensor_scalar(aP[:, P:3 * P], aP[:, P:3 * P], arc[:, 1:2], None, ALU.mult).then_inc(s["anorm"], 1)
                if q + 1 < NS:
                    page_sums(q + 1, range(2, NPG))
                dve.wait_ge(s["anorm"], h + 1)
                if q < CT:
                    conv(q)
                if q == 0:
                    n = BASE["vmean"]
                    t = fulls(n)
                    link(V.tensor_scalar(rstd[:], t[:, 0:NT], 1.0 / CW, None, ALU.mult))
                    dve.sem_inc(free[n % 4], 1)
                    link(V.tensor_tensor(vn, vn, rows(rstd[:], CT), ALU.subtract))
                    dve.sem_inc(s["vcen"], 1)
                if q == CT - 1:
                    dve.sem_inc(s["conv"], 1)
                if q == 1:
                    inv_var("vvar", CW, rstd[:])
                    dve.sem_inc(s["varv"], 1)
                    dve.wait_ge(s["rsv"], 1)
                    for k in range(CT):
                        last = V.scalar_tensor_tensor(out=vn[:, k, :], in0=vn[:, k, :],
                                                      scalar=vec[:, V_GV + k:V_GV + k + 1], in1=rstd[:],
                                                      op0=ALU.mult, op1=ALU.mult)
                    link(last)
                    dve.sem_inc(s["vn"], 1)
                if q == 3:
                    for c in range(CT):
                        n = BASE["spat"] + c
                        t = fulls(n)
                        link(V.tensor_tensor(big[:, c, 0:NP_].rearrange("p (b t) -> p b t", b=2),
                                             t[:, 0:NP_].rearrange("p (b t) -> p b t", b=2), rows(bsp[:, c, :], 2), ALU.add))
                        dve.sem_inc(free[n % 4], 1)
                        link(V.tensor_scalar(big[:, c, NP_:NT], vn[:, c, NP_:NT], vec[:, V_W00 + c:V_W00 + c + 1],
                                             bsp[:, c, 0:1], ALU.mult, ALU.add))
                    link(V.tensor_tensor(pT[:, T_U:T_U + CT, :], pT[:, T_U:T_U + CT, :], big[:, 0:CT, :], ALU.mult))
                    dve.sem_inc(s["sg"], 1)

            dve.wait_ge(s["ksq_used"], NPG * NS)
            link(V.memset(orow, 0.0))
            kssp = kss.rearrange("p q j h -> p (q j) h")
            link(V.tensor_tensor(kssp, kssp, lanes(krss[:].rearrange("p q j -> p (q j)"), H), ALU.add))
            link(V.tensor_scalar(kss, kss, 1.0 / QK, EPS, ALU.mult, ALU.add))
            link(V.reciprocal(kss, kss))
            dve.sem_inc(s["kss"], 1)
            dve.wait_ge(s["rstds"], 1)
            dve.wait_ge(s["fold"], NS)
            link(V.tensor_tensor(ssc, pA[:].rearrange("p (q j h) -> p q j h", q=NS, j=NPG), kss, ALU.mult))
            link(V.tensor_reduce(out=smx, in_=ssc.rearrange("p q j h -> p q h j"), op=ALU.max, axis=AX.X))
            dve.sem_inc(s["smx"], 1)
            dve.wait_ge(s["allmx"], 1)
            link(V.tensor_tensor(samx, samx, sself[:], ALU.max))
            V.tensor_tensor(ssub, sself[:], samx, ALU.subtract)
            for q in range(NS):
                last = V.tensor_tensor(ssc[:, q], ssc[:, q], rows(samx[:, q], NPG), ALU.subtract)
            link(last)
            dve.sem_inc(s["ssub"], 1)
            dve.wait_ge(s["pexp"], 1)
            link(V.tensor_reduce(out=ssum, in_=sp_.rearrange("p q j h -> p q h j"), op=ALU.add, axis=AX.X))
            dve.sem_inc(s["psumd"], 1)
            dve.wait_ge(s["pexp"], 2)
            dve.wait_ge(s["tot_mm"], 1)
            link(V.tensor_tensor(stot, pB[:, 0:NG].rearrange("p (q h) -> p q h", q=NS), eself, ALU.add))
            link(V.reciprocal(stot, stot))
            for k in range(KT_):
                last = V.tensor_tensor(otmp[:, k].rearrange("p (q h) -> p q h", q=NS), eself,
                                       lanes(pT[:, T_KV + k, NP_:NT], H), ALU.mult)
            link(last)
            for g in range(2):
                n = BASE["otr"] + g
                t = fulls(n)
                for k in range(KT_):
                    ot = otmp[:, k, g * 4 * H:(g + 1) * 4 * H].rearrange("p (q h) -> p q h", q=4)
                    link(V.tensor_tensor(ot, ot, t[:, k * P:(k + 1) * P].rearrange("p (q x) -> p q x", q=4)[:, :, 0:H],
                                         ALU.add))
                    link(V.tensor_tensor(olat[:, k, :, 4 * g:4 * g + 4].rearrange("p h q -> p q h"), ot,
                                         stot[:, 4 * g:4 * g + 4], ALU.mult))
                dve.sem_inc(free[n % 4], 1)
                dve.sem_inc(s["olat"], 1)

            for m in range(DT):
                for b in range(3):
                    n = BASE[f"bo{m}"] + b
                    t = fulls(n)
                    dve.wait_ge(s["gsig"], 3 * m + b + 1)
                    g = gs[m % 3]
                    link(V.tensor_tensor(g[:, b, :], t[:, 0:NT], g[:, b, :], ALU.mult))
                    dve.sem_inc(free[n % 4], 1)
                link(V.tensor_tensor(g[:, 0, :], g[:, 0, :], g[:, 1, :], ALU.add))
                link(V.tensor_tensor(mg[:, m, :], g[:, 0, :], g[:, 2, :], ALU.add))
                dve.sem_inc(s["merged"], 1)

            def residual(dst, ps, j, m):
                V.scalar_tensor_tensor(out=dst[:, m, 0:NP_], in0=ps[:, 0:NP_], scalar=ada[:, j, m, 0:1],
                                       in1=xT[:, m, 0:NP_], op0=ALU.mult, op1=ALU.add)
                tmp = ksq[:, 0, 0:NS]
                link(V.tensor_tensor(tmp, ps[:, NP_:NT], ada[:, j, m, 1:NC], ALU.mult))
                link(V.tensor_tensor(dst[:, m, NP_:NT], tmp, xT[:, m, NP_:NT], ALU.add))

            for m in range(DT):
                n = BASE["out"] + m
                t = fulls(n)
                residual(xT, t, 2, m)
                dve.sem_inc(free[n % 4], 1)
                dve.sem_inc(s["x1"], 1)
            inv_var("norm2", D, rstd[:])
            dve.sem_inc(s["var2"], 1)
            modulate(hT, 3, s["rs2"], s["h2"])

            dve.wait_ge(s["lsig"], 3)
            link(V.tensor_tensor(ch[:], lg[:], rows(brou[:], 3), ALU.add))
            for j in range(3):
                for g in range(8):
                    last = V.max(top[:, j, g, :], ch[:, j, g * 8:(g + 1) * 8])
            V.memset(gsc[:, :, 8:12], 3 * BIG)
            link(last)
            link(V.tensor_tensor(gsc[:, :, 0:8], top[:, :, :, 0], top[:, :, :, 1], ALU.add))
            for j in range(3):
                last = V.max(gtop[:, j], gsc[:, j, 0:8])
            link(last)
            link(V.memset(gtop[:, :, 4:8], 3 * BIG))
            for j in range(3):
                last = V.match_replace(out=gms[:, j], in_to_replace=gtop[:, j], in_values=gsc[:, j], imm_value=-BIG)
            link(last)
            link(V.tensor_scalar(gms[:], gms[:], -BIG, BIG, ALU.is_equal, ALU.mult))
            link(V.tensor_scalar(gms[:], gms[:], BIG, None, ALU.subtract))
            for j in range(3):
                last = V.tensor_tensor(cm[:, j].rearrange("p (g e) -> p g e", g=8), ch[:, j].rearrange("p (g e) -> p g e", g=8),
                                       lanes(gms[:, j, 0:8], 8), ALU.add)
            link(last)
            for j in range(3):
                last = V.max(gtop[:, j], cm[:, j])
            link(last)
            for j in range(3):
                last = V.match_replace(out=ch[:, j], in_to_replace=gtop[:, j], in_values=cm[:, j], imm_value=-3 * BIG)
            link(last)
            link(V.tensor_scalar(ch[:], ch[:], -3 * BIG, None, ALU.is_equal))
            link(V.tensor_tensor(lg[:], lg[:], ch[:], ALU.mult))
            link(V.tensor_reduce(out=wsum[:], in_=lg[:], op=ALU.add, axis=AX.X))
            link(V.reciprocal(wsum[:], wsum[:]))
            for j in range(3):
                last = V.tensor_scalar(lg[:, j], lg[:, j], wsum[:, j:j + 1], ROUTED, ALU.mult, ALU.mult)
            link(last)
            dve.sem_inc(s["gates"], 1)

            for f in range(FT):
                n = BASE["shgu"] + 2 * f + 1
                t = fulls(n)
                dve.wait_ge(s["silu"], f + 1)
                V.tensor_tensor(actg[:, 1, f, :], acts[:, 1, f, :], t[:, 0:NT], ALU.mult).then_inc(s["act"], 1)
                dve.wait_ge(s["act"], f + 1)
                dve.sem_inc(free[n % 4], 1)
            link(V.memset(posm, -1.0))
            n = BASE["pos"]
            t = fulls(n)
            for j, m in enumerate((P, P, NS)):
                link(V.tensor_tensor(posm[0:m, j], t[0:m, j * E:(j + 1) * E], ch[0:m, j], ALU.mult))
                link(V.tensor_scalar(posm[0:m, j], posm[0:m, j], 1.0, None, ALU.subtract))
            dve.sem_inc(free[n % 4], 1)

            at = [0, None, c_dve]

            def step(ins):
                at[0] += 1
                ins.then_inc(c_dve, 1)
                dve.wait_ge(c_dve, at[0] if at[1] is None else at[1] + at[0])

            def build_gates(q, i):
                e = 2 * q if i is None else i * 8 + 2 * q
                for x in range(2):
                    for j, m in enumerate((P, P, NS)):
                        last = V.tensor_scalar(gtm[0:m, j, CAP * x:CAP * (x + 1)], iota[0:m, :],
                                               posm[0:m, j, bass.ds(e + x, 1)], lg[0:m, j, bass.ds(e + x, 1)],
                                               ALU.is_equal, ALU.mult)
                last.then_inc(s["gt"], 1)

            def index(q, i):
                n = USE["G", q]
                dve.wait_ge(free[n % 4], turn(i, n // 4 + 1, 3))
                step(V.scalar_tensor_tensor(out=idw, in0=gm[q % 4], scalar=0.0, in1=toki[:], op0=ALU.is_gt,
                                            op1=ALU.mult, accum_out=idxf[:, q % 2:q % 2 + 1]))
                V.tensor_copy(idx[:, q % 2:q % 2 + 1], idxf[:, q % 2:q % 2 + 1]).then_inc(s["idx"], 1)

            def add(q, i, ms):
                for m in ms:
                    n = USE["C", q, m]
                    dve.wait_ge(full[n % 4], turn(i, n // 4 + 1, 3))
                    V.tensor_tensor(yacc[:, m, :], yacc[:, m, :], bk[n % 4][:, 0:NT], ALU.add).then_inc(free[n % 4], 1)

            def pair(p, i=None):
                if p + 2 < NPAIR:
                    index(p + 2, i)
                if p + 3 < NPAIR:
                    build_gates(p + 3, i)
                dve.wait_ge(s["silu_s"], turn(i, p + 1, 1))
                V.tensor_tensor(act_s, silu_s, pA[:, FE:2 * FE], ALU.mult).then_inc(s["act_s"], 1)
                if p:
                    add(p - 1, i, range(8))
                dve.wait_ge(s["dn0"], turn(i, p + 1, 1))
                V.tensor_copy(yrow[:, 0:512], pB[:]).then_inc(s["y0"], 1)

            dve.wait_ge(d_tabs, 16 * 3)
            def shared_sum(ms):
                for m in ms:
                    n = BASE[f"shdn{m - m % 4}"] + m % 4
                    t = fulls(n)
                    V.tensor_copy(yacc[:, m, :], t[:, 0:NT]).then_inc(free[n % 4], 1)

            at[0] = chain[0]
            build_gates(0, None)
            V.tensor_reduce(out=pmax[:], in_=posm.rearrange("p j e -> p (j e)"), op=ALU.max, axis=AX.X
                            ).then_inc(s["pmax"], 1)
            index(0, None)
            build_gates(1, None)
            shared_sum(range(0, 4))
            index(1, None)
            build_gates(2, None)
            shared_sum(range(4, 8))
            for b in range(4):
                n = BASE["shdn4"] + b
                dve.wait_ge(free[n % 4], n // 4 + 1)
            pair(0)
            dve.wait_ge(s["pall"], 1)
            V.tensor_scalar(flag[:], pall[:], float(LIMIT), None, ALU.is_ge).then_inc(s["flag"], 1)
            first = at[0]
            with dve.Fori(0, 7) as i:
                for b in range(4):
                    at[1] = i * 4
                    at[0] = first + b
                    pair(1 + b, i)
            at[0], at[1] = first + 28, None
            for p in range(29, NPAIR):
                pair(p)
            add(NPAIR - 1, None, range(8))

            dve.wait_ge(s["flag"], 1)
            with dve.If(dve.value_load(flag[0:1, 0:1], min_val=0, max_val=1) >= 1):
                for j, m in enumerate((P, P, NS)):
                    last = V.scalar_tensor_tensor(out=ch[0:m, j], in0=posm[0:m, j], scalar=float(LIMIT), in1=lg[0:m, j],
                                                  op0=ALU.is_ge, op1=ALU.mult)
                last.then_inc(s["fgates"], 1)
                dve.wait_ge(s["gatesT"], 1)
                per = 13
                with dve.Fori(0, E // 4) as i:
                    for b in range(4):
                        nth = [per * b]

                        def fstep(ins):
                            nth[0] += 1
                            ins.then_inc(c_f, 1)
                            dve.wait_ge(c_f, i * (4 * per) + nth[0])

                        par = b % 2
                        n0 = BASE["fexp"] + 12 * b
                        fstep(V.tensor_scalar(gsel[:, par, :], gatesT, ident[0:E, bass.ds(i * 4 + b, 1)], None, ALU.mult))
                        dve.sem_inc(s["gsel"], 1)
                        for f in range(FT):
                            n = n0 + 2 * f + 1
                            dve.wait_ge(full[n % 4], i * 12 + (n // 4 + 1))
                            dve.wait_ge(s["silu"], i * 8 + (2 * b + f + 3))
                            fstep(V.tensor_tensor(actg[:, par, f, :], acts[:, par, f, :], bk[n % 4][:, 0:NT], ALU.mult))
                            dve.sem_inc(free[n % 4], 1)
                        dve.wait_ge(s["gbc"], i * 4 + (b + 1))
                        for f in range(FT):
                            fstep(V.tensor_tensor(actg[:, par, f, :], actg[:, par, f, :], [pC, pD][par][:, 0:NT],
                                                  ALU.mult))
                            dve.sem_inc(s["act"], 1)
                        for m in range(DT):
                            n = n0 + 4 + m
                            dve.wait_ge(full[n % 4], i * 12 + (n // 4 + 1))
                            fstep(V.tensor_tensor(yacc[:, m, :], yacc[:, m, :], bk[n % 4][:, 0:NT], ALU.add))
                            dve.sem_inc(free[n % 4], 1)
                        assert nth[0] == per * (b + 1)
            V.memset(idxf[:], 0.0).then_inc(c_end, 1)
            dve.wait_ge(c_end, 1)
            chain[0], chain[1] = 1, c_end
            tail = hT[:, :, NP_:NT]
            link(V.tensor_tensor(tail, yacc[:, :, NP_:NT], ada[:, 5, :, 1:NC], ALU.mult))
            link(V.tensor_tensor(tail, tail, xT[:, :, NP_:NT], ALU.add))
            for m in range(DT):
                last = V.scalar_tensor_tensor(out=hT[:, m, 0:NP_], in0=yacc[:, m, 0:NP_], scalar=ada[:, 5, m, 0:1],
                                              in1=xT[:, m, 0:NP_], op0=ALU.mult, op1=ALU.add)
                if m % 2:
                    last.then_inc(s["yout"], 1)


def _constants():
    pos = np.concatenate([np.arange(NP_), np.full(NS, NPG * P)]).astype(np.float32)
    inv = (np.float32(10000.0) ** (-np.arange(0, ROPE, 2, dtype=np.float32) / np.float32(ROPE))).astype(np.float32)
    ang = (pos[:, None] * inv[None, :]).astype(np.float32).T
    cos, sin = np.zeros((P, NT), np.float32), np.zeros((P, NT), np.float32)
    cos[NOPE:QK] = np.concatenate([np.cos(ang), np.cos(ang)])
    sin[NOPE:QK] = np.concatenate([np.sin(ang), np.sin(ang)])
    swap = np.zeros((P, ROPE), np.float32)
    h = ROPE // 2
    for j in range(h):
        swap[NOPE + h + j, j] = -1.0
        swap[NOPE + j, h + j] = 1.0
    t = np.arange(P)
    slots = np.arange(CAP)
    tri = np.where(t[None, :] <= t[:, None], 0.0, -BIG).astype(np.float32)
    mask = np.concatenate([tri, np.zeros((P, P), np.float32), tri], axis=1)
    return {"ident": np.eye(P, dtype=np.float32), "swapm": swap, "cosT": cos, "sinT": sin, "mask": mask,
            "fold": (t[:, None] % 32 == np.arange(NC)[None, :]).astype(np.float32),
            "fold2": (t[:, None] // 32 % 2 * H + t[:, None] % 32 == np.arange(2 * H)[None, :]
                      ).astype(np.float32) * (t[:, None] % 32 < H),
            "tri": (t[:, None] <= t[None, :]).astype(np.float32),
            "iota": np.tile(np.where(slots < LIMIT, slots, -7).astype(np.float32), (P, 1)),
            "toki": np.tile(np.arange(NT, dtype=np.float32), (P, 1))}


_OUTS = {"yT": (P, DT, NT), "ckvT": (P, KT_, NT), "krT": (ROPE, NT), "convP": (P, CT, 2), "convS": (P, CT, NS, 2),
         "vnP": (P, CT, P), "vnS": (P, CT, NS)}


def kernel(**inputs):
    import concourse.bacc as _bacc
    from concourse.bass_utils import run_bass_kernel_spmd as _run

    a = {k: np.asarray(v) for k, v in inputs.items()}
    a = {k: (v[0] if v.ndim > 1 and k not in ("x_prompt", "x_sample", "page_table", "c_prompt", "c_sample") else v)
         for k, v in a.items()}

    def feat(v, t):
        return v.T.reshape(t, P, -1).transpose(1, 0, 2)

    def wrows(w):
        return w.reshape(-1, P, w.shape[-1]).transpose(1, 0, 2)

    x = np.concatenate([a["x_prompt"][0], a["x_sample"][:, 0]], axis=0)
    c = np.concatenate([a["c_prompt"], a["c_sample"]], axis=0)
    vecs = [v.reshape(-1, P).T for v in (a["b_ada"], a["g_norm_mix"], a["g_norm_ffn"], a["g_q_lat"], a["g_kv_lat"],
                                         a["g_v_ln"], a["w_conv"].reshape(-1), np.repeat(a["w_spatial"][:, 0, 0], 64))]
    vecs += [np.pad(a[g], (0, P - QK))[:, None] for g in ("g_qk_q", "g_qk_k")]
    lat = a["cache_kv_latent"]
    kr = a["cache_k_rope"]
    latT = lat.transpose(0, 2, 1).reshape(NPOOL, KT_, P, P).transpose(0, 2, 1, 3).reshape(NPOOL, P, KL)
    krT = np.pad(kr.transpose(0, 2, 1), ((0, 0), (NOPE, P - QK), (0, 0)))
    arrays = {
        "xT": feat(x, DT), "cT": feat(c, DT), "vec": np.concatenate(vecs, axis=1),
        "ptab": a["page_table"].reshape(1, -1).astype(np.int32),
        "poolR": lat, "poolT": np.concatenate([latT, krT, kr], axis=2),
        "stateT": a["state_conv"].transpose(2, 0, 1).reshape(CT, P, NS, 2).transpose(1, 0, 2, 3),
        "w_uq": wrows(a["w_uq"].reshape(QL, -1)), "w_uk": wrows(a["w_uk"].reshape(KL, -1)),
        "w_uv": wrows(a["w_uv"].reshape(KL, -1)), "w_ukT": a["w_uk"].transpose(2, 1, 0),
        "wspT": a["w_spatial"].transpose(2, 0, 1), "w_router": wrows(a["w_router"]),
        "bsp": np.repeat(a["b_spatial"].reshape(CT, 2, 1, P), 64, axis=2).reshape(CT, P, P).transpose(1, 0, 2),
        "brou": np.broadcast_to(a["b_router"], (P, E)),
    }
    for k in ("w_ada", "w_in", "w_br_a", "w_br_b", "w_br_c", "w_out", "w_sh_gate", "w_sh_up", "w_sh_down",
              "w_e_gate", "w_e_up", "w_e_down"):
        arrays[k] = a[k]
    arrays.update(_constants())
    arrays = {k: np.ascontiguousarray(v) for k, v in arrays.items()}

    nc = _bacc.Bacc("TRN2", target_bir_lowering=False, num_devices=1)
    A = {k: nc.dram_tensor(f"in_{k}", v.shape, mybir.dt.from_np(v.dtype), kind="ExternalInput").ap()
         for k, v in arrays.items()}
    O = {k: nc.dram_tensor(f"out_{k}", v, F32, kind="ExternalOutput").ap() for k, v in _OUTS.items()}
    build(nc, A, O)
    r = _run(nc, [{f"in_{k}": v for k, v in arrays.items()}], core_ids=[0]).results[0]
    o = {k: np.asarray(r[f"out_{k}"]) for k in _OUTS}

    def tokens(v):
        return v.transpose(1, 0, 2).reshape(-1, v.shape[2]).T

    y, ckv, krope = tokens(o["yT"]), tokens(o["ckvT"]), o["krT"].T
    conv_p, vn_p, vn_s = tokens(o["convP"]), tokens(o["vnP"]), tokens(o["vnS"])
    conv_s = o["convS"].transpose(2, 3, 1, 0).reshape(NS, 2, CW)
    c_ = np.ascontiguousarray
    return (c_(y[None, :NP_]), c_(y[NP_:, None]), c_(ckv[None, None, :NP_]), c_(krope[None, None, :NP_]),
            c_(conv_p[None, None]), c_(vn_p[None, None]), c_(ckv[None, NP_:, None]), c_(krope[None, NP_:, None]),
            c_(conv_s[None]), c_(vn_s[None, :, None]))
```
